# Optimizing a Trainium2 kernel written in Bass

```python
import math
import jax, jax.numpy as jnp
from jax import lax
import numpy as np

D_MODEL = 2048
BATCH = 1
SEQ = 1024
DEPTH = 1

MIX_WIDTH = D_MODEL
HEAD_DIM = 64
BLOCK = 128
ROPE_THETA = 10000.0
EPS = 1e-6
NEG_INF = -1e30

A_WIDTH = MIX_WIDTH // 2
A_VDIM = 2 * HEAD_DIM
A_HEADS = A_WIDTH // A_VDIM
A_SUB = HEAD_DIM

B_WIDTH = MIX_WIDTH - A_WIDTH
B_HEADS = B_WIDTH // HEAD_DIM
B_KV_HEADS = B_HEADS // 8
B_GROUP = B_HEADS // B_KV_HEADS
WINDOW = 128

SPLIT_SIZES = (
    A_HEADS * 2 * A_SUB,
    A_HEADS * 2 * A_SUB,
    A_WIDTH,
    A_WIDTH,
    B_HEADS * HEAD_DIM,
    B_KV_HEADS * HEAD_DIM,
    B_KV_HEADS * HEAD_DIM,
    B_WIDTH,
)
PROJ_WIDTH = sum(SPLIT_SIZES)
SPLIT_IDX = tuple(int(i) for i in np.cumsum(SPLIT_SIZES)[:-1])

kernel_name = "hymba_diffattn_swa_sinks_layer"

def rmsnorm(x, w):
    xf = x.astype(jnp.float32)
    y = xf * lax.rsqrt(jnp.mean(xf * xf, axis=-1, keepdims=True) + EPS)
    return (y * w.astype(jnp.float32)).astype(x.dtype)

def rope_tables(positions):
    inv_freq = ROPE_THETA ** (-(jnp.arange(0, HEAD_DIM, 2, dtype=jnp.float32) / HEAD_DIM))
    ang = positions.astype(jnp.float32)[..., None] * inv_freq
    return jnp.cos(ang), jnp.sin(ang)

def apply_rope(x, cos, sin):
    shape = cos.shape[:2] + (1,) * (x.ndim - 3) + cos.shape[-1:]
    c = cos.reshape(shape)
    s = sin.reshape(shape)
    xf = x.astype(jnp.float32)
    x1, x2 = jnp.split(xf, 2, axis=-1)
    out = jnp.concatenate([x1 * c - x2 * s, x2 * c + x1 * s], axis=-1)
    return out.astype(x.dtype)

def diff_attention(q, k, v, lam):
    b, s_len, h = q.shape[:3]
    nblk = s_len // BLOCK
    scale = A_SUB ** -0.5
    key_pos = jnp.arange(s_len)
    lam = lam.astype(jnp.float32)

    def one_block(i):
        qb = lax.dynamic_slice_in_dim(q, i * BLOCK, BLOCK, axis=1)
        sc = jnp.einsum('bthcd,bshcd->bhcts', qb, k,
                        preferred_element_type=jnp.float32) * scale
        q_pos = i * BLOCK + jnp.arange(BLOCK)
        mask = key_pos[None, :] <= q_pos[:, None]
        sc = jnp.where(mask, sc, NEG_INF)
        p = jax.nn.softmax(sc, axis=-1)
        a = p[:, :, 0] - lam * p[:, :, 1]
        return jnp.einsum('bhts,bshe->bthe', a.astype(v.dtype), v)

    out = lax.map(one_block, jnp.arange(nblk))
    return jnp.moveaxis(out, 0, 1).reshape(b, s_len, h, A_VDIM)

def swa_sinks_attention(q, k, v, sinks):
    b, s_len = q.shape[:2]
    n = s_len // BLOCK
    scale = HEAD_DIM ** -0.5
    qb = q.reshape(b, n, BLOCK, B_KV_HEADS, B_GROUP, HEAD_DIM)
    kb = k.reshape(b, n, BLOCK, B_KV_HEADS, HEAD_DIM)
    vb = v.reshape(b, n, BLOCK, B_KV_HEADS, HEAD_DIM)
    pad = ((0, 0), (1, 0), (0, 0), (0, 0), (0, 0))
    k_band = jnp.concatenate([jnp.pad(kb[:, :-1], pad), kb], axis=2)
    v_band = jnp.concatenate([jnp.pad(vb[:, :-1], pad), vb], axis=2)
    sc = jnp.einsum('bntkgd,bnskd->bnkgts', qb, k_band,
                    preferred_element_type=jnp.float32) * scale
    t_loc = jnp.arange(BLOCK)
    s_loc = jnp.arange(2 * BLOCK)
    rel = t_loc[:, None] + BLOCK - s_loc[None, :]
    in_window = (rel >= 0) & (rel < WINDOW)
    key_abs = jnp.arange(n)[:, None] * BLOCK - BLOCK + s_loc[None, :]
    mask = in_window[None, :, :] & (key_abs >= 0)[:, None, :]
    sc = jnp.where(mask[None, :, None, None], sc, NEG_INF)
    sink = sinks.astype(jnp.float32).reshape(1, 1, B_KV_HEADS, B_GROUP, 1, 1)
    sink = jnp.broadcast_to(sink, sc.shape[:-1] + (1,))
    p = jax.nn.softmax(jnp.concatenate([sc, sink], axis=-1), axis=-1)[..., :-1]
    o = jnp.einsum('bnkgts,bnskd->bntkgd', p.astype(v.dtype), v_band)
    return o.reshape(b, s_len, B_HEADS * HEAD_DIM)

def setup_inputs(seed: int = 0) -> dict:
    key = jax.random.key(seed)
    ks = jax.random.split(key, 16)
    f32 = jnp.float32
    x = jax.random.normal(ks[0], (BATCH, SEQ, D_MODEL), f32)
    positions = jnp.broadcast_to(jnp.arange(SEQ, dtype=jnp.int32), (BATCH, SEQ))
    gain = lambda k, shape: 1.0 + 0.05 * jax.random.normal(k, shape, f32)
    return {
        "x": x,
        "positions": positions,
        "norm_w": gain(ks[1], (DEPTH, D_MODEL)),
        "w_in": jax.random.normal(ks[2], (DEPTH, D_MODEL, PROJ_WIDTH), f32) * D_MODEL ** -0.5,
        "q_norm_a": gain(ks[3], (DEPTH, A_SUB)),
        "k_norm_a": gain(ks[4], (DEPTH, A_SUB)),
        "lambda_q1": 0.1 * jax.random.normal(ks[5], (DEPTH, A_SUB), f32),
        "lambda_k1": 0.1 * jax.random.normal(ks[6], (DEPTH, A_SUB), f32),
        "lambda_q2": 0.1 * jax.random.normal(ks[7], (DEPTH, A_SUB), f32),
        "lambda_k2": 0.1 * jax.random.normal(ks[8], (DEPTH, A_SUB), f32),
        "subln_w": gain(ks[9], (DEPTH, A_VDIM)),
        "q_norm_b": gain(ks[10], (DEPTH, HEAD_DIM)),
        "k_norm_b": gain(ks[11], (DEPTH, HEAD_DIM)),
        "sinks": 0.5 * jax.random.normal(ks[12], (DEPTH, B_HEADS), f32),
        "w_out": jax.random.normal(ks[13], (DEPTH, MIX_WIDTH, D_MODEL), f32) * MIX_WIDTH ** -0.5,
    }

def reference(x, positions, norm_w, w_in, q_norm_a, k_norm_a, lambda_q1, lambda_k1,
              lambda_q2, lambda_k2, subln_w, q_norm_b, k_norm_b, sinks, w_out):
    b, s_len, _ = x.shape
    cos, sin = rope_tables(positions)
    for layer in range(DEPTH):
        lam_init = 0.8 - 0.6 * math.exp(-0.3 * layer)
        h = rmsnorm(x, norm_w[layer])
        proj = jnp.einsum('bsd,dp->bsp', h, w_in[layer])
        qa, ka, va, ga, qb, kb, vb, gb = jnp.split(proj, SPLIT_IDX, axis=-1)

        qa = apply_rope(rmsnorm(qa.reshape(b, s_len, A_HEADS, 2, A_SUB), q_norm_a[layer]), cos, sin)
        ka = apply_rope(rmsnorm(ka.reshape(b, s_len, A_HEADS, 2, A_SUB), k_norm_a[layer]), cos, sin)
        va = va.reshape(b, s_len, A_HEADS, A_VDIM)
        lam = (jnp.exp(jnp.sum(lambda_q1[layer].astype(jnp.float32) * lambda_k1[layer].astype(jnp.float32)))
               - jnp.exp(jnp.sum(lambda_q2[layer].astype(jnp.float32) * lambda_k2[layer].astype(jnp.float32)))
               + lam_init)
        oa = diff_attention(qa, ka, va, lam)
        oa = rmsnorm(oa, subln_w[layer]) * (1.0 - lam_init)
        ya = oa.reshape(b, s_len, A_WIDTH) * jax.nn.silu(ga)

        qb = apply_rope(rmsnorm(qb.reshape(b, s_len, B_HEADS, HEAD_DIM), q_norm_b[layer]), cos, sin)
        kb = apply_rope(rmsnorm(kb.reshape(b, s_len, B_KV_HEADS, HEAD_DIM), k_norm_b[layer]), cos, sin)
        vb = vb.reshape(b, s_len, B_KV_HEADS, HEAD_DIM)
        ob = swa_sinks_attention(qb, kb, vb, sinks[layer])
        yb = ob * jax.nn.silu(gb)

        y = jnp.concatenate([ya, yb], axis=-1)
        x = x + jnp.einsum('bsm,md->bsd', y, w_out[layer])
    return x


_drawn_inputs = setup_inputs


def setup_inputs(seed=0):
    import zlib

    import numpy as np

    out = dict(_drawn_inputs(seed))
    spreads = {}
    factors = {'q_norm_a': 2.742,
     'k_norm_a': 3.454,
     'lambda_q1': 200.0,
     'lambda_q2': 2.994,
     'lambda_k2': 4.603,
     'subln_w': 3.179,
     'q_norm_b': 8.0,
     'k_norm_b': 8.0,
     'sinks': 200.0}
    for name, (base, spread) in spreads.items():
        noise = np.random.default_rng([zlib.crc32(name.encode()), seed]).standard_normal(out[name].shape)
        drawn = base * np.exp(spread * noise) if base else spread * noise
        out[name] = __import__('jax').numpy.asarray(drawn.astype(out[name].dtype))
    for name, factor in factors.items():
        out[name] = (out[name] * factor).astype(out[name].dtype)
    return out
```

```python
import math
from contextlib import ExitStack

import concourse.bass as bass
import numpy as np
from concourse import mybir

F32 = mybir.dt.float32
F32R = mybir.dt.float32r
I32 = mybir.dt.int32
ALU = mybir.AluOpType
ACT = mybir.ActivationFunctionType
AX = mybir.AxisListType.X

P = 128
D = 2048
S = 1024
HD = 64
HALF = HD // 2
NR = S // P
KT = D // P
AH = 8
BC = 4
AW = 1024
QB0 = 4 * AW
KB0 = QB0 + 1024
VB0 = KB0 + 128
GB0 = VB0 + 128
EPS = 1e-6
NEG = -1e30
LAM_INIT = 0.8 - 0.6 * math.exp(-0.3 * 0)
QSCALE = HD ** -0.5
NQ_IN = 4 * (2 + 4 * (AH + BC))
N_AT_A = [1, 1, 1, 1, 2, 2, 2, 2]

KINDS = "A" * AH + "B" * BC
PHASES = [(0, 1), (1, 6), (7, 1), (8, 1), (9, 2), (11, 1), (12, 1)]
SP_PHASES = [(0, 1), (1, 5), (6, 1), (7, 1), (8, 1), (9, 1), (10, 1), (11, 1), (12, 1)]


def kind(it):
    return KINDS[it] if 0 <= it < len(KINDS) else None


def tile_desc(c, p):
    k, c = c
    if k == "A":
        return dict(unit=c, p=p, kind=k, T=c * 3 + (2 + min(p, 3)), K=c * 2 + (1 + p), GT=c, w=p,
                    norm=p < 2, turned=p < 3)
    return dict(unit=c, p=p, kind=k, T=c * 2 + (26 - 2 * AH + min(p, 2)), K=c * 2 + (17 - 2 * AH + p),
                GT=c * 2 + (8 - 2 * AH + max(p - 2, 0)), w=2, norm=p < 2, turned=p < 2)


KV_TILES = [dict(kind="kv", p=0, T=0, K=0, GT=0, w=3, norm=True, turned=True),
            dict(kind="kv", p=1, T=1, K=1, GT=0, w=3, norm=False, turned=True)]


def step_at(i, it, first_it):
    back = i < 0
    k = kind(first_it - 1 if back else first_it)
    i = i % NR
    unit = it - 1 if back else it
    return dict(i=i, k=k, G=unit * NR + i, unit=unit) if k else None


def uses_of(first_it):
    out = []
    cur, prev, nxt = kind(first_it), kind(first_it - 1), kind(first_it + 1)
    for s in range(16):
        i = s // 2
        turned = []
        if s % 4 < 2 and s >= 4:
            p = s // 4 - 1
            if nxt and tile_desc((nxt, 0), p)["turned"]:
                turned.append(("PT", p, s % 2))
        elif s < 2 and first_it == -1:
            turned.append(("PT", "v", s))
        if s % 2 == 0:
            out += turned
            k, j = (cur, i - 1) if i >= 1 else (prev, NR - 1)
            if k:
                out += [("AT", j, m) for m in range(2 if k == "B" else N_AT_A[j])]
        else:
            k, j = (cur, i - 2) if i >= 2 else (prev, NR - 2 + i)
            if k == "A":
                out.append(("YT", j))
            out += turned
            if i + 1 < NR and cur or i + 1 == NR and nxt:
                out.append(("T", (i + 1) % NR))
    return out


KV_USES = [("PT", "k", 0), ("PT", "k", 1)]
BASE = {}


def _count_bases():
    n = 32 + len(KV_USES)
    for it in range(-1, 13):
        BASE[it] = n
        n += len(uses_of(it))
    return n


_count_bases()


def use_number(name, it, first_it):
    return BASE[first_it] + uses_of(first_it).index(name) + (it - first_it) * len(uses_of(first_it))


def bank_of(name, first_it):
    return (BASE[first_it] + uses_of(first_it).index(name)) % 2


def qk_split(i, it, first):
    if i:
        return use_number(("T", i), it, first) + 1
    return BASE[first] + (it - first) * len(uses_of(first))


def at_spans(st):
    if st["k"] == "A":
        w = (st["i"] + 1) * P
        return [(0, min(w, 512))] + ([(512, w)] if w > 512 else [])
    return [(0, 512), (512, 1024)] if st["i"] else [(0, 256), (256, 512)]


def loads_by(k, unit, i):
    if k == "A":
        return unit * 64 + 16 * (i // 2 + 1)
    return (unit - AH) * 192 + (AH * 64 + 48 * (i // 2 + 1))


def stored_before(st):
    if st["k"] == "A":
        return st["unit"] * 64 + 16 * (st["i"] // 2)
    return (st["unit"] - AH) * 128 + (AH * 64 + 32 * (st["i"] // 2))


def decoder_layer(nc, x, positions, norm_w, w_in, q_norm_a, k_norm_a, lambda_q1, lambda_k1,
                  lambda_q2, lambda_k2, subln_w, q_norm_b, k_norm_b, sinks, w_out, inv_freq, out):
    for f, n in PHASES:
        assert n == 1 or len({len(uses_of(f + d)) for d in range(n)}) == 1
        assert n == 1 or len(uses_of(f)) % 2 == 0

    x2, out2 = x[0], out[0]
    scr_a = nc.dram_tensor("qkv_a_dram", (AH, S, 3 * P), F32).ap()
    scr_q = nc.dram_tensor("q_b_dram", (BC, S, 2 * P), F32).ap()
    scr_kv = nc.dram_tensor("kv_b_dram", (S, 2 * P), F32).ap()
    scr_g = nc.dram_tensor("gates_dram", (AH + 2 * BC, P, S), F32).ap()
    scr_y = nc.dram_tensor("y_dram", (D, S), F32).ap()

    with ExitStack() as ctx:
        def sb(name, shape, dt=F32):
            return ctx.enter_context(nc.sbuf_tensor(name, shape, dt))

        def sem(name):
            return ctx.enter_context(nc.semaphore(name))

        hT_hi = sb("hT_hi", [P, KT, S], F32R)
        hT_lo = sb("hT_lo", [P, KT, S], F32R)
        w_raw = sb("w_raw_sb", [P, 2, 512])
        w_hi = sb("w_hi_sb", [P, 4, 512], F32R)
        w_lo = sb("w_lo_sb", [P, 4, 512], F32R)
        kT_hi = sb("kT_hi", [P, S], F32R)
        kT_lo = sb("kT_lo", [P, S], F32R)
        v_hi = sb("v_hi_sb", [P, NR, P], F32R)
        v_lo = sb("v_lo_sb", [P, NR, P], F32R)
        qT_hi = sb("qT_hi", [P, 2 * P], F32R)
        qT_lo = sb("qT_lo", [P, 2 * P], F32R)
        expd = sb("expd", [P, 2, S])
        aT_hi = sb("aT_hi", [P, S], F32R)
        aT_lo = sb("aT_lo", [P, S], F32R)
        stage_rows = sb("stage_rows", [P, 4 * 512])
        tmp = sb("tmp", [P, 512])
        qkv = sb("qkv_sb", [P, 2, 448])
        gate_y = sb("gate_y", [P, 2, 512])
        o_sb = sb("o_sb", [P, 256])
        mask = sb("mask", [P, 2 * P])
        ident = sb("ident", [P, P])
        cos_t = sb("cos_t", [P, NR, HALF])
        sin_t = sb("sin_t", [P, NR, HALF])
        head_w = sb("head_w", [P, 4, HD])
        norm_c = sb("norm_c", [P, KT])
        sub_c = sb("sub_c", [P, 2])
        sink_t = sb("sink_t", [P, 4 * BC])
        pos_i = sb("pos_i", [P, NR], I32)
        pos_f = sb("pos_f", [P, NR])
        ss_x = sb("ss_x", [P, 2 * NR])
        small = sb("small", [P, 5, 8])
        neg_lam = sb("neg_lam", [P, 8])
        neg_max = sb("neg_max", [P, 8])
        sink_e = sb("sink_e", [P, 4])
        sums = sb("sums", [P, 4])
        inv_sum = sb("inv_sum", [P, 2, 4])
        coef = sb("coef", [P, 1])
        ss_o = sb("ss_o", [P, 3])
        ss_h = sb("ss_h", [P, 24])

        stage = stage_rows[:, 0:1024].rearrange("p (b c) -> p b c", b=2)
        rows = stage_rows[:, 1024:2048].rearrange("p (b c) -> p b c", b=2)
        x_buf = [expd[:, :, :].rearrange("p a b -> p (a b)"), stage_rows[:, :]]
        x_sc = gate_y

        ps_a = ctx.enter_context(nc.psum_tensor("ps_a", [P, 4, 512], F32))
        ps_b = ctx.enter_context(nc.psum_tensor("ps_b", [P, 4, 512], F32))
        p_proj = [ps_a[:, 0, :], ps_a[:, 1, :]]
        p_s = ps_a[:, 2:4, :]
        p_tr = [ps_b[:, 0, :], ps_b[:, 1, :]]
        p_o = ps_b[:, 2, :]
        p_junk = ps_b[:, 3, :]

        names = """consts ident_ready par_in lam_in lam_prod lam_sum lam_exp lam_ready pos_in ang rope_arg rope_ready
            x_sq x_pow x_scaled x_wnorm x_hi x_lo
            w_hi_ready w_lo_ready w_used
            tp_done tp_free sq_ready ss_ready norm_chain rs_ready
            t_hi v_hi_ready v_split s_done masked max_ready x_done sink_ready sink_exp
            comb_chain comb_done at_hi pv_done o_read o_pow o_ready b_sum probs_scaled
            y_hi y_lo out_ready pp_done""".split()
        sm = {n: sem("s_" + n) for n in names}

        def pair(name):
            return [sem(f"s_{name}{b}") for b in range(2)]

        x_in, w_in_sem, pp_copied = pair("x_in"), pair("w_in"), pair("pp_copied")
        pp_tanh, pp_gated, gstored = pair("pp_tanh"), pair("pp_gated"), pair("gstored")
        rst_ready, stored, loaded = pair("rst_ready"), pair("stored"), pair("loaded")
        gate_ld, ystored = pair("gate_ld"), pair("ystored")
        y_in, res_in, out_st = pair("y_in"), pair("res_in"), pair("out_st")
        block = ctx.enter_context(nc.Block())

        def wait(eng, s, value):
            if isinstance(value, int) and value <= 0:
                return
            eng.wait_ge(s, value)

        def iterations(eng, body, phases=PHASES):
            body(-1, -1)
            for f, n in phases:
                if n == 1:
                    body(f, f)
                else:
                    with eng.Fori(f, f + n) as it:
                        body(it, f)

        def proj_tile(it, first, s):
            nxt = kind(first + 1)
            if not nxt:
                return None, None, None
            p = s // 4
            d = tile_desc((nxt, it + 1), p)
            u = (it + 1) * 4 + (2 + p)
            if p:
                before = tile_desc((nxt, it + 1), p - 1)
            elif first == -1:
                before = KV_TILES[1]
            else:
                before = tile_desc((kind(first), it), 3)
            return d, u, before

        def turned_before(it, first, s):
            d, u, before = proj_tile(it, first, s)
            if d is None or s % 4 > 1 or not before["turned"]:
                return None
            name = ("PT", "v", s) if s < 2 else ("PT", s // 4 - 1, s % 2)
            return before, name, s % 2

        @block.sync
        def _(sp):
            def load_x(r):
                if r >= 2:
                    wait(sp, sm["tp_done"], 4 * (r - 1))
                sp.dma_start(x_buf[r % 2], x2[r * P:(r + 1) * P, :]).then_inc(x_in[r % 2], 16)

            def load_quarter(u, q, col):
                wait(sp, sm["w_lo_ready"], u * 4 + (q - 1))
                src = w_in[0, q * 512:(q + 1) * 512, bass.ds(col, P)].rearrange("(k r) c -> r k c", k=4)
                sp.dma_start(w_raw[:, q % 2, :].rearrange("p (k c) -> p k c", k=4), src)\
                  .then_inc(w_in_sem[q % 2], 16)

            def load_w_out(g, k):
                Q = NQ_IN + 16 * g + k
                wait(sp, sm["w_lo_ready"], Q - 1)
                sp.dma_start(w_raw[:, Q % 2, :], w_out[0, k * P:(k + 1) * P, (g % 4) * 512:(g % 4 + 1) * 512])\
                  .then_inc(w_in_sem[Q % 2], 16)

            def column(k, c, p):
                if k == "A":
                    return c * P + AW * p
                return (c - AH) * 256 + ((QB0 if p < 2 else GB0) + P * (p % 2))

            def load_ahead(it, first, s):
                p, q, far = (s + 4) // 4, s % 4, 0
                if p == 4:
                    p, far = 0, 1
                k = kind(first + 1 + far)
                if k:
                    c = it + (1 + far)
                    load_quarter(c * 4 + (2 + p), q, column(k, c, p))
                elif first == len(KINDS) - 2 and far:
                    load_w_out(0, q)

            def store_rows(d, b, n):
                if d["norm"]:
                    wait(sp, rst_ready[b], d["K"] + 1)
                else:
                    wait(sp, sm["tp_free"], n + 1)
                t, p = slice(b * 512, (b + 1) * 512), d["p"]
                c = slice(p * P, (p + 1) * P)
                if d["kind"] == "A":
                    dst = scr_a[bass.ds(d["unit"], 1), t, c].rearrange("a (r t) c -> t (a r) c", r=4)
                elif d["kind"] == "B":
                    dst = scr_q[bass.ds(d["unit"] - AH, 1), t, c].rearrange("a (r t) c -> t (a r) c", r=4)
                else:
                    dst = scr_kv[t, c].rearrange("(r t) c -> t r c", r=4)
                sp.dma_start(dst, rows[:, b, :].rearrange("p (r c) -> p r c", r=4)).then_inc(stored[b], 16)

            def store_gate(d, b):
                wait(sp, pp_gated[b], d["GT"] + 1)
                sp.dma_start(scr_g[bass.ds(d["GT"], 1), :, b * 512:(b + 1) * 512].rearrange("a p t -> p (a t)"),
                               stage[:, b, :]).then_inc(gstored[b], 16)

            def load_step(nk, unit, i):
                G = unit * NR + i
                if not (isinstance(G, int) and G < 2):
                    wait(sp, sm["v_split"], G - 1)
                t = slice(i * P, (i + 1) * P)
                if nk == "A":
                    wait(sp, stored[i // 4], unit * 48 + 80)
                    sp.dma_start(qkv[:, i % 2, 0:3 * P], scr_a[bass.ds(unit, 1), t, :].rearrange("a t c -> t (a c)"))\
                        .then_inc(loaded[i % 2], 16)
                    return
                j = unit - AH
                wait(sp, stored[i // 4], j * 32 + 16 * 28)
                kv = (j // 2) * HD
                sp.dma_start(qkv[:, i % 2, 0:2 * P], scr_q[bass.ds(j, 1), t, :].rearrange("a t c -> t (a c)"))\
                    .then_inc(loaded[i % 2], 16)
                sp.dma_start(qkv[:, i % 2, 256:384].rearrange("p (a c) -> p a c", a=2),
                               scr_kv[t, bass.ds(kv, HD)].unsqueeze(1).to_broadcast([P, 2, HD]))\
                    .then_inc(loaded[i % 2], 16)
                sp.dma_start(qkv[:, i % 2, 384:448], scr_kv[t, bass.ds(kv + P, HD)]).then_inc(loaded[i % 2], 16)

            def load_gate(st):
                i, unit = st["i"], st["unit"]
                t = slice(i * P, (i + 1) * P)
                wait(sp, ystored[i % 2], stored_before(st))
                if st["k"] == "A":
                    wait(sp, gstored[i // 4], unit * 16 + 16)
                    sp.dma_start(gate_y[:, i % 2, 0:P], scr_g[bass.ds(unit, 1), :, t].rearrange("a p t -> p (a t)"))\
                      .then_inc(gate_ld[i % 2], 16)
                    return
                j = unit - AH
                wait(sp, gstored[i // 4], j * 32 + 160)
                for r in range(2):
                    dst = gate_y[0:HD, i % 2, r * 256:(r + 1) * 256].rearrange("d (a t) -> d a t", a=2)
                    src = scr_g[bass.ds(j * 2 + AH, 2), r * HD:(r + 1) * HD, t].rearrange("a d t -> d a t")
                    sp.dma_start(dst, src).then_inc(gate_ld[i % 2], 16)

            def store_y(st, it, first):
                i = st["i"]
                t = slice(i * P, (i + 1) * P)
                if st["k"] == "A":
                    wait(sp, sm["tp_free"], use_number(("YT", i), it, first) + 1)
                    sp.dma_start(scr_y[bass.ds(st["unit"] * P, P), t], gate_y[:, i % 2, 0:P])\
                      .then_inc(ystored[i % 2], 16)
                    return
                wait(sp, sm["o_read"], st["G"] * 2 + 2)
                for r in range(2):
                    dst = scr_y[bass.ds((st["unit"] - AH) * 256 + AW, 256), t]\
                        .rearrange("(a r d) t -> r d a t", a=2, r=2)[r]
                    sp.dma_start(dst, gate_y[0:HD, i % 2, r * 256:(r + 1) * 256].rearrange("d (a t) -> d a t", a=2))\
                      .then_inc(ystored[i % 2], 16)

            load_x(0)
            load_x(1)
            load_quarter(0, 0, KB0)
            load_quarter(0, 1, KB0)
            for r in range(2, NR):
                load_x(r)
            load_quarter(0, 2, KB0)
            load_quarter(0, 3, KB0)
            for s in range(8):
                if s < 4:
                    load_quarter(1, s, VB0)
                else:
                    load_quarter(2, s - 4, 0)
                if 4 <= s < 6:
                    store_rows(KV_TILES[0], s - 4, 32 + s - 4)
            sp.wait_ge(sm["lam_sum"], 1)

            def body(it, first):
                for s in range(16):
                    i = s // 2
                    d, u, before = proj_tile(it, first, s)
                    load_ahead(it, first, s)
                    if d and s % 4 == 3 and not d["turned"]:
                        store_gate(d, 0)
                        store_gate(d, 1)
                    cur = step_at(i, it, first)
                    back1 = step_at(i - 1, it, first)
                    back2 = step_at(i - 2, it, first)
                    if s % 2 == 0:
                        if cur and i + 1 < NR:
                            load_step(cur["k"], it, i + 1)
                        elif i + 1 == NR and kind(first + 1):
                            load_step(kind(first + 1), it + 1, 0)
                        if back2 and back2["k"] == "B":
                            store_y(back2, it, first)
                        if back1:
                            load_gate(back1)
                    elif back2 and back2["k"] == "A":
                        store_y(back2, it, first)
                    tb = turned_before(it, first, s)
                    if tb:
                        store_rows(tb[0], tb[2], use_number(tb[1], it, first))

            iterations(sp, body, SP_PHASES)

            for b in range(2):
                sp.wait_ge(ystored[b], 8 * NR * (AH + 2 * BC))
                sp.wait_ge(gstored[b], 16 * (AH + 2 * BC))

            def load_y(k, half):
                n = half * KT + k
                if n >= 2:
                    sp.wait_ge(sm["y_lo"], n - 1)
                sp.dma_start(x_sc[:, n % 2, :], scr_y[k * P:(k + 1) * P, half * 512:(half + 1) * 512])\
                  .then_inc(y_in[n % 2], 16)

            def part(a, g):
                t, c = slice((g // 4) * 512, (g // 4 + 1) * 512), slice((g % 4) * 512, (g % 4 + 1) * 512)
                return a[t, c].rearrange("(r p) c -> p r c", r=4)

            def load_res(g):
                if g >= 2:
                    sp.wait_ge(out_st[g % 2], 16 * (g // 2))
                sp.dma_start(x_buf[g % 2].rearrange("p (r c) -> p r c", r=4), part(x2, g))\
                  .then_inc(res_in[g % 2], 16)

            def store_out(g):
                sp.wait_ge(sm["out_ready"], 4 * (g + 1))
                sp.dma_start(part(out2, g), x_buf[g % 2].rearrange("p (r c) -> p r c", r=4))\
                  .then_inc(out_st[g % 2], 16)

            for k in range(KT):
                load_y(k, 0)
            load_res(0)
            load_res(1)
            for g in range(8):
                for k in range(KT):
                    if 16 * g + k + 4 < 128:
                        load_w_out((16 * g + k + 4) // 16, (k + 4) % 16)
                    if g == 0:
                        load_y(k, 1)
                    elif k == 4:
                        store_out(g - 1)
                    elif k == 8 and g < 7:
                        load_res(g + 1)
            store_out(7)
            for b in range(2):
                sp.wait_ge(out_st[b], 64)

        @block.scalar
        def _(act):
            def split_w(Q, b4):
                wait(act, w_in_sem[b4 % 2], (Q - b4) * 8 + 16 * (b4 // 2 + 1))
                wait(act, sm["w_used"], Q - 3)
                act.activation(w_hi[:, b4, :], w_raw[:, b4 % 2, :], ACT.Copy).then_inc(sm["w_hi_ready"], 1)

            pars = [(head_w[:, n, :], w.partition_broadcast(P)[:, 0, :])
                    for n, w in enumerate((q_norm_a, k_norm_a, q_norm_b, k_norm_b))]
            pars += [(norm_c[:, :], norm_w[0].rearrange("(k p) -> p k", p=P)),
                     (sub_c[:, 0:1], subln_w[0].rearrange("(p a) -> p a", a=1))]
            pars += [(sink_t[:, :], sinks.partition_broadcast(P)[:, 0, :])]
            act.dma_start(pos_i[:, :], positions[0].rearrange("(r p) -> p r", p=P),
                          allow_slow_non_contiguous=True).then_inc(sm["pos_in"], 16)
            act.dma_start(tmp[:, 0:HALF], inv_freq.partition_broadcast(P)[:, 0, :]).then_inc(sm["pos_in"], 16)
            for n, w in enumerate((lambda_q1, lambda_k1, lambda_q2, lambda_k2)):
                act.dma_start(qkv[:, 0, n * HD:(n + 1) * HD], w.partition_broadcast(P)[:, 0, :])\
                   .then_inc(sm["lam_in"], 16)
            for dst, src in pars:
                act.dma_start(dst, src, allow_slow_non_contiguous=True).then_inc(sm["par_in"], 16)

            act.wait_ge(sm["rope_arg"], 2)
            act.activation(cos_t[:, :, :], cos_t[:, :, :], ACT.Sin).then_inc(sm["rope_ready"], 1)
            act.activation(sin_t[:, :, :], sin_t[:, :, :], ACT.Sin).then_inc(sm["rope_ready"], 1)
            act.wait_ge(sm["lam_sum"], 1)
            act.activation(neg_lam[:, 2:4], neg_lam[:, 0:2], ACT.Exp).then_inc(sm["lam_exp"], 1)

            def square_x(r):
                act.wait_ge(x_in[r % 2], 16 * (r // 2 + 1))
                if r:
                    act.wait_ge(sm["x_sq"], r)
                act.activation(ps_a[:, :, :].rearrange("p a b -> p (a b)"), x_buf[r % 2], ACT.Square,
                               accum_out=ss_x[:, r:r + 1]).then_inc(sm["x_sq"], 1)

            def scale_x(r):
                act.wait_ge(sm["x_pow"], 3 * (r + 1))
                act.activation(x_buf[r % 2], x_buf[r % 2], ACT.Copy, scale=ss_x[:, r:r + 1])\
                   .then_inc(sm["x_scaled"], 1)

            square_x(0)
            for r in range(NR):
                scale_x(r)
                if r + 1 < NR:
                    square_x(r + 1)
                for g in range(4):
                    act.wait_ge(sm["tp_free"], 4 * r + g + 1)
                    act.activation(hT_hi[:, 4 * g:4 * g + 4, r * P:(r + 1) * P],
                                   x_sc[:, g % 2, :].rearrange("p (k t) -> p k t", k=4), ACT.Copy)\
                       .then_inc(sm["x_hi"], 1)

            def stage_free(before, b, it, first):
                if before is None:
                    return
                if before["norm"]:
                    wait(act, rst_ready[b], before["K"] + 1)
                elif before["turned"]:
                    n = (use_number(("PT", 2, b), it, first) if before is not KV_TILES[1]
                         else BASE[-1] + b)
                    wait(act, sm["tp_free"], n + 1)
                else:
                    wait(act, gstored[b], before["GT"] * 16 + 16)

            def evacuate(d, before, u, it, first):
                for b in range(2):
                    wait(act, sm["w_used" if b else "pp_done"], u * 4 + 4 if b else u + 1)
                    stage_free(before, b, it, first)
                    if d["turned"]:
                        act.activation(stage[:, b, :], p_proj[b], ACT.Copy).then_inc(pp_copied[b], 1)
                    else:
                        act.activation(stage[:, b, :], p_proj[b], ACT.Tanh, scale=0.5).then_inc(pp_tanh[b], 1)

            def square_heads(d, n, bank, b):
                wait(act, sm["tp_done"], n + 1)
                if not (isinstance(d["K"], int) and d["K"] == 0 and b == 0):
                    wait(act, sm["norm_chain"], d["K"] * 6 + 3 * b)
                act.activation(tmp[:, :], p_tr[bank], ACT.Square).then_inc(sm["sq_ready"], 1)

            def body(it, first):
                Q0 = (it + 1) * 16 + 8
                for s in range(16):
                    i = s // 2
                    d, u, before = proj_tile(it, first, s)
                    if d:
                        split_w(Q0 + (s + 2), (s + 2) % 4)
                        if s % 4 == 3:
                            evacuate(d, before, u, it, first)
                    cur = step_at(i, it, first)
                    back1 = step_at(i - 1, it, first)
                    back2 = step_at(i - 2, it, first)
                    tb = turned_before(it, first, s)
                    if tb and tb[0]["norm"]:
                        square_heads(tb[0], use_number(tb[1], it, first), bank_of(tb[1], first), tb[2])
                    if s % 2 == 0:
                        if back2 and back2["k"] == "A":
                            wait(act, sm["o_pow"], back2["G"] * 3 + 3)
                            wait(act, sm["o_read"], back2["G"] * 2 + 2)
                            act.activation(o_sb[:, 0:P], o_sb[:, 0:P], ACT.Copy, scale=ss_o[:, 0:1])\
                               .then_inc(sm["o_ready"], 1)
                        if back1:
                            wait(act, sm["pv_done"], back1["G"])
                            for m, (lo, hi) in enumerate(at_spans(back1)):
                                name = ("AT", back1["i"], m)
                                wait(act, sm["tp_done"], use_number(name, it, first) + 1)
                                act.activation(aT_hi[:, lo:hi], p_tr[bank_of(name, first)][:, 0:hi - lo],
                                               ACT.Copy).then_inc(sm["at_hi"], 1)
                        if cur and cur["k"] == "A":
                            exp_a(cur, 0)
                        elif cur:
                            exp_b(cur, it - AH)
                    else:
                        if cur and cur["k"] == "A":
                            exp_a(cur, 1)
                        if back1 and back1["k"] == "A":
                            wait(act, sm["pv_done"], back1["G"] + 1)
                            r0 = inv_sum[:, back1["i"] % 2, 0:1]
                            act.activation(p_junk[:, 0:P], p_o[:, 0:P], ACT.Square, scale=r0,
                                           accum_out=ss_o[:, 2:3]).then_inc(sm["o_read"], 1)
                            act.activation(o_sb[:, 0:P], p_o[:, 0:P], ACT.Copy, scale=r0)\
                               .then_inc(sm["o_read"], 1)
                        nk = cur["k"] if cur and i + 1 < NR else kind(first + 1) if i + 1 == NR else None
                        if nk:
                            name = ("T", (i + 1) % NR)
                            n = use_number(name, it, first)
                            bank = p_tr[bank_of(name, first)]
                            w = P if nk == "A" else 2 * P
                            wait(act, sm["tp_done"], n + 1)
                            act.activation(qT_hi[:, 0:w], bank[:, 0:w], ACT.Copy, scale=QSCALE)\
                               .then_inc(sm["t_hi"], 1)
                            j = (i + 1) % NR
                            act.activation(kT_hi[:, j * P:(j + 1) * P], bank[:, w:w + P], ACT.Copy)\
                               .then_inc(sm["t_hi"], 1)
                        if cur:
                            hi_v(cur, it)

            def hi_v(st, it):
                i, k = st["i"], st["k"]
                lo, w = (2 * P, P) if k == "A" else (3 * P, HD)
                if i == 0:
                    wait(act, sm["pv_done"], st["G"])
                wait(act, loaded[i % 2], loads_by(k, it, i))
                act.activation(v_hi[:, i, 0:w], qkv[:, i % 2, lo:lo + w], ACT.Copy).then_inc(sm["v_hi_ready"], 1)

            def exp_a(st, c):
                wait(act, sm["max_ready"], st["G"] * 2 + (c + 1))
                if c == 0:
                    wait(act, sm["comb_done"], st["G"])
                w = (st["i"] + 1) * P
                flat = p_s.rearrange("p a b -> p (a b)")
                act.activation(expd[:, c, 0:w], flat[:, 0:w], ACT.Exp, bias=neg_max[:, c:c + 1],
                               accum_out=sums[:, c:c + 1]).then_inc(sm["x_done"], 1)

            def exp_b(st, j):
                gb = st["G"] - AH * NR
                lo = P if st["i"] == 0 else 0
                wait(act, sm["sink_ready"], gb * 4 + 4)
                wait(act, sm["b_sum"], gb * 2)
                for r in range(2):
                    for p in range(2):
                        n = 2 * r + p
                        ins = act.activation(expd[:, st["i"] % 2, n * 256 + lo:n * 256 + 256],
                                             p_s[:, r, p * 256 + lo:p * 256 + 256], ACT.Exp,
                                             bias=neg_max[:, n:n + 1], accum_out=sums[:, n:n + 1])
                    ins.then_inc(sm["x_done"], 1)
                act.activation(sink_e[:, :], neg_max[:, 4:8], ACT.Exp).then_inc(sm["sink_exp"], 1)

            for Q in range(2):
                split_w(Q, Q)
            for s in range(8):
                split_w(s + 2, (s + 2) % 4)
                u = s // 4
                if s % 4 == 3:
                    evacuate(KV_TILES[u], KV_TILES[0] if u else None, u, -1, -1)
                if 4 <= s < 6:
                    square_heads(KV_TILES[0], 32 + s - 4, (32 + s - 4) % 2, s - 4)
            iterations(act, body)

            act.wait_ge(sm["w_used"], NQ_IN)

            def y_piece(k, half):
                n = half * KT + k
                act.wait_ge(y_in[n % 2], 16 * (n // 2 + 1))
                act.activation(hT_hi[:, k, half * 512:(half + 1) * 512], x_sc[:, n % 2, :], ACT.Copy)\
                   .then_inc(sm["y_hi"], 1)

            for k in range(KT):
                y_piece(k, 0)
            for half, n2 in ((h, m) for h in range(2) for m in range(2)):
                for g in range(2):
                    for k in range(KT):
                        Q = NQ_IN + 64 * half + 32 * n2 + 16 * g + k + 2
                        if Q < NQ_IN + 128:
                            split_w(Q, Q % 4)
                        if half == n2 == g == 0:
                            y_piece(k, 1)

        @block.tensor
        def _(pe):
            def three(dst, a_hi, a_lo, b_hi, b_lo, start, stop):
                pe.matmul(dst, a_hi, b_hi, start=start, stop=False)
                pe.matmul(dst, a_hi, b_lo, start=False, stop=False)
                return pe.matmul(dst, a_lo, b_hi, start=False, stop=stop)

            def bank_free(n):
                wait(pe, sm["tp_free"], n - 1)

            pe.wait_ge(sm["ident_ready"], 2)
            for r in range(NR):
                pe.wait_ge(sm["x_scaled"], r + 1)
                for g in range(4):
                    n = 4 * r + g
                    bank_free(n)
                    for k in range(4):
                        f = (4 * g + k) * P
                        mm = pe.transpose(p_tr[n % 2][:, k * P:(k + 1) * P], x_buf[r % 2][:, f:f + P], ident[:, :])
                    mm.then_inc(sm["tp_done"], 1)

            def quarter(u, q, b, before):
                if b == 0:
                    wait(pe, sm["w_lo_ready"], u * 4 + (q + 1))
                if q == 0 and before is not None:
                    if before["turned"]:
                        wait(pe, pp_copied[b], before["T"] + 1)
                    else:
                        wait(pe, pp_gated[b], before["GT"] + 1)
                for k in range(4):
                    w = slice(k * P, (k + 1) * P)
                    t = slice(b * 512, (b + 1) * 512)
                    kk = 4 * q + k
                    mm = three(p_proj[b], w_hi[:, q, w], w_lo[:, q, w], hT_hi[:, kk, t], hT_lo[:, kk, t],
                               kk == 0, kk == KT - 1)
                if b:
                    mm.then_inc(sm["w_used"], 1)
                elif q == 3:
                    mm.then_inc(sm["pp_done"], 1)

            def turn_tile(d, b, n, bank):
                wait(pe, pp_copied[b], d["T"] + 1)
                bank_free(n)
                for r in range(4):
                    mm = pe.transpose(p_tr[bank][:, r * P:(r + 1) * P], stage[:, b, r * P:(r + 1) * P], ident[:, :])
                mm.then_inc(sm["tp_done"], 1)

            def scores_a(st, c, it, first):
                i = st["i"]
                w = (i + 1) * P
                if c == 0:
                    wait(pe, sm["tp_free"], qk_split(i, it, first))
                wait(pe, sm["x_done"], st["G"] * 2 + c)
                flat = p_s.rearrange("p a b -> p (a b)")
                h = slice(c * HD, (c + 1) * HD)
                for lo in range(0, w, 512):
                    t = slice(lo, min(w, lo + 512))
                    mm = three(flat[:, t], qT_hi[h, 0:P], qT_lo[h, 0:P], kT_hi[h, t], kT_lo[h, t], True, True)
                mm.then_inc(sm["s_done"], 1)

            def scores_b(st, it, first):
                i = st["i"]
                wait(pe, sm["tp_free"], qk_split(i, it, first))
                wait(pe, sm["x_done"], st["G"] * 2)
                t = slice(max(i - 1, 0) * P, (i + 1) * P)
                lo = P if i == 0 else 0
                for r in range(2):
                    h = slice(r * HD, (r + 1) * HD)
                    for p in range(2):
                        mm = three(p_s[:, r, p * 256 + lo:p * 256 + 256], qT_hi[h, p * P:(p + 1) * P],
                                   qT_lo[h, p * P:(p + 1) * P], kT_hi[h, t], kT_lo[h, t], True, True)
                    mm.then_inc(sm["s_done"], 1)

            def turn_probs(st, it, first):
                i = st["i"]
                if st["k"] == "A":
                    wait(pe, sm["comb_done"], st["G"] + 1)
                    blocks = [expd[:, 1, b * P:(b + 1) * P] for b in range(i + 1)]
                else:
                    wait(pe, sm["probs_scaled"], st["G"] - (AH * NR - 1))
                    blocks = [expd[:, i % 2, n * 256 + b * P:n * 256 + (b + 1) * P]
                              for n in range(4) for b in ((0, 1) if i else (1,))]
                for m, (lo, hi) in enumerate(at_spans(st)):
                    name = ("AT", i, m)
                    bank_free(use_number(name, it, first))
                    for b in range((hi - lo) // P):
                        mm = pe.transpose(p_tr[bank_of(name, first)][:, b * P:(b + 1) * P],
                                          blocks[lo // P + b], ident[:, :])
                    mm.then_inc(sm["tp_done"], 1)

            def values(st, it, first):
                i = st["i"]
                last = ("AT", i, len(at_spans(st)) - 1)
                wait(pe, sm["v_split"], st["G"] + 1)
                wait(pe, sm["tp_free"], use_number(last, it, first) + 1)
                wait(pe, sm["o_read"], st["G"] * 2)
                if st["k"] == "A":
                    for b in range(i + 1):
                        a = slice(b * P, (b + 1) * P)
                        mm = three(p_o[:, 0:P], aT_hi[:, a], aT_lo[:, a], v_hi[:, b, :], v_lo[:, b, :], b == 0, b == i)
                else:
                    nb = 2 if i else 1
                    a_hi, a_lo = (a[:, 0:4 * nb * P].rearrange("k (n b t) -> k b n t", n=4, b=nb)
                                  for a in (aT_hi, aT_lo))
                    dst = p_o[0:HD, :].rearrange("d (n t) -> d n t", n=4)
                    for b in range(nb):
                        vb = i - (nb - 1) + b
                        mm = three(dst, v_hi[:, vb, 0:HD], v_lo[:, vb, 0:HD], a_hi[:, b], a_lo[:, b],
                                   b == 0, b == nb - 1)
                mm.then_inc(sm["pv_done"], 1)

            def turn_o(st, it, first):
                name = ("YT", st["i"])
                wait(pe, sm["o_ready"], st["G"] + 1)
                bank_free(use_number(name, it, first))
                pe.transpose(p_tr[bank_of(name, first)][:, 0:P], o_sb[:, 0:P], ident[:, :])\
                  .then_inc(sm["tp_done"], 1)

            def turn_qk(nk, i, it, first):
                name = ("T", i)
                wait(pe, loaded[i % 2], loads_by(nk, it + 1 if i == 0 else it, i))
                n = use_number(name, it, first)
                bank_free(n)
                bank = p_tr[bank_of(name, first)]
                for a in range(2 if nk == "A" else 3):
                    mm = pe.transpose(bank[:, a * P:(a + 1) * P], qkv[:, i % 2, a * P:(a + 1) * P], ident[:, :])
                mm.then_inc(sm["tp_done"], 1)

            def body(it, first):
                for s in range(16):
                    i = s // 2
                    d, u, before = proj_tile(it, first, s)
                    cur = step_at(i, it, first)
                    back1 = step_at(i - 1, it, first)
                    back2 = step_at(i - 2, it, first)
                    tb = turned_before(it, first, s)
                    if d:
                        quarter(u, s % 4, 0, before)
                    if s % 2 == 0:
                        if tb:
                            turn_tile(tb[0], tb[2], use_number(tb[1], it, first), bank_of(tb[1], first))
                    elif back2 and back2["k"] == "A":
                        turn_o(back2, it, first)
                    if d:
                        quarter(u, s % 4, 1, before)
                    if s % 2 == 0:
                        if cur and cur["k"] == "A":
                            scores_a(cur, 0, it, first)
                        elif cur:
                            scores_b(cur, it, first)
                        if back1:
                            turn_probs(back1, it, first)
                        continue
                    if tb:
                        turn_tile(tb[0], tb[2], use_number(tb[1], it, first), bank_of(tb[1], first))
                    if cur and cur["k"] == "A":
                        scores_a(cur, 1, it, first)
                    if back1:
                        values(back1, it, first)
                    nk = cur["k"] if cur and i + 1 < NR else kind(first + 1) if i + 1 == NR else None
                    if nk:
                        turn_qk(nk, (i + 1) % NR, it, first)

            pe.wait_ge(sm["x_lo"], 32)
            for s in range(8):
                u = s // 4
                for b in range(2):
                    quarter(u, s % 4, b, KV_TILES[0] if u else None)
                if 4 <= s < 6:
                    turn_tile(KV_TILES[0], s - 4, 32 + s - 4, s % 2)
            iterations(pe, body)

            for half in range(2):
                for n in range(4):
                    g = 4 * half + n
                    bank = (ps_a, ps_b)[g % 2]
                    if g == 0:
                        for b in range(2):
                            pe.wait_ge(pp_gated[b], AH + 2 * BC)
                        pe.wait_ge(sm["x_done"], 2 * NR * len(KINDS))
                    elif g == 1:
                        pe.wait_ge(sm["tp_free"], BASE[12] + len(uses_of(12)))
                        pe.wait_ge(sm["o_read"], 2 * NR * len(KINDS))
                    else:
                        pe.wait_ge(sm["out_ready"], 4 * (g - 1))
                    for k in range(KT):
                        pe.wait_ge(sm["w_lo_ready"], NQ_IN + 16 * g + k + 1)
                        pe.wait_ge(sm["y_lo"], KT * half + k + 1)
                        for r in range(4):
                            t = slice(half * 512 + r * P, half * 512 + (r + 1) * P)
                            mm = three(bank[:, r, :], hT_hi[:, k, t], hT_lo[:, k, t],
                                       w_hi[:, k % 4, :], w_lo[:, k % 4, :], k == 0, k == KT - 1)
                        mm.then_inc(sm["w_used"], 1)

        @block.vector
        def _(dve):
            links = [0]

            def link(ins):
                links[0] += 1
                ins.then_inc(sm["ang"], 1)
                dve.wait_ge(sm["ang"], links[0])

            def tt(o, a, b, op):
                return dve.tensor_tensor(o, a, b, op)

            ang = tmp[:, 256:512]
            ang3 = ang.rearrange("p (r f) -> p r f", r=NR)
            dve.wait_ge(sm["pos_in"], 32)
            link(dve.tensor_copy(pos_f[:, :], pos_i[:, :]))
            link(tt(ang3, pos_f[:, :].unsqueeze(2).to_broadcast([P, NR, HALF]),
                    tmp[:, 0:HALF].unsqueeze(1).to_broadcast([P, NR, HALF]), ALU.mult))
            left, parts = 2 * math.pi, []
            for _ in range(3):
                e = 2.0 ** (math.floor(math.log2(left)) - 7)
                parts.append(math.floor(left / e) * e)
                left -= parts[-1]
            parts.append(left)
            magic = 1.5 * 2.0 ** 23
            turns = o_sb[:, :]
            for table, quarter_turn in ((cos_t, 0.25), (sin_t, 0.0)):
                t2 = table[:, :, :].rearrange("p r f -> p (r f)")
                link(dve.tensor_scalar(turns, ang, 0.5 / math.pi, quarter_turn, ALU.mult, ALU.add))
                link(dve.tensor_scalar(turns, turns, magic, magic, ALU.add, ALU.subtract))
                src = ang
                for c in parts:
                    link(dve.scalar_tensor_tensor(t2, turns, -c, src, ALU.mult, ALU.add))
                    src = t2
                link(dve.tensor_scalar(t2, t2, quarter_turn * 2 * math.pi, 3.1415925, ALU.add, ALU.min))
                dve.tensor_scalar(t2, t2, -3.1415925, None, ALU.max).then_inc(sm["rope_arg"], 1)

            dve.wait_ge(sm["lam_in"], 64)
            lv = qkv[:, 0, 0:256].rearrange("p (a b c) -> p a b c", a=2, b=2)
            prod = qkv[:, 1, 0:128].rearrange("p (a c) -> p a c", a=2)
            link(tt(prod, lv[:, :, 0, :], lv[:, :, 1, :], ALU.mult))
            dve.tensor_reduce(neg_lam[:, 0:2], prod, AX, ALU.add).then_inc(sm["lam_sum"], 1)
            dve.wait_ge(sm["lam_exp"], 1)
            link(tt(neg_lam[:, 4:5], neg_lam[:, 3:4], neg_lam[:, 2:3], ALU.subtract))
            link(dve.tensor_scalar(neg_lam[:, 5:6], neg_lam[:, 4:5], LAM_INIT, None, ALU.subtract))
            dve.wait_ge(sm["par_in"], 16 * 7)
            link(dve.tensor_scalar(sub_c[:, 1:2], sub_c[:, 0:1], 0.5 * (1 - LAM_INIT), None, ALU.mult))

            def x_lo_part(n):
                r, g = n // 4, n % 4
                dst = (slice(None), slice(4 * g, 4 * g + 4), slice(r * P, (r + 1) * P))
                dve.wait_ge(sm["x_hi"], n + 1)
                tt(hT_lo[dst], x_sc[:, n % 2, :].rearrange("p (k t) -> p k t", k=4),
                   hT_hi[dst].bitcast(F32), ALU.subtract).then_inc(sm["x_lo"], 1)

            for n in range(4 * NR):
                g = n % 4
                dve.wait_ge(sm["tp_done"], n + 1)
                if n >= 2:
                    dve.wait_ge(sm["x_lo"], n - 1)
                tt(x_sc[:, n % 2, :].rearrange("p (k t) -> p k t", k=4),
                   p_tr[n % 2].rearrange("p (k t) -> p k t", k=4),
                   norm_c[:, 4 * g:4 * g + 4].unsqueeze(2).to_broadcast([P, 4, P]), ALU.mult)\
                    .then_inc(sm["tp_free"], 1)
                if n:
                    x_lo_part(n - 1)
            x_lo_part(4 * NR - 1)

            def split_w(Q, b4):
                wait(dve, sm["w_hi_ready"], Q + 1)
                tt(w_lo[:, b4, :], w_raw[:, b4 % 2, :], w_hi[:, b4, :].bitcast(F32), ALU.subtract)\
                    .then_inc(sm["w_lo_ready"], 1)

            def gate(d, b):
                wait(dve, pp_tanh[b], d["GT"] + 1)
                dve.scalar_tensor_tensor(stage[:, b, :], stage[:, b, :], 1.0, p_proj[b], ALU.add, ALU.mult)\
                   .then_inc(pp_gated[b], 1)

            def rows_out(d, b, n, bank):
                dst = rows[:, b, :]
                wait(dve, stored[b], d["T"] * 16)
                if not d["norm"]:
                    wait(dve, sm["tp_done"], n + 1)
                    dve.tensor_copy(dst, p_tr[bank]).then_inc(sm["tp_free"], 1)
                    return
                seq = d["K"] * 2 + b
                wait(dve, sm["sq_ready"], seq + 1)
                dve.tensor_reduce(ss_h[:, 0:8], tmp[:, :].rearrange("p (g c) -> p g c", g=8), AX, ALU.add)\
                   .then_inc(sm["ss_ready"], 1)
                x3 = dst.rearrange("p (g c) -> p g c", g=8)
                tt(x3, p_tr[bank].rearrange("p (g c) -> p g c", g=8),
                   head_w[:, d["w"], :].unsqueeze(1).to_broadcast([P, 8, HD]), ALU.mult)\
                    .then_inc(sm["tp_free"], 1)

            def rotate(d, b, n):
                if not d["norm"]:
                    return
                seq = d["K"] * 2 + b
                dst = rows[:, b, :]
                x3 = dst.rearrange("p (g c) -> p g c", g=8)
                x5 = dst.rearrange("p (r h f c) -> p r h f c", r=4, h=2, f=2)
                t5 = tmp[:, :].rearrange("p (r h f c) -> p r h f c", r=4, h=2, f=2)
                r4 = slice(4 * b, 4 * b + 4)
                sn = sin_t[:, r4, :].unsqueeze(2).to_broadcast([P, 4, 2, HALF])
                cs = cos_t[:, r4, :].unsqueeze(2).to_broadcast([P, 4, 4, HALF])
                wait(dve, sm["tp_free"], n + 1)
                wait(dve, sm["ss_ready"], seq + 1)
                tt(t5[:, :, :, 0, :], x5[:, :, :, 1, :], sn, ALU.mult)
                tt(t5[:, :, :, 1, :], x5[:, :, :, 0, :], sn, ALU.mult).then_inc(sm["norm_chain"], 1)
                x4 = dst.rearrange("p (r g c) -> p r g c", r=4, g=4)
                wait(dve, sm["norm_chain"], seq * 3 + 1)
                tt(x4, x4, cs, ALU.mult).then_inc(sm["norm_chain"], 1)
                wait(dve, sm["norm_chain"], seq * 3 + 2)
                tt(x5[:, :, :, 0, :], x5[:, :, :, 0, :], t5[:, :, :, 0, :], ALU.subtract)
                tt(x5[:, :, :, 1, :], x5[:, :, :, 1, :], t5[:, :, :, 1, :], ALU.add)\
                    .then_inc(sm["norm_chain"], 1)
                wait(dve, sm["norm_chain"], seq * 3 + 3)
                wait(dve, sm["rs_ready"], seq * 3 + 3)
                tt(x3, x3, ss_h[:, 16:24].unsqueeze(2).to_broadcast([P, 8, HD]), ALU.mult)\
                    .then_inc(rst_ready[b], 1)

            def max_a(st, c):
                i = st["i"]
                flat = p_s.rearrange("p a b -> p (a b)")
                last = flat[:, i * P:(i + 1) * P]
                n = st["G"] * 2 + (c + 1)
                wait(dve, sm["s_done"], n)
                tt(last, last, mask[:, P:2 * P], ALU.add).then_inc(sm["masked"], 1)
                wait(dve, sm["masked"], n)
                dve.tensor_reduce(neg_max[:, c:c + 1], flat[:, 0:(i + 1) * P], AX, ALU.max, negate=True)\
                   .then_inc(sm["max_ready"], 1)

            def max_b(st, j):
                lo = P if st["i"] == 0 else 0
                gb = st["G"] - AH * NR
                for r in range(2):
                    wait(dve, sm["s_done"], st["G"] * 2 + (r + 1))
                    part = p_s[:, r, :].rearrange("p (a b) -> p a b", a=2)[:, :, lo:256]
                    tt(part, part, mask[:, lo:256].unsqueeze(1).to_broadcast([P, 2, 256 - lo]), ALU.add)\
                        .then_inc(sm["masked"], 1)
                wait(dve, sm["masked"], st["G"] * 2 + 2)
                sk = sink_t[:, bass.ds(j * 4, 4)].rearrange("t (p r) -> t r p", r=2)
                low, high = (neg_max[:, n:n + 4].rearrange("t (r p) -> t r p", r=2) for n in (0, 4))
                flat = p_s.rearrange("p a b -> p (a b)").rearrange("p (n s) -> p n s", n=4)
                dve.tensor_reduce(neg_max[:, 0:4], flat[:, :, lo:256], AX, ALU.max).then_inc(sm["sink_ready"], 1)
                wait(dve, sm["sink_ready"], gb * 4 + 1)
                tt(high, low, sk, ALU.max).then_inc(sm["sink_ready"], 1)
                wait(dve, sm["sink_ready"], gb * 4 + 2)
                dve.tensor_scalar(neg_max[:, 0:4], neg_max[:, 4:8], -1.0, None, ALU.mult)\
                   .then_inc(sm["sink_ready"], 1)
                wait(dve, sm["sink_ready"], gb * 4 + 3)
                tt(high, low, sk, ALU.add).then_inc(sm["sink_ready"], 1)

            def lo_probs(st, it, first):
                for m, (lo, hi) in enumerate(at_spans(st)):
                    name = ("AT", st["i"], m)
                    if st["k"] == "A":
                        seq = st["unit"] * 12 + sum(N_AT_A[:st["i"]]) + m
                    else:
                        seq = (st["unit"] - AH) * 16 + (12 * AH + 2 * st["i"] + m)
                    wait(dve, sm["at_hi"], seq + 1)
                    tt(aT_lo[:, lo:hi], p_tr[bank_of(name, first)][:, 0:hi - lo], aT_hi[:, lo:hi].bitcast(F32),
                       ALU.subtract).then_inc(sm["tp_free"], 1)

            def lo_qk(nk, i, it, first):
                name = ("T", i)
                bank = p_tr[bank_of(name, first)]
                w = P if nk == "A" else 2 * P
                unit = it + 1 if i == 0 else it
                wait(dve, sm["t_hi"], (unit * NR + i) * 2 + 2)
                dve.scalar_tensor_tensor(qT_lo[:, 0:w], bank[:, 0:w], QSCALE, qT_hi[:, 0:w].bitcast(F32),
                                         ALU.mult, ALU.subtract)
                tt(kT_lo[:, i * P:(i + 1) * P], bank[:, w:w + P], kT_hi[:, i * P:(i + 1) * P].bitcast(F32),
                   ALU.subtract).then_inc(sm["tp_free"], 1)

            def combine(st):
                inv = inv_sum[:, st["i"] % 2, :]
                wait(dve, sm["x_done"], st["G"] * 2 + 2)
                dve.reciprocal(inv[:, 0:2], sums[:, 0:2]).then_inc(sm["comb_chain"], 1)
                wait(dve, sm["comb_chain"], st["G"] * 2 + 1)
                dve.tensor_scalar(coef[:, :], sums[:, 0:1], neg_lam[:, 5:6], inv[:, 1:2], ALU.mult, ALU.mult)\
                   .then_inc(sm["comb_chain"], 1)
                wait(dve, sm["comb_chain"], st["G"] * 2 + 2)
                w = (st["i"] + 1) * P
                dve.scalar_tensor_tensor(expd[:, 1, 0:w], expd[:, 1, 0:w], coef[:, :], expd[:, 0, 0:w],
                                         ALU.mult, ALU.add).then_inc(sm["comb_done"], 1)

            def sum_b(st):
                gb = st["G"] - AH * NR
                wait(dve, sm["sink_exp"], gb + 1)
                tt(sums[:, :], sums[:, :], sink_e[:, :], ALU.add).then_inc(sm["b_sum"], 1)
                wait(dve, sm["b_sum"], gb * 2 + 1)
                dve.reciprocal(inv_sum[:, st["i"] % 2, :], sums[:, :]).then_inc(sm["b_sum"], 1)

            def y_out(st, it, first):
                i = st["i"]
                wait(dve, gate_ld[i % 2], stored_before(st) + (16 if st["k"] == "A" else 32))
                if st["k"] == "A":
                    name, w = ("YT", i), P
                    wait(dve, sm["tp_done"], use_number(name, it, first) + 1)
                    dve.scalar_tensor_tensor(gate_y[:, i % 2, 0:w], p_tr[bank_of(name, first)][:, 0:w], sub_c[:, 1:2],
                                             gate_y[:, i % 2, 0:w], ALU.mult, ALU.mult).then_inc(sm["tp_free"], 1)
                else:
                    wait(dve, sm["pv_done"], st["G"] + 1)
                    dve.scalar_tensor_tensor(gate_y[0:HD, i % 2, :], p_o[0:HD, :], 0.5, gate_y[0:HD, i % 2, :],
                                             ALU.mult, ALU.mult).then_inc(sm["o_read"], 2)

            dve.wait_ge(sm["consts"], 8)
            dve.wait_ge(sm["rope_ready"], 2)
            for Q in range(2):
                split_w(Q, Q)
            for s in range(8):
                split_w(s + 2, (s + 2) % 4)
                if 4 <= s < 6:
                    rows_out(KV_TILES[0], s - 4, 32 + s - 4, s % 2)
                    rotate(KV_TILES[0], s - 4, 32 + s - 4)

            def body(it, first):
                Q0 = (it + 1) * 16 + 8
                for s in range(16):
                    i = s // 2
                    d, u, before = proj_tile(it, first, s)
                    if d:
                        split_w(Q0 + (s + 2), (s + 2) % 4)
                    cur = step_at(i, it, first)
                    back1 = step_at(i - 1, it, first)
                    back2 = step_at(i - 2, it, first)
                    if back2 and back2["k"] == ("A" if s % 2 else "B"):
                        y_out(back2, it, first)
                    if d and s % 4 == 3 and not d["turned"]:
                        gate(d, 0)
                        gate(d, 1)
                    if s % 2 and cur and cur["k"] == "B":
                        sum_b(cur)
                    tb = turned_before(it, first, s)
                    if tb:
                        n = use_number(tb[1], it, first)
                        rows_out(tb[0], tb[2], n, bank_of(tb[1], first))
                    if s % 2 == 0:
                        if cur and cur["k"] == "A":
                            max_a(cur, 0)
                        elif cur:
                            max_b(cur, it - AH)
                        if back1:
                            lo_probs(back1, it, first)
                    else:
                        if cur and cur["k"] == "A":
                            max_a(cur, 1)
                        nk = cur["k"] if cur and i + 1 < NR else kind(first + 1) if i + 1 == NR else None
                        if nk:
                            lo_qk(nk, (i + 1) % NR, it, first)
                        if cur and cur["k"] == "A":
                            combine(cur)
                    if tb:
                        rotate(tb[0], tb[2], n)

            iterations(dve, body)

            def y_piece(k, half):
                dst = (slice(None), k, slice(half * 512, (half + 1) * 512))
                n = half * KT + k
                dve.wait_ge(sm["y_hi"], n + 1)
                tt(hT_lo[dst], x_sc[:, n % 2, :], hT_hi[dst].bitcast(F32), ALU.subtract).then_inc(sm["y_lo"], 1)

            for k in range(KT):
                y_piece(k, 0)
            for g in range(8):
                for k in range(KT):
                    Q = NQ_IN + 16 * g + k + 2
                    if Q < NQ_IN + 128:
                        split_w(Q, Q % 4)
                    if g == 0:
                        y_piece(k, 1)
                dve.wait_ge(sm["w_used"], NQ_IN + 16 * (g + 1))
                dve.wait_ge(res_in[g % 2], 16 * (g // 2 + 1))
                res = x_buf[g % 2].rearrange("p (r c) -> p r c", r=4)
                for r in range(4):
                    tt(res[:, r, :], (ps_a, ps_b)[g % 2][:, r, :], res[:, r, :], ALU.add)\
                        .then_inc(sm["out_ready"], 1)

        @block.gpsimd
        def _(pool):
            pool.memset(ident[:, :], 0.0).then_inc(sm["ident_ready"], 1)
            pool.memset(mask[:, :], 0.0).then_inc(sm["consts"], 1)
            for c, value in enumerate((-0.5, EPS, 1 / HD, 1 / D, 1 / P)):
                pool.memset(small[:, c, :], value).then_inc(sm["consts"], 1)
            pool.wait_ge(sm["ident_ready"], 1)
            pool.affine_select(out=ident[:, :], in_=ident[:, :], compare_op=ALU.not_equal, fill=1.0, base=0,
                               pattern=[[-1, P]], channel_multiplier=1).then_inc(sm["ident_ready"], 1)
            pool.wait_ge(sm["consts"], 6)
            pool.affine_select(out=mask[:, 0:P], in_=mask[:, 0:P], compare_op=ALU.is_gt, fill=NEG, base=0,
                               pattern=[[1, P]], channel_multiplier=-1).then_inc(sm["consts"], 1)
            pool.affine_select(out=mask[:, P:2 * P], in_=mask[:, P:2 * P], compare_op=ALU.is_ge, fill=NEG, base=0,
                               pattern=[[-1, P]], channel_multiplier=1).then_inc(sm["consts"], 1)

            def inv_rms(src, mean, dst, c, s, before):
                w = src.shape[1]
                pool.tensor_tensor(mean, src, small[:, c, 0:w], ALU.mult).then_inc(s, 1)
                wait(pool, s, before + 1)
                pool.tensor_tensor(mean, mean, small[:, 1, 0:w], ALU.add).then_inc(s, 1)
                wait(pool, s, before + 2)
                pool.tensor_tensor(dst, mean, small[:, 0, 0:w], ALU.pow).then_inc(s, 1)

            for r in range(NR):
                pool.wait_ge(sm["x_sq"], r + 1)
                inv_rms(ss_x[:, r:r + 1], ss_x[:, NR + r:NR + r + 1], ss_x[:, r:r + 1], 3, sm["x_pow"], 3 * r)

            def norms(d, b):
                seq = d["K"] * 2 + b
                wait(pool, sm["ss_ready"], seq + 1)
                inv_rms(ss_h[:, 0:8], ss_h[:, 8:16], ss_h[:, 16:24], 2, sm["rs_ready"], seq * 3)

            def lo_v(st):
                i, k = st["i"], st["k"]
                lo, w = (2 * P, P) if k == "A" else (3 * P, HD)
                wait(pool, sm["v_hi_ready"], st["G"] + 1)
                pool.tensor_tensor(v_lo[:, i, 0:w], qkv[:, i % 2, lo:lo + w], v_hi[:, i, 0:w].bitcast(F32),
                                   ALU.subtract).then_inc(sm["v_split"], 1)

            def scale_probs(st):
                i, lo = st["i"], P if st["i"] == 0 else 0
                wait(pool, sm["b_sum"], (st["G"] - AH * NR) * 2 + 2)
                part = expd[:, i % 2, :].rearrange("p (n s) -> p n s", n=4)[:, :, lo:256]
                pool.tensor_tensor(part, part, inv_sum[:, i % 2, :].unsqueeze(2).to_broadcast([P, 4, 256 - lo]),
                                   ALU.mult).then_inc(sm["probs_scaled"], 1)

            for s in range(4, 6):
                norms(KV_TILES[0], s - 4)

            def body(it, first):
                for s in range(16):
                    i = s // 2
                    cur = step_at(i, it, first)
                    back1 = step_at(i - 1, it, first)
                    if s % 2 and cur and cur["k"] == "B":
                        scale_probs(cur)
                    tb = turned_before(it, first, s)
                    if tb and tb[0]["norm"]:
                        norms(tb[0], tb[2])
                    if s % 2:
                        if back1 and back1["k"] == "A":
                            wait(pool, sm["o_read"], back1["G"] * 2 + 1)
                            inv_rms(ss_o[:, 2:3], ss_o[:, 1:2], ss_o[:, 0:1], 4, sm["o_pow"], back1["G"] * 3)
                        if cur:
                            lo_v(cur)

            iterations(pool, body)


_INS = ["x", "positions", "norm_w", "w_in", "q_norm_a", "k_norm_a", "lambda_q1", "lambda_k1", "lambda_q2",
        "lambda_k2", "subln_w", "q_norm_b", "k_norm_b", "sinks", "w_out"]


def kernel(**inputs):
    import concourse.bacc as bacc
    from concourse.bass_utils import run_bass_kernel_spmd

    nc = bacc.Bacc("TRN2", target_bir_lowering=False, num_devices=1)
    arrays, args = {}, []
    for name in _INS:
        a = np.ascontiguousarray(inputs[name])
        arrays[f"in_{name}"] = a
        args.append(nc.dram_tensor(f"in_{name}", a.shape, mybir.dt.from_np(a.dtype), kind="ExternalInput").ap())
    freq = (np.float32(10000.0) ** (-(np.arange(0, HD, 2, dtype=np.float32) / np.float32(HD)))).astype(np.float32)
    arrays["in_inv_freq"] = freq.reshape(1, HALF)
    args.append(nc.dram_tensor("in_inv_freq", (1, HALF), F32, kind="ExternalInput").ap())
    out = nc.dram_tensor("out_0", (1, S, D), F32, kind="ExternalOutput").ap()
    decoder_layer(nc, *args, out)
    r = run_bass_kernel_spmd(nc, [arrays], core_ids=[0])
    return r.results[0]["out_0"]
```

```python
import math
from contextlib import ExitStack

import concourse.bass as bass
import numpy as np
from concourse import mybir

F32 = mybir.dt.float32
F32R = mybir.dt.float32r
I32 = mybir.dt.int32
ALU = mybir.AluOpType
ACT = mybir.ActivationFunctionType
AX = mybir.AxisListType.X

P = 128
D = 2048
S = 1024
HD = 64
HALF = HD // 2
NR = S // P
KT = D // P
AH = 8
BC = 4
AW = 1024
QB0 = 4 * AW
KB0 = QB0 + 1024
VB0 = KB0 + 128
GB0 = VB0 + 128
EPS = 1e-6
NEG = -1e30
LAM_INIT = 0.8 - 0.6 * math.exp(-0.3 * 0)
QSCALE = HD ** -0.5
NQ_IN = 4 * (2 + 4 * (AH + BC))
N_AT_A = [1, 1, 1, 1, 2, 2, 2, 2]

KINDS = "A" * AH + "B" * BC
PHASES = [(0, 1), (1, 6), (7, 1), (8, 1), (9, 1), (10, 1), (11, 1), (12, 1)]
SP_PHASES = [(0, 1), (1, 5), (6, 1), (7, 1), (8, 1), (9, 1), (10, 1), (11, 1), (12, 1)]


OK = 12
GROUPS = [(h, n) for h in range(2) for n in (1, 2, 3)] + [(0, 0), (1, 0)]
OUT_TILES = [(g, k) for g, (h, n) in enumerate(GROUPS) for k in range(0 if n else OK, KT)]
NQ_OUT = NQ_IN + 16
Y_PARTS = [(0, 3), (3, 6), (6, 9), (9, 12), (12, 14), (14, 16)]


def kind(it):
    return KINDS[it] if 0 <= it < len(KINDS) else None


def proj_kind(it):
    return "O" if it == len(KINDS) else kind(it)


def tile_desc(c, p):
    k, c = c
    if k == "O":
        return dict(kind=k, p=p, T=26 + 2 * BC + p, GT=0, norm=False, turned=True)
    if k == "A":
        return dict(unit=c, p=p, kind=k, T=c * 3 + (2 + min(p, 3)), K=c * 2 + (1 + p), GT=c, w=p,
                    norm=p < 2, turned=p < 3)
    return dict(unit=c, p=p, kind=k, T=c * 2 + (26 - 2 * AH + min(p, 2)), K=c * 2 + (17 - 2 * AH + p),
                GT=c * 2 + (8 - 2 * AH + max(p - 2, 0)), w=2, norm=p < 2, turned=p < 2)


KV_TILES = [dict(kind="kv", p=0, T=0, K=0, GT=0, w=3, norm=True, turned=True),
            dict(kind="kv", p=1, T=1, K=1, GT=0, w=3, norm=False, turned=True)]


def step_at(i, it, first_it):
    back = i < 0
    k = kind(first_it - 1 if back else first_it)
    i = i % NR
    unit = it - 1 if back else it
    return dict(i=i, k=k, G=unit * NR + i, unit=unit) if k else None


def uses_of(first_it):
    out = []
    cur, prev, nxt = kind(first_it), kind(first_it - 1), kind(first_it + 1)
    proj = proj_kind(first_it + 1)
    for s in range(16):
        i = s // 2
        turned = []
        if s % 4 < 2 and s >= 4:
            p = s // 4 - 1
            if proj and tile_desc((proj, 0), p)["turned"]:
                turned.append(("PT", p, s % 2))
        elif s < 2 and first_it in (-1, len(KINDS)):
            turned.append(("PT", "before", s))
        if s % 2 == 0:
            out += turned
            k, j = (cur, i - 1) if i >= 1 else (prev, NR - 1)
            if k:
                out += [("AT", j, m) for m in range(2 if k == "B" else N_AT_A[j])]
        else:
            k, j = (cur, i - 2) if i >= 2 else (prev, NR - 2 + i)
            if k == "A":
                out.append(("YT", j))
            out += turned
            if i + 1 < NR and cur or i + 1 == NR and nxt:
                out.append(("T", (i + 1) % NR))
    return out


KV_USES = [("PT", "k", 0), ("PT", "k", 1)]
BASE = {}


def _count_bases():
    n = 32 + len(KV_USES)
    for it in range(-1, 13):
        BASE[it] = n
        n += len(uses_of(it))
    return n


_count_bases()


def use_number(name, it, first_it):
    return BASE[first_it] + uses_of(first_it).index(name) + (it - first_it) * len(uses_of(first_it))


def bank_of(name, first_it):
    return (BASE[first_it] + uses_of(first_it).index(name)) % 2


def qk_split(i, it, first):
    if i:
        return use_number(("T", i), it, first) + 1
    return BASE[first] + (it - first) * len(uses_of(first))


def at_spans(st):
    if st["k"] == "A":
        w = (st["i"] + 1) * P
        return [(0, min(w, 512))] + ([(512, w)] if w > 512 else [])
    return [(0, 512), (512, 1024)] if st["i"] else [(0, 256), (256, 512)]


def loads_by(k, unit, i):
    if k == "A":
        return unit * 64 + 16 * (i // 2 + 1)
    return (unit - AH) * 192 + (AH * 64 + 48 * (i // 2 + 1))


def stored_before(st):
    if st["k"] == "A":
        return st["unit"] * 64 + 16 * (st["i"] // 2)
    return (st["unit"] - AH) * 128 + (AH * 64 + 32 * (st["i"] // 2))


def decoder_layer(nc, x, positions, norm_w, w_in, q_norm_a, k_norm_a, lambda_q1, lambda_k1,
                  lambda_q2, lambda_k2, subln_w, q_norm_b, k_norm_b, sinks, w_out, inv_freq, out):
    for f, n in PHASES:
        assert n == 1 or len({len(uses_of(f + d)) for d in range(n)}) == 1
        assert n == 1 or len(uses_of(f)) % 2 == 0

    x2, out2 = x[0], out[0]
    scr_a = nc.dram_tensor("qkv_a_dram", (AH, S, 3 * P), F32).ap()
    scr_q = nc.dram_tensor("q_b_dram", (BC, S, 2 * P), F32).ap()
    scr_kv = nc.dram_tensor("kv_b_dram", (S, 2 * P), F32).ap()
    scr_g = nc.dram_tensor("gates_dram", (AH + 2 * BC, P, S), F32).ap()
    scr_part = nc.dram_tensor("out_part_dram", (S, 512), F32).ap()
    scr_y = nc.dram_tensor("y_dram", (D, S), F32).ap()

    with ExitStack() as ctx:
        def sb(name, shape, dt=F32):
            return ctx.enter_context(nc.sbuf_tensor(name, shape, dt))

        def sem(name):
            return ctx.enter_context(nc.semaphore(name))

        hT_hi = sb("hT_hi", [P, KT, S], F32R)
        hT_lo = sb("hT_lo", [P, KT, S], F32R)
        w_raw = sb("w_raw_sb", [P, 2, 512])
        w_hi = sb("w_hi_sb", [P, 4, 512], F32R)
        w_lo = sb("w_lo_sb", [P, 4, 512], F32R)
        kT_hi = sb("kT_hi", [P, S], F32R)
        kT_lo = sb("kT_lo", [P, S], F32R)
        v_hi = sb("v_hi_sb", [P, NR, P], F32R)
        v_lo = sb("v_lo_sb", [P, NR, P], F32R)
        qT_hi = sb("qT_hi", [P, 2 * P], F32R)
        qT_lo = sb("qT_lo", [P, 2 * P], F32R)
        expd = sb("expd", [P, 2, S])
        aT_hi = sb("aT_hi", [P, S], F32R)
        aT_lo = sb("aT_lo", [P, S], F32R)
        stage_rows = sb("stage_rows", [P, 4 * 512])
        tmp = sb("tmp", [P, 512])
        qkv = sb("qkv_sb", [P, 2, 448])
        gate_y = sb("gate_y", [P, 2, 512])
        o_sb = sb("o_sb", [P, 256])
        mask = sb("mask", [P, 2 * P])
        ident = sb("ident", [P, P])
        cos_t = sb("cos_t", [P, NR, HALF])
        sin_t = sb("sin_t", [P, NR, HALF])
        head_w = sb("head_w", [P, 4, HD])
        norm_c = sb("norm_c", [P, KT])
        sub_c = sb("sub_c", [P, 2])
        sink_t = sb("sink_t", [P, 4 * BC])
        pos_i = sb("pos_i", [P, NR], I32)
        pos_f = sb("pos_f", [P, NR])
        ss_x = sb("ss_x", [P, 2 * NR])
        small = sb("small", [P, 5, 8])
        neg_lam = sb("neg_lam", [P, 8])
        neg_max = sb("neg_max", [P, 8])
        sink_e = sb("sink_e", [P, 4])
        sums = sb("sums", [P, 4])
        inv_sum = sb("inv_sum", [P, 2, 4])
        coef = sb("coef", [P, 1])
        ss_o = sb("ss_o", [P, 3])
        ss_h = sb("ss_h", [P, 24])

        stage = stage_rows[:, 0:1024].rearrange("p (b c) -> p b c", b=2)
        rows = stage_rows[:, 1024:2048].rearrange("p (b c) -> p b c", b=2)
        x_buf = [expd[:, :, :].rearrange("p a b -> p (a b)"), stage_rows[:, :]]
        x_sc = gate_y

        ps_a = ctx.enter_context(nc.psum_tensor("ps_a", [P, 4, 512], F32))
        ps_b = ctx.enter_context(nc.psum_tensor("ps_b", [P, 4, 512], F32))
        p_proj = [ps_a[:, 0, :], ps_a[:, 1, :]]
        p_s = ps_a[:, 2:4, :]
        p_tr = [ps_b[:, 0, :], ps_b[:, 1, :]]
        p_o = ps_b[:, 2, :]
        p_junk = ps_b[:, 3, :]

        names = """consts ident_ready par_in lam_in lam_prod lam_sum lam_exp lam_ready pos_in ang rope_arg rope_ready
            x_sq x_pow x_scaled x_wnorm x_hi x_lo
            w_hi_ready w_lo_ready w_used
            tp_done tp_free sq_ready ss_ready norm_chain rs_ready
            t_hi v_hi_ready v_split s_done masked max_ready x_done sink_ready sink_exp
            comb_chain comb_done at_hi pv_done o_read o_pow o_ready b_sum probs_scaled
            y_hi out_ready row_summed pp_done""".split()
        sm = {n: sem("s_" + n) for n in names}

        def pair(name):
            return [sem(f"s_{name}{b}") for b in range(2)]

        x_in, w_in_sem, pp_copied = pair("x_in"), pair("w_in"), pair("pp_copied")
        pp_tanh, pp_gated, gstored = pair("pp_tanh"), pair("pp_gated"), pair("gstored")
        rst_ready, stored, loaded = pair("rst_ready"), pair("stored"), pair("loaded")
        gate_ld, ystored = pair("gate_ld"), pair("ystored")
        y_in, res_in, out_st, x_rows_in = pair("y_in"), pair("res_in"), pair("out_st"), pair("x_rows_in")
        y_lo = pair("y_lo")
        block = ctx.enter_context(nc.Block())

        def wait(eng, s, value):
            if isinstance(value, int) and value <= 0:
                return
            eng.wait_ge(s, value)

        def iterations(eng, body, phases=PHASES):
            body(-1, -1)
            for f, n in phases:
                if n == 1:
                    body(f, f)
                else:
                    with eng.Fori(f, f + n) as it:
                        body(it, f)

        def proj_tile(it, first, s):
            nxt = proj_kind(first + 1)
            if not nxt:
                return None, None, tile_desc(("O", 0), 3)
            p = s // 4
            d = tile_desc((nxt, it + 1), p)
            u = (it + 1) * 4 + (2 + p)
            if p:
                before = tile_desc((nxt, it + 1), p - 1)
            elif first == -1:
                before = KV_TILES[1]
            else:
                before = tile_desc((kind(first), it), 3)
            return d, u, before

        def y_split_at(first, s):
            if first >= len(KINDS) - 2:
                t = (first - (len(KINDS) - 2)) * 16 + s
                return {15: 0, 16: 1, 17: 2, 18: 3, 24: 4, 35: 5}.get(t)
            return None

        def split_width(first, s):
            return OK // 4 * P if proj_kind(first + 1 + s // 16) == "O" and s // 16 < 2 else 512

        def turned_before(it, first, s):
            d, u, before = proj_tile(it, first, s)
            if s % 4 > 1 or not before["turned"] or d is None and s > 1:
                return None
            name = ("PT", "before", s) if s < 2 else ("PT", s // 4 - 1, s % 2)
            return before, name, s % 2

        @block.sync
        def _(sp):
            def load_x(r):
                if r >= 2:
                    wait(sp, sm["tp_done"], 4 * (r - 1))
                sp.dma_start(x_buf[r % 2], x2[r * P:(r + 1) * P, :]).then_inc(x_in[r % 2], 16)

            def load_quarter(u, q, col):
                wait(sp, sm["w_lo_ready"], u * 4 + (q - 1))
                src = w_in[0, q * 512:(q + 1) * 512, bass.ds(col, P)].rearrange("(k r) c -> r k c", k=4)
                sp.dma_start(w_raw[:, q % 2, :].rearrange("p (k c) -> p k c", k=4), src)\
                  .then_inc(w_in_sem[q % 2], 16)

            def load_quarter_o(p, q):
                Q = NQ_IN + 4 * p + q
                wait(sp, sm["w_lo_ready"], Q - 1)
                n = OK // 4
                src = w_out[0, q * n * P:(q + 1) * n * P, p * P:(p + 1) * P].rearrange("(k r) c -> r k c", k=n)
                sp.dma_start(w_raw[:, Q % 2, 0:n * P].rearrange("p (k c) -> p k c", k=n), src)\
                  .then_inc(w_in_sem[Q % 2], 16)

            def load_w_out(j):
                if j >= len(OUT_TILES):
                    return
                g, k = OUT_TILES[j]
                n, Q = GROUPS[g][1], NQ_OUT + j
                wait(sp, sm["w_lo_ready"], Q - 1)
                sp.dma_start(w_raw[:, Q % 2, :], w_out[0, k * P:(k + 1) * P, n * 512:(n + 1) * 512])\
                  .then_inc(w_in_sem[Q % 2], 16)

            def load_y(j):
                lo, hi = Y_PARTS[j]
                done = NR // 2 * 16 * (AH + 2 * min(BC, (hi * P - AW) // 256))
                for b in range(2):
                    sp.wait_ge(ystored[b], done)
                sp.wait_ge(sm["w_used"], NQ_IN - 4 + (hi - 1) // 4 + 1)
                if j >= 2:
                    for b in range(2):
                        sp.wait_ge(y_lo[b], Y_PARTS[j - 2][1])
                sp.dma_start(hT_lo[:, lo:hi, :].bitcast(F32), scr_y[lo * P:hi * P, :].rearrange("(k p) t -> p k t", p=P))\
                  .then_inc(y_in[j % 2], 16)

            def load_x_rows(p, b):
                wait(sp, stored[b], 16 * tile_desc(("O", 0), p)["T"])
                src = x2[b * 512:(b + 1) * 512, p * P:(p + 1) * P].rearrange("(r t) c -> t r c", r=4)
                sp.dma_start(rows[:, b, :].rearrange("p (r c) -> p r c", r=4), src).then_inc(x_rows_in[b], 16)

            def column(k, c, p):
                if k == "A":
                    return c * P + AW * p
                return (c - AH) * 256 + ((QB0 if p < 2 else GB0) + P * (p % 2))

            def load_ahead(it, first, s):
                p, q, far = (s + 4) // 4, s % 4, 0
                if p == 4:
                    p, far = 0, 1
                k = proj_kind(first + 1 + far)
                if k == "O":
                    load_quarter_o(p, q)
                elif k:
                    c = it + (1 + far)
                    load_quarter(c * 4 + (2 + p), q, column(k, c, p))
                elif first == len(KINDS) - 1:
                    load_w_out(q)
                elif s < 4:
                    for j in range(4):
                        load_w_out(4 * s + 4 + j)

            def store_rows(d, b, n):
                if d["norm"]:
                    wait(sp, rst_ready[b], d["K"] + 1)
                else:
                    wait(sp, sm["tp_free"], n + 1)
                t, p = slice(b * 512, (b + 1) * 512), d["p"]
                c = slice(p * P, (p + 1) * P)
                if d["kind"] == "A":
                    dst = scr_a[bass.ds(d["unit"], 1), t, c].rearrange("a (r t) c -> t (a r) c", r=4)
                elif d["kind"] == "B":
                    dst = scr_q[bass.ds(d["unit"] - AH, 1), t, c].rearrange("a (r t) c -> t (a r) c", r=4)
                elif d["kind"] == "O":
                    dst = scr_part[t, c].rearrange("(r t) c -> t r c", r=4)
                else:
                    dst = scr_kv[t, c].rearrange("(r t) c -> t r c", r=4)
                sp.dma_start(dst, rows[:, b, :].rearrange("p (r c) -> p r c", r=4)).then_inc(stored[b], 16)

            def store_gate(d, b):
                wait(sp, pp_gated[b], d["GT"] + 1)
                sp.dma_start(scr_g[bass.ds(d["GT"], 1), :, b * 512:(b + 1) * 512].rearrange("a p t -> p (a t)"),
                               stage[:, b, :]).then_inc(gstored[b], 16)

            def load_step(nk, unit, i):
                G = unit * NR + i
                if not (isinstance(G, int) and G < 2):
                    wait(sp, sm["v_split"], G - 1)
                t = slice(i * P, (i + 1) * P)
                if nk == "A":
                    wait(sp, stored[i // 4], unit * 48 + 80)
                    sp.dma_start(qkv[:, i % 2, 0:3 * P], scr_a[bass.ds(unit, 1), t, :].rearrange("a t c -> t (a c)"))\
                        .then_inc(loaded[i % 2], 16)
                    return
                j = unit - AH
                wait(sp, stored[i // 4], j * 32 + 16 * 28)
                kv = (j // 2) * HD
                sp.dma_start(qkv[:, i % 2, 0:2 * P], scr_q[bass.ds(j, 1), t, :].rearrange("a t c -> t (a c)"))\
                    .then_inc(loaded[i % 2], 16)
                sp.dma_start(qkv[:, i % 2, 256:384].rearrange("p (a c) -> p a c", a=2),
                               scr_kv[t, bass.ds(kv, HD)].unsqueeze(1).to_broadcast([P, 2, HD]))\
                    .then_inc(loaded[i % 2], 16)
                sp.dma_start(qkv[:, i % 2, 384:448], scr_kv[t, bass.ds(kv + P, HD)]).then_inc(loaded[i % 2], 16)

            def load_gate(st):
                i, unit = st["i"], st["unit"]
                t = slice(i * P, (i + 1) * P)
                wait(sp, ystored[i % 2], stored_before(st))
                if st["k"] == "A":
                    wait(sp, gstored[i // 4], unit * 16 + 16)
                    sp.dma_start(gate_y[:, i % 2, 0:P], scr_g[bass.ds(unit, 1), :, t].rearrange("a p t -> p (a t)"))\
                      .then_inc(gate_ld[i % 2], 16)
                    return
                j = unit - AH
                wait(sp, gstored[i // 4], j * 32 + 160)
                for r in range(2):
                    dst = gate_y[0:HD, i % 2, r * 256:(r + 1) * 256].rearrange("d (a t) -> d a t", a=2)
                    src = scr_g[bass.ds(j * 2 + AH, 2), r * HD:(r + 1) * HD, t].rearrange("a d t -> d a t")
                    sp.dma_start(dst, src).then_inc(gate_ld[i % 2], 16)

            def store_y(st, it, first):
                i = st["i"]
                t = slice(i * P, (i + 1) * P)
                if st["k"] == "A":
                    wait(sp, sm["tp_free"], use_number(("YT", i), it, first) + 1)
                    sp.dma_start(scr_y[bass.ds(st["unit"] * P, P), t], gate_y[:, i % 2, 0:P])\
                      .then_inc(ystored[i % 2], 16)
                    return
                wait(sp, sm["o_read"], st["G"] * 2 + 2)
                for r in range(2):
                    dst = scr_y[bass.ds((st["unit"] - AH) * 256 + AW, 256), t]\
                        .rearrange("(a r d) t -> r d a t", a=2, r=2)[r]
                    sp.dma_start(dst, gate_y[0:HD, i % 2, r * 256:(r + 1) * 256].rearrange("d (a t) -> d a t", a=2))\
                      .then_inc(ystored[i % 2], 16)

            load_x(0)
            load_x(1)
            load_quarter(0, 0, KB0)
            load_quarter(0, 1, KB0)
            for r in range(2, NR):
                load_x(r)
            load_quarter(0, 2, KB0)
            load_quarter(0, 3, KB0)
            for s in range(8):
                if s < 4:
                    load_quarter(1, s, VB0)
                else:
                    load_quarter(2, s - 4, 0)
                if 4 <= s < 6:
                    store_rows(KV_TILES[0], s - 4, 32 + s - 4)
            sp.wait_ge(sm["lam_sum"], 1)

            def body(it, first):
                for s in range(16):
                    i = s // 2
                    d, u, before = proj_tile(it, first, s)
                    load_ahead(it, first, s)
                    if d and s % 4 == 3 and not d["turned"]:
                        store_gate(d, 0)
                        store_gate(d, 1)
                    cur = step_at(i, it, first)
                    back1 = step_at(i - 1, it, first)
                    back2 = step_at(i - 2, it, first)
                    if s % 2 == 0:
                        if cur and i + 1 < NR:
                            load_step(cur["k"], it, i + 1)
                        elif i + 1 == NR and kind(first + 1):
                            load_step(kind(first + 1), it + 1, 0)
                        if back2 and back2["k"] == "B":
                            store_y(back2, it, first)
                        if back1:
                            load_gate(back1)
                    elif back2 and back2["k"] == "A":
                        store_y(back2, it, first)
                    tb = turned_before(it, first, s)
                    if tb:
                        store_rows(tb[0], tb[2], use_number(tb[1], it, first))
                    if d and d["kind"] == "O" and s % 4 == 2:
                        for b in range(2):
                            load_x_rows(d["p"], b)
                    t = (first - (len(KINDS) - 2)) * 16 + s
                    if t in (13, 14, 15, 16, 20, 34):
                        load_y((13, 14, 15, 16, 20, 34).index(t))
                    if first == len(KINDS) and s == 1:
                        sp.wait_ge(sm["tp_done"], use_number(("AT", NR - 1, 1), it, first) + 1)
                        load_res(0)
                    if first == len(KINDS) and s == 3:
                        load_res(1)

            def part(a, g):
                h, n = GROUPS[g]
                return a[h * 512:(h + 1) * 512, n * 512:(n + 1) * 512].rearrange("(r p) c -> p r c", r=4)

            def load_res(g):
                if g >= 2:
                    sp.wait_ge(out_st[g % 2], 16 * (g // 2))
                else:
                    for b in range(2):
                        sp.wait_ge(stored[b], 16 * (26 + 2 * BC + 4))
                src = part(x2 if GROUPS[g][1] else scr_part, g)
                sp.dma_start(x_buf[g % 2].rearrange("p (r c) -> p r c", r=4), src).then_inc(res_in[g % 2], 16)

            def store_out(g):
                sp.wait_ge(sm["out_ready"], 4 * (g + 1))
                sp.dma_start(part(out2, g), x_buf[g % 2].rearrange("p (r c) -> p r c", r=4))\
                  .then_inc(out_st[g % 2], 16)

            iterations(sp, body, SP_PHASES)

            for j in range(16, len(OUT_TILES)):
                g, k = OUT_TILES[j]
                load_w_out(j + 4)
                if k == (4 if GROUPS[g][1] else OK + 2):
                    store_out(g - 1)
                if k == 8 and g + 1 < len(GROUPS):
                    load_res(g + 1)
                if g == len(GROUPS) - 1 and k == OK:
                    load_res(g)
            for r in range(4):
                g = len(GROUPS) - 1
                sp.wait_ge(sm["out_ready"], 4 * g + r + 1)
                sp.dma_start(part(out2, g)[:, r], x_buf[g % 2][:, r * 512:(r + 1) * 512]).then_inc(out_st[g % 2], 16)
            for b in range(2):
                sp.wait_ge(out_st[b], 16 * (len(GROUPS) // 2) + (48 if b else 0))
                sp.wait_ge(gstored[b], 16 * (AH + 2 * BC))
                sp.wait_ge(ystored[b], 8 * NR * (AH + 2 * BC))

        @block.scalar
        def _(act):
            def split_w(Q, b4, w=512):
                wait(act, w_in_sem[b4 % 2], (Q - b4) * 8 + 16 * (b4 // 2 + 1))
                wait(act, sm["w_used"], Q - 3)
                act.activation(w_hi[:, b4, 0:w], w_raw[:, b4 % 2, 0:w], ACT.Copy).then_inc(sm["w_hi_ready"], 1)

            pars = [(head_w[:, n, :], w.partition_broadcast(P)[:, 0, :])
                    for n, w in enumerate((q_norm_a, k_norm_a, q_norm_b, k_norm_b))]
            pars += [(norm_c[:, :], norm_w[0].rearrange("(k p) -> p k", p=P)),
                     (sub_c[:, 0:1], subln_w[0].rearrange("(p a) -> p a", a=1))]
            pars += [(sink_t[:, :], sinks.partition_broadcast(P)[:, 0, :])]
            act.dma_start(pos_i[:, :], positions[0].rearrange("(r p) -> p r", p=P),
                          allow_slow_non_contiguous=True).then_inc(sm["pos_in"], 16)
            act.dma_start(tmp[:, 0:HALF], inv_freq.partition_broadcast(P)[:, 0, :]).then_inc(sm["pos_in"], 16)
            for n, w in enumerate((lambda_q1, lambda_k1, lambda_q2, lambda_k2)):
                act.dma_start(qkv[:, 0, n * HD:(n + 1) * HD], w.partition_broadcast(P)[:, 0, :])\
                   .then_inc(sm["lam_in"], 16)
            for dst, src in pars:
                act.dma_start(dst, src, allow_slow_non_contiguous=True).then_inc(sm["par_in"], 16)

            act.wait_ge(sm["rope_arg"], 2)
            act.activation(cos_t[:, :, :], cos_t[:, :, :], ACT.Sin).then_inc(sm["rope_ready"], 1)
            act.activation(sin_t[:, :, :], sin_t[:, :, :], ACT.Sin).then_inc(sm["rope_ready"], 1)
            act.wait_ge(sm["lam_sum"], 1)
            act.activation(neg_lam[:, 2:4], neg_lam[:, 0:2], ACT.Exp).then_inc(sm["lam_exp"], 1)

            def square_x(r):
                act.wait_ge(x_in[r % 2], 16 * (r // 2 + 1))
                if r:
                    act.wait_ge(sm["x_sq"], r)
                act.activation(ps_a[:, :, :].rearrange("p a b -> p (a b)"), x_buf[r % 2], ACT.Square,
                               accum_out=ss_x[:, r:r + 1]).then_inc(sm["x_sq"], 1)

            def scale_x(r):
                act.wait_ge(sm["x_pow"], 3 * (r + 1))
                act.activation(x_buf[r % 2], x_buf[r % 2], ACT.Copy, scale=ss_x[:, r:r + 1])\
                   .then_inc(sm["x_scaled"], 1)

            square_x(0)
            for r in range(NR):
                scale_x(r)
                if r + 1 < NR:
                    square_x(r + 1)
                for g in range(4):
                    act.wait_ge(sm["tp_free"], 4 * r + g + 1)
                    act.activation(hT_hi[:, 4 * g:4 * g + 4, r * P:(r + 1) * P],
                                   x_sc[:, g % 2, :].rearrange("p (k t) -> p k t", k=4), ACT.Copy)\
                       .then_inc(sm["x_hi"], 1)

            def stage_free(before, b, it, first):
                if before is None:
                    return
                if before["norm"]:
                    wait(act, rst_ready[b], before["K"] + 1)
                elif before["turned"]:
                    n = (use_number(("PT", before["p"], b), it, first) if before is not KV_TILES[1]
                         else BASE[-1] + b)
                    wait(act, sm["tp_free"], n + 1)
                else:
                    wait(act, gstored[b], before["GT"] * 16 + 16)

            def evacuate(d, before, u, it, first):
                for b in range(2):
                    wait(act, sm["w_used" if b else "pp_done"], u * 4 + 4 if b else u + 1)
                    stage_free(before, b, it, first)
                    if d["turned"]:
                        act.activation(stage[:, b, :], p_proj[b], ACT.Copy).then_inc(pp_copied[b], 1)
                    else:
                        act.activation(stage[:, b, :], p_proj[b], ACT.Tanh, scale=0.5).then_inc(pp_tanh[b], 1)

            def square_heads(d, n, bank, b):
                wait(act, sm["tp_done"], n + 1)
                if not (isinstance(d["K"], int) and d["K"] == 0 and b == 0):
                    wait(act, sm["norm_chain"], d["K"] * 6 + 3 * b)
                act.activation(tmp[:, :], p_tr[bank], ACT.Square).then_inc(sm["sq_ready"], 1)

            def body(it, first):
                Q0 = (it + 1) * 16 + 8
                for s in range(16):
                    i = s // 2
                    d, u, before = proj_tile(it, first, s)
                    split_y(y_split_at(first, s))
                    if d:
                        split_w(Q0 + (s + 2), (s + 2) % 4, split_width(first, s + 2))
                        if s % 4 == 3:
                            evacuate(d, before, u, it, first)
                    elif s < 4:
                        for j in range(4 * s + 2, 4 * s + 6):
                            split_w(NQ_OUT + j, j % 4)
                    cur = step_at(i, it, first)
                    back1 = step_at(i - 1, it, first)
                    back2 = step_at(i - 2, it, first)
                    tb = turned_before(it, first, s)
                    if tb and tb[0]["norm"]:
                        square_heads(tb[0], use_number(tb[1], it, first), bank_of(tb[1], first), tb[2])
                    if s % 2 == 0:
                        if back2 and back2["k"] == "A":
                            wait(act, sm["o_pow"], back2["G"] * 3 + 3)
                            wait(act, sm["o_read"], back2["G"] * 2 + 2)
                            act.activation(o_sb[:, 0:P], o_sb[:, 0:P], ACT.Copy, scale=ss_o[:, 0:1])\
                               .then_inc(sm["o_ready"], 1)
                        if back1:
                            wait(act, sm["pv_done"], back1["G"])
                            for m, (lo, hi) in enumerate(at_spans(back1)):
                                name = ("AT", back1["i"], m)
                                wait(act, sm["tp_done"], use_number(name, it, first) + 1)
                                act.activation(aT_hi[:, lo:hi], p_tr[bank_of(name, first)][:, 0:hi - lo],
                                               ACT.Copy).then_inc(sm["at_hi"], 1)
                        if cur and cur["k"] == "A":
                            exp_a(cur, 0)
                        elif cur:
                            exp_b(cur, it - AH)
                    else:
                        if cur and cur["k"] == "A":
                            exp_a(cur, 1)
                        if back1 and back1["k"] == "A":
                            wait(act, sm["pv_done"], back1["G"] + 1)
                            r0 = inv_sum[:, back1["i"] % 2, 0:1]
                            act.activation(p_junk[:, 0:P], p_o[:, 0:P], ACT.Square, scale=r0,
                                           accum_out=ss_o[:, 2:3]).then_inc(sm["o_read"], 1)
                            act.activation(o_sb[:, 0:P], p_o[:, 0:P], ACT.Copy, scale=r0)\
                               .then_inc(sm["o_read"], 1)
                        nk = cur["k"] if cur and i + 1 < NR else kind(first + 1) if i + 1 == NR else None
                        if nk:
                            name = ("T", (i + 1) % NR)
                            n = use_number(name, it, first)
                            bank = p_tr[bank_of(name, first)]
                            w = P if nk == "A" else 2 * P
                            wait(act, sm["tp_done"], n + 1)
                            act.activation(qT_hi[:, 0:w], bank[:, 0:w], ACT.Copy, scale=QSCALE)\
                               .then_inc(sm["t_hi"], 1)
                            j = (i + 1) % NR
                            act.activation(kT_hi[:, j * P:(j + 1) * P], bank[:, w:w + P], ACT.Copy)\
                               .then_inc(sm["t_hi"], 1)
                        if cur:
                            hi_v(cur, it)

            def split_y(part):
                if part is None:
                    return
                act.wait_ge(y_in[part % 2], 16 * (part // 2 + 1))
                for k in range(*Y_PARTS[part]):
                    act.activation(hT_hi[:, k, :], hT_lo[:, k, :].bitcast(F32), ACT.Copy).then_inc(sm["y_hi"], 1)

            def hi_v(st, it):
                i, k = st["i"], st["k"]
                lo, w = (2 * P, P) if k == "A" else (3 * P, HD)
                if i == 0:
                    wait(act, sm["pv_done"], st["G"])
                wait(act, loaded[i % 2], loads_by(k, it, i))
                act.activation(v_hi[:, i, 0:w], qkv[:, i % 2, lo:lo + w], ACT.Copy).then_inc(sm["v_hi_ready"], 1)

            def exp_a(st, c):
                wait(act, sm["max_ready"], st["G"] * 2 + (c + 1))
                if c == 0:
                    wait(act, sm["comb_done"], st["G"])
                w = (st["i"] + 1) * P
                flat = p_s.rearrange("p a b -> p (a b)")
                act.activation(expd[:, c, 0:w], flat[:, 0:w], ACT.Exp, bias=neg_max[:, c:c + 1],
                               accum_out=sums[:, c:c + 1]).then_inc(sm["x_done"], 1)

            def exp_b(st, j):
                gb = st["G"] - AH * NR
                lo = P if st["i"] == 0 else 0
                wait(act, sm["sink_ready"], gb * 4 + 4)
                wait(act, sm["b_sum"], gb * 2)
                for r in range(2):
                    for p in range(2):
                        n = 2 * r + p
                        ins = act.activation(expd[:, st["i"] % 2, n * 256 + lo:n * 256 + 256],
                                             p_s[:, r, p * 256 + lo:p * 256 + 256], ACT.Exp,
                                             bias=neg_max[:, n:n + 1], accum_out=sums[:, n:n + 1])
                    ins.then_inc(sm["x_done"], 1)
                act.activation(sink_e[:, :], neg_max[:, 4:8], ACT.Exp).then_inc(sm["sink_exp"], 1)

            for Q in range(2):
                split_w(Q, Q)
            for s in range(8):
                split_w(s + 2, (s + 2) % 4)
                u = s // 4
                if s % 4 == 3:
                    evacuate(KV_TILES[u], KV_TILES[0] if u else None, u, -1, -1)
                if 4 <= s < 6:
                    square_heads(KV_TILES[0], 32 + s - 4, (32 + s - 4) % 2, s - 4)
            iterations(act, body)

            for j in range(18, len(OUT_TILES)):
                split_w(NQ_OUT + j, j % 4)

        @block.tensor
        def _(pe):
            def three(dst, a_hi, a_lo, b_hi, b_lo, start, stop):
                pe.matmul(dst, a_hi, b_hi, start=start, stop=False)
                pe.matmul(dst, a_hi, b_lo, start=False, stop=False)
                return pe.matmul(dst, a_lo, b_hi, start=False, stop=stop)

            def bank_free(n):
                wait(pe, sm["tp_free"], n - 1)

            pe.wait_ge(sm["ident_ready"], 2)
            for r in range(NR):
                pe.wait_ge(sm["x_scaled"], r + 1)
                for g in range(4):
                    n = 4 * r + g
                    bank_free(n)
                    for k in range(4):
                        f = (4 * g + k) * P
                        mm = pe.transpose(p_tr[n % 2][:, k * P:(k + 1) * P], x_buf[r % 2][:, f:f + P], ident[:, :])
                    mm.then_inc(sm["tp_done"], 1)

            def quarter(d, u, q, b, before):
                part_o = d["kind"] == "O"
                nk = OK // 4 if part_o else 4
                if part_o:
                    wait(pe, y_lo[b], nk * (q + 1))
                if b == 0:
                    wait(pe, sm["w_lo_ready"], u * 4 + (q + 1))
                if q == 0 and before is not None:
                    if before["turned"]:
                        wait(pe, pp_copied[b], before["T"] + 1)
                    else:
                        wait(pe, pp_gated[b], before["GT"] + 1)
                for k in range(nk):
                    w = slice(k * P, (k + 1) * P)
                    t = slice(b * 512, (b + 1) * 512)
                    kk = nk * q + k
                    mm = three(p_proj[b], w_hi[:, q, w], w_lo[:, q, w], hT_hi[:, kk, t], hT_lo[:, kk, t],
                               kk == 0, kk == 4 * nk - 1)
                if b:
                    mm.then_inc(sm["w_used"], 1)
                elif q == 3:
                    mm.then_inc(sm["pp_done"], 1)

            def turn_tile(d, b, n, bank):
                wait(pe, pp_copied[b], d["T"] + 1)
                bank_free(n)
                for r in range(4):
                    mm = pe.transpose(p_tr[bank][:, r * P:(r + 1) * P], stage[:, b, r * P:(r + 1) * P], ident[:, :])
                mm.then_inc(sm["tp_done"], 1)

            def scores_a(st, c, it, first):
                i = st["i"]
                w = (i + 1) * P
                if c == 0:
                    wait(pe, sm["tp_free"], qk_split(i, it, first))
                wait(pe, sm["x_done"], st["G"] * 2 + c)
                flat = p_s.rearrange("p a b -> p (a b)")
                h = slice(c * HD, (c + 1) * HD)
                for lo in range(0, w, 512):
                    t = slice(lo, min(w, lo + 512))
                    mm = three(flat[:, t], qT_hi[h, 0:P], qT_lo[h, 0:P], kT_hi[h, t], kT_lo[h, t], True, True)
                mm.then_inc(sm["s_done"], 1)

            def scores_b(st, it, first):
                i = st["i"]
                wait(pe, sm["tp_free"], qk_split(i, it, first))
                wait(pe, sm["x_done"], st["G"] * 2)
                t = slice(max(i - 1, 0) * P, (i + 1) * P)
                lo = P if i == 0 else 0
                for r in range(2):
                    h = slice(r * HD, (r + 1) * HD)
                    for p in range(2):
                        mm = three(p_s[:, r, p * 256 + lo:p * 256 + 256], qT_hi[h, p * P:(p + 1) * P],
                                   qT_lo[h, p * P:(p + 1) * P], kT_hi[h, t], kT_lo[h, t], True, True)
                    mm.then_inc(sm["s_done"], 1)

            def turn_probs(st, it, first):
                i = st["i"]
                if st["k"] == "A":
                    wait(pe, sm["comb_done"], st["G"] + 1)
                    blocks = [expd[:, 1, b * P:(b + 1) * P] for b in range(i + 1)]
                else:
                    wait(pe, sm["probs_scaled"], st["G"] - (AH * NR - 1))
                    blocks = [expd[:, i % 2, n * 256 + b * P:n * 256 + (b + 1) * P]
                              for n in range(4) for b in ((0, 1) if i else (1,))]
                for m, (lo, hi) in enumerate(at_spans(st)):
                    name = ("AT", i, m)
                    bank_free(use_number(name, it, first))
                    for b in range((hi - lo) // P):
                        mm = pe.transpose(p_tr[bank_of(name, first)][:, b * P:(b + 1) * P],
                                          blocks[lo // P + b], ident[:, :])
                    mm.then_inc(sm["tp_done"], 1)

            def values(st, it, first):
                i = st["i"]
                last = ("AT", i, len(at_spans(st)) - 1)
                wait(pe, sm["v_split"], st["G"] + 1)
                wait(pe, sm["tp_free"], use_number(last, it, first) + 1)
                wait(pe, sm["o_read"], st["G"] * 2)
                if st["k"] == "A":
                    for b in range(i + 1):
                        a = slice(b * P, (b + 1) * P)
                        mm = three(p_o[:, 0:P], aT_hi[:, a], aT_lo[:, a], v_hi[:, b, :], v_lo[:, b, :], b == 0, b == i)
                else:
                    nb = 2 if i else 1
                    a_hi, a_lo = (a[:, 0:4 * nb * P].rearrange("k (n b t) -> k b n t", n=4, b=nb)
                                  for a in (aT_hi, aT_lo))
                    dst = p_o[0:HD, :].rearrange("d (n t) -> d n t", n=4)
                    for b in range(nb):
                        vb = i - (nb - 1) + b
                        mm = three(dst, v_hi[:, vb, 0:HD], v_lo[:, vb, 0:HD], a_hi[:, b], a_lo[:, b],
                                   b == 0, b == nb - 1)
                mm.then_inc(sm["pv_done"], 1)

            def turn_o(st, it, first):
                name = ("YT", st["i"])
                wait(pe, sm["o_ready"], st["G"] + 1)
                bank_free(use_number(name, it, first))
                pe.transpose(p_tr[bank_of(name, first)][:, 0:P], o_sb[:, 0:P], ident[:, :])\
                  .then_inc(sm["tp_done"], 1)

            def turn_qk(nk, i, it, first):
                name = ("T", i)
                wait(pe, loaded[i % 2], loads_by(nk, it + 1 if i == 0 else it, i))
                n = use_number(name, it, first)
                bank_free(n)
                bank = p_tr[bank_of(name, first)]
                for a in range(2 if nk == "A" else 3):
                    mm = pe.transpose(bank[:, a * P:(a + 1) * P], qkv[:, i % 2, a * P:(a + 1) * P], ident[:, :])
                mm.then_inc(sm["tp_done"], 1)

            def out_bank_free(g):
                if g == 0:
                    for b in range(2):
                        pe.wait_ge(pp_copied[b], tile_desc(("O", 0), 3)["T"] + 1)
                    pe.wait_ge(sm["x_done"], 2 * NR * len(KINDS))
                elif g == 1:
                    pe.wait_ge(sm["tp_free"], BASE[12] + len(uses_of(12)))
                    pe.wait_ge(sm["o_read"], 2 * NR * len(KINDS))
                else:
                    pe.wait_ge(sm["out_ready"], 4 * (g - 1))

            def out_tile(j):
                g, k = OUT_TILES[j]
                half, n = GROUPS[g]
                first_k = 0 if n else OK
                if k == first_k:
                    out_bank_free(g)
                pe.wait_ge(sm["w_lo_ready"], NQ_OUT + j + 1)
                pe.wait_ge(y_lo[half], k + 1)
                for r in range(4):
                    t = slice(half * 512 + r * P, half * 512 + (r + 1) * P)
                    mm = three((ps_a, ps_b)[g % 2][:, r, :], hT_hi[:, k, t], hT_lo[:, k, t],
                               w_hi[:, j % 4, :], w_lo[:, j % 4, :], k == first_k, k == KT - 1)
                mm.then_inc(sm["w_used"], 1)

            def body(it, first):
                for s in range(16):
                    i = s // 2
                    d, u, before = proj_tile(it, first, s)
                    cur = step_at(i, it, first)
                    back1 = step_at(i - 1, it, first)
                    back2 = step_at(i - 2, it, first)
                    tb = turned_before(it, first, s)
                    if d:
                        quarter(d, u, s % 4, 0, before)
                    elif s < 4:
                        out_tile(4 * s)
                        out_tile(4 * s + 1)
                    if s % 2 == 0:
                        if tb:
                            turn_tile(tb[0], tb[2], use_number(tb[1], it, first), bank_of(tb[1], first))
                    elif back2 and back2["k"] == "A":
                        turn_o(back2, it, first)
                    if d:
                        quarter(d, u, s % 4, 1, before)
                    elif s < 4:
                        out_tile(4 * s + 2)
                        out_tile(4 * s + 3)
                    if s % 2 == 0:
                        if cur and cur["k"] == "A":
                            scores_a(cur, 0, it, first)
                        elif cur:
                            scores_b(cur, it, first)
                        if back1:
                            turn_probs(back1, it, first)
                        continue
                    if tb:
                        turn_tile(tb[0], tb[2], use_number(tb[1], it, first), bank_of(tb[1], first))
                    if cur and cur["k"] == "A":
                        scores_a(cur, 1, it, first)
                    if back1:
                        values(back1, it, first)
                    nk = cur["k"] if cur and i + 1 < NR else kind(first + 1) if i + 1 == NR else None
                    if nk:
                        turn_qk(nk, (i + 1) % NR, it, first)

            pe.wait_ge(sm["x_lo"], 32)
            for s in range(8):
                u = s // 4
                for b in range(2):
                    quarter(KV_TILES[u], u, s % 4, b, KV_TILES[0] if u else None)
                if 4 <= s < 6:
                    turn_tile(KV_TILES[0], s - 4, 32 + s - 4, s % 2)
            iterations(pe, body)

            last = [j for j, (g, k) in enumerate(OUT_TILES) if g == len(GROUPS) - 1]
            for j in range(16, last[0]):
                out_tile(j)
            out_bank_free(len(GROUPS) - 1)
            pe.wait_ge(sm["w_lo_ready"], NQ_OUT + len(OUT_TILES))
            for r in range(4):
                t = slice(512 + r * P, 512 + (r + 1) * P)
                for j in last:
                    k = OUT_TILES[j][1]
                    mm = three(ps_b[:, r, :], hT_hi[:, k, t], hT_lo[:, k, t], w_hi[:, j % 4, :], w_lo[:, j % 4, :],
                               j == last[0], j == last[-1])
                mm.then_inc(sm["row_summed"], 1)

        @block.vector
        def _(dve):
            links = [0]

            def link(ins):
                links[0] += 1
                ins.then_inc(sm["ang"], 1)
                dve.wait_ge(sm["ang"], links[0])

            def tt(o, a, b, op):
                return dve.tensor_tensor(o, a, b, op)

            ang = tmp[:, 256:512]
            ang3 = ang.rearrange("p (r f) -> p r f", r=NR)
            dve.wait_ge(sm["pos_in"], 32)
            link(dve.tensor_copy(pos_f[:, :], pos_i[:, :]))
            link(tt(ang3, pos_f[:, :].unsqueeze(2).to_broadcast([P, NR, HALF]),
                    tmp[:, 0:HALF].unsqueeze(1).to_broadcast([P, NR, HALF]), ALU.mult))
            left, parts = 2 * math.pi, []
            for _ in range(3):
                e = 2.0 ** (math.floor(math.log2(left)) - 7)
                parts.append(math.floor(left / e) * e)
                left -= parts[-1]
            parts.append(left)
            magic = 1.5 * 2.0 ** 23
            turns = o_sb[:, :]
            for table, quarter_turn in ((cos_t, 0.25), (sin_t, 0.0)):
                t2 = table[:, :, :].rearrange("p r f -> p (r f)")
                link(dve.tensor_scalar(turns, ang, 0.5 / math.pi, quarter_turn, ALU.mult, ALU.add))
                link(dve.tensor_scalar(turns, turns, magic, magic, ALU.add, ALU.subtract))
                src = ang
                for c in parts:
                    link(dve.scalar_tensor_tensor(t2, turns, -c, src, ALU.mult, ALU.add))
                    src = t2
                link(dve.tensor_scalar(t2, t2, quarter_turn * 2 * math.pi, 3.1415925, ALU.add, ALU.min))
                dve.tensor_scalar(t2, t2, -3.1415925, None, ALU.max).then_inc(sm["rope_arg"], 1)

            dve.wait_ge(sm["lam_in"], 64)
            lv = qkv[:, 0, 0:256].rearrange("p (a b c) -> p a b c", a=2, b=2)
            prod = qkv[:, 1, 0:128].rearrange("p (a c) -> p a c", a=2)
            link(tt(prod, lv[:, :, 0, :], lv[:, :, 1, :], ALU.mult))
            dve.tensor_reduce(neg_lam[:, 0:2], prod, AX, ALU.add).then_inc(sm["lam_sum"], 1)
            dve.wait_ge(sm["lam_exp"], 1)
            link(tt(neg_lam[:, 4:5], neg_lam[:, 3:4], neg_lam[:, 2:3], ALU.subtract))
            link(dve.tensor_scalar(neg_lam[:, 5:6], neg_lam[:, 4:5], LAM_INIT, None, ALU.subtract))
            dve.wait_ge(sm["par_in"], 16 * 7)
            link(dve.tensor_scalar(sub_c[:, 1:2], sub_c[:, 0:1], 0.5 * (1 - LAM_INIT), None, ALU.mult))

            def x_lo_part(n):
                r, g = n // 4, n % 4
                dst = (slice(None), slice(4 * g, 4 * g + 4), slice(r * P, (r + 1) * P))
                dve.wait_ge(sm["x_hi"], n + 1)
                tt(hT_lo[dst], x_sc[:, n % 2, :].rearrange("p (k t) -> p k t", k=4),
                   hT_hi[dst].bitcast(F32), ALU.subtract).then_inc(sm["x_lo"], 1)

            for n in range(4 * NR):
                g = n % 4
                dve.wait_ge(sm["tp_done"], n + 1)
                if n >= 2:
                    dve.wait_ge(sm["x_lo"], n - 1)
                tt(x_sc[:, n % 2, :].rearrange("p (k t) -> p k t", k=4),
                   p_tr[n % 2].rearrange("p (k t) -> p k t", k=4),
                   norm_c[:, 4 * g:4 * g + 4].unsqueeze(2).to_broadcast([P, 4, P]), ALU.mult)\
                    .then_inc(sm["tp_free"], 1)
                if n:
                    x_lo_part(n - 1)
            x_lo_part(4 * NR - 1)

            def split_w(Q, b4, w=512):
                wait(dve, sm["w_hi_ready"], Q + 1)
                tt(w_lo[:, b4, 0:w], w_raw[:, b4 % 2, 0:w], w_hi[:, b4, 0:w].bitcast(F32), ALU.subtract)\
                    .then_inc(sm["w_lo_ready"], 1)

            def split_y(part):
                if part is None:
                    return
                for k in range(*Y_PARTS[part]):
                    dve.wait_ge(sm["y_hi"], k + 1)
                    dst = hT_lo[:, k, 0:512]
                    tt(dst, dst.bitcast(F32), hT_hi[:, k, 0:512].bitcast(F32), ALU.subtract).then_inc(y_lo[0], 1)

            def gate(d, b):
                wait(dve, pp_tanh[b], d["GT"] + 1)
                dve.scalar_tensor_tensor(stage[:, b, :], stage[:, b, :], 1.0, p_proj[b], ALU.add, ALU.mult)\
                   .then_inc(pp_gated[b], 1)

            def rows_out(d, b, n, bank):
                dst = rows[:, b, :]
                wait(dve, stored[b], d["T"] * 16)
                if d["kind"] == "O":
                    wait(dve, x_rows_in[b], 16 * (d["p"] + 1))
                    wait(dve, sm["tp_done"], n + 1)
                    tt(dst, p_tr[bank], dst, ALU.add).then_inc(sm["tp_free"], 1)
                    return
                if not d["norm"]:
                    wait(dve, sm["tp_done"], n + 1)
                    dve.tensor_copy(dst, p_tr[bank]).then_inc(sm["tp_free"], 1)
                    return
                seq = d["K"] * 2 + b
                wait(dve, sm["sq_ready"], seq + 1)
                dve.tensor_reduce(ss_h[:, 0:8], tmp[:, :].rearrange("p (g c) -> p g c", g=8), AX, ALU.add)\
                   .then_inc(sm["ss_ready"], 1)
                x3 = dst.rearrange("p (g c) -> p g c", g=8)
                tt(x3, p_tr[bank].rearrange("p (g c) -> p g c", g=8),
                   head_w[:, d["w"], :].unsqueeze(1).to_broadcast([P, 8, HD]), ALU.mult)\
                    .then_inc(sm["tp_free"], 1)

            def rotate(d, b, n):
                if not d["norm"]:
                    return
                seq = d["K"] * 2 + b
                dst = rows[:, b, :]
                x3 = dst.rearrange("p (g c) -> p g c", g=8)
                x5 = dst.rearrange("p (r h f c) -> p r h f c", r=4, h=2, f=2)
                t5 = tmp[:, :].rearrange("p (r h f c) -> p r h f c", r=4, h=2, f=2)
                r4 = slice(4 * b, 4 * b + 4)
                sn = sin_t[:, r4, :].unsqueeze(2).to_broadcast([P, 4, 2, HALF])
                cs = cos_t[:, r4, :].unsqueeze(2).to_broadcast([P, 4, 4, HALF])
                wait(dve, sm["tp_free"], n + 1)
                wait(dve, sm["ss_ready"], seq + 1)
                tt(t5[:, :, :, 0, :], x5[:, :, :, 1, :], sn, ALU.mult)
                tt(t5[:, :, :, 1, :], x5[:, :, :, 0, :], sn, ALU.mult).then_inc(sm["norm_chain"], 1)
                x4 = dst.rearrange("p (r g c) -> p r g c", r=4, g=4)
                wait(dve, sm["norm_chain"], seq * 3 + 1)
                tt(x4, x4, cs, ALU.mult).then_inc(sm["norm_chain"], 1)
                wait(dve, sm["norm_chain"], seq * 3 + 2)
                tt(x5[:, :, :, 0, :], x5[:, :, :, 0, :], t5[:, :, :, 0, :], ALU.subtract)
                tt(x5[:, :, :, 1, :], x5[:, :, :, 1, :], t5[:, :, :, 1, :], ALU.add)\
                    .then_inc(sm["norm_chain"], 1)
                wait(dve, sm["norm_chain"], seq * 3 + 3)
                wait(dve, sm["rs_ready"], seq * 3 + 3)
                tt(x3, x3, ss_h[:, 16:24].unsqueeze(2).to_broadcast([P, 8, HD]), ALU.mult)\
                    .then_inc(rst_ready[b], 1)

            def max_a(st, c):
                i = st["i"]
                flat = p_s.rearrange("p a b -> p (a b)")
                last = flat[:, i * P:(i + 1) * P]
                n = st["G"] * 2 + (c + 1)
                wait(dve, sm["s_done"], n)
                tt(last, last, mask[:, P:2 * P], ALU.add).then_inc(sm["masked"], 1)
                wait(dve, sm["masked"], n)
                dve.tensor_reduce(neg_max[:, c:c + 1], flat[:, 0:(i + 1) * P], AX, ALU.max, negate=True)\
                   .then_inc(sm["max_ready"], 1)

            def max_b(st, j):
                lo = P if st["i"] == 0 else 0
                gb = st["G"] - AH * NR
                for r in range(2):
                    wait(dve, sm["s_done"], st["G"] * 2 + (r + 1))
                    part = p_s[:, r, :].rearrange("p (a b) -> p a b", a=2)[:, :, lo:256]
                    tt(part, part, mask[:, lo:256].unsqueeze(1).to_broadcast([P, 2, 256 - lo]), ALU.add)\
                        .then_inc(sm["masked"], 1)
                wait(dve, sm["masked"], st["G"] * 2 + 2)
                sk = sink_t[:, bass.ds(j * 4, 4)].rearrange("t (p r) -> t r p", r=2)
                low, high = (neg_max[:, n:n + 4].rearrange("t (r p) -> t r p", r=2) for n in (0, 4))
                flat = p_s.rearrange("p a b -> p (a b)").rearrange("p (n s) -> p n s", n=4)
                dve.tensor_reduce(neg_max[:, 0:4], flat[:, :, lo:256], AX, ALU.max).then_inc(sm["sink_ready"], 1)
                wait(dve, sm["sink_ready"], gb * 4 + 1)
                tt(high, low, sk, ALU.max).then_inc(sm["sink_ready"], 1)
                wait(dve, sm["sink_ready"], gb * 4 + 2)
                dve.tensor_scalar(neg_max[:, 0:4], neg_max[:, 4:8], -1.0, None, ALU.mult)\
                   .then_inc(sm["sink_ready"], 1)
                wait(dve, sm["sink_ready"], gb * 4 + 3)
                tt(high, low, sk, ALU.add).then_inc(sm["sink_ready"], 1)

            def lo_probs(st, it, first):
                for m, (lo, hi) in enumerate(at_spans(st)):
                    name = ("AT", st["i"], m)
                    if st["k"] == "A":
                        seq = st["unit"] * 12 + sum(N_AT_A[:st["i"]]) + m
                    else:
                        seq = (st["unit"] - AH) * 16 + (12 * AH + 2 * st["i"] + m)
                    wait(dve, sm["at_hi"], seq + 1)
                    tt(aT_lo[:, lo:hi], p_tr[bank_of(name, first)][:, 0:hi - lo], aT_hi[:, lo:hi].bitcast(F32),
                       ALU.subtract).then_inc(sm["tp_free"], 1)

            def lo_qk(nk, i, it, first):
                name = ("T", i)
                bank = p_tr[bank_of(name, first)]
                w = P if nk == "A" else 2 * P
                unit = it + 1 if i == 0 else it
                wait(dve, sm["t_hi"], (unit * NR + i) * 2 + 2)
                dve.scalar_tensor_tensor(qT_lo[:, 0:w], bank[:, 0:w], QSCALE, qT_hi[:, 0:w].bitcast(F32),
                                         ALU.mult, ALU.subtract)
                tt(kT_lo[:, i * P:(i + 1) * P], bank[:, w:w + P], kT_hi[:, i * P:(i + 1) * P].bitcast(F32),
                   ALU.subtract).then_inc(sm["tp_free"], 1)

            def combine(st):
                inv = inv_sum[:, st["i"] % 2, :]
                wait(dve, sm["x_done"], st["G"] * 2 + 2)
                dve.reciprocal(inv[:, 0:2], sums[:, 0:2]).then_inc(sm["comb_chain"], 1)
                wait(dve, sm["comb_chain"], st["G"] * 2 + 1)
                dve.tensor_scalar(coef[:, :], sums[:, 0:1], neg_lam[:, 5:6], inv[:, 1:2], ALU.mult, ALU.mult)\
                   .then_inc(sm["comb_chain"], 1)
                wait(dve, sm["comb_chain"], st["G"] * 2 + 2)
                w = (st["i"] + 1) * P
                dve.scalar_tensor_tensor(expd[:, 1, 0:w], expd[:, 1, 0:w], coef[:, :], expd[:, 0, 0:w],
                                         ALU.mult, ALU.add).then_inc(sm["comb_done"], 1)

            def sum_b(st):
                gb = st["G"] - AH * NR
                wait(dve, sm["sink_exp"], gb + 1)
                tt(sums[:, :], sums[:, :], sink_e[:, :], ALU.add).then_inc(sm["b_sum"], 1)
                wait(dve, sm["b_sum"], gb * 2 + 1)
                dve.reciprocal(inv_sum[:, st["i"] % 2, :], sums[:, :]).then_inc(sm["b_sum"], 1)

            def y_out(st, it, first):
                i = st["i"]
                wait(dve, gate_ld[i % 2], stored_before(st) + (16 if st["k"] == "A" else 32))
                if st["k"] == "A":
                    name, w = ("YT", i), P
                    wait(dve, sm["tp_done"], use_number(name, it, first) + 1)
                    dve.scalar_tensor_tensor(gate_y[:, i % 2, 0:w], p_tr[bank_of(name, first)][:, 0:w], sub_c[:, 1:2],
                                             gate_y[:, i % 2, 0:w], ALU.mult, ALU.mult).then_inc(sm["tp_free"], 1)
                else:
                    wait(dve, sm["pv_done"], st["G"] + 1)
                    dve.scalar_tensor_tensor(gate_y[0:HD, i % 2, :], p_o[0:HD, :], 0.5, gate_y[0:HD, i % 2, :],
                                             ALU.mult, ALU.mult).then_inc(sm["o_read"], 2)

            dve.wait_ge(sm["consts"], 8)
            dve.wait_ge(sm["rope_ready"], 2)
            for Q in range(2):
                split_w(Q, Q)
            for s in range(8):
                split_w(s + 2, (s + 2) % 4)
                if 4 <= s < 6:
                    rows_out(KV_TILES[0], s - 4, 32 + s - 4, s % 2)
                    rotate(KV_TILES[0], s - 4, 32 + s - 4)

            def body(it, first):
                Q0 = (it + 1) * 16 + 8
                for s in range(16):
                    i = s // 2
                    d, u, before = proj_tile(it, first, s)
                    split_y(y_split_at(first, s))
                    if d:
                        split_w(Q0 + (s + 2), (s + 2) % 4, split_width(first, s + 2))
                    elif s < 4:
                        for j in range(4 * s + 2, 4 * s + 6):
                            split_w(NQ_OUT + j, j % 4)
                    cur = step_at(i, it, first)
                    back1 = step_at(i - 1, it, first)
                    back2 = step_at(i - 2, it, first)
                    if back2 and back2["k"] == ("A" if s % 2 else "B"):
                        y_out(back2, it, first)
                    if d and s % 4 == 3 and not d["turned"]:
                        gate(d, 0)
                        gate(d, 1)
                    if s % 2 and cur and cur["k"] == "B":
                        sum_b(cur)
                    tb = turned_before(it, first, s)
                    if tb:
                        n = use_number(tb[1], it, first)
                        rows_out(tb[0], tb[2], n, bank_of(tb[1], first))
                    if s % 2 == 0:
                        if cur and cur["k"] == "A":
                            max_a(cur, 0)
                        elif cur:
                            max_b(cur, it - AH)
                        if back1:
                            lo_probs(back1, it, first)
                    else:
                        if cur and cur["k"] == "A":
                            max_a(cur, 1)
                        nk = cur["k"] if cur and i + 1 < NR else kind(first + 1) if i + 1 == NR else None
                        if nk:
                            lo_qk(nk, (i + 1) % NR, it, first)
                        if cur and cur["k"] == "A":
                            combine(cur)
                    if tb:
                        rotate(tb[0], tb[2], n)

            iterations(dve, body)

            def add_group(g):
                dve.wait_ge(res_in[g % 2], 16 * (g // 2 + 1))
                res = x_buf[g % 2].rearrange("p (r c) -> p r c", r=4)
                for r in range(4):
                    if g == len(GROUPS) - 1:
                        dve.wait_ge(sm["row_summed"], r + 1)
                    tt(res[:, r, :], (ps_a, ps_b)[g % 2][:, r, :], res[:, r, :], ALU.add)\
                        .then_inc(sm["out_ready"], 1)

            for j in range(16, len(OUT_TILES)):
                if j + 2 < len(OUT_TILES):
                    split_w(NQ_OUT + j + 2, (j + 2) % 4)
                g = OUT_TILES[j - 1][0]
                if OUT_TILES[j][0] != g:
                    dve.wait_ge(sm["w_used"], NQ_OUT + j)
                    add_group(g)
            add_group(len(GROUPS) - 1)

        @block.gpsimd
        def _(pool):
            pool.memset(ident[:, :], 0.0).then_inc(sm["ident_ready"], 1)
            pool.memset(mask[:, :], 0.0).then_inc(sm["consts"], 1)
            for c, value in enumerate((-0.5, EPS, 1 / HD, 1 / D, 1 / P)):
                pool.memset(small[:, c, :], value).then_inc(sm["consts"], 1)
            pool.wait_ge(sm["ident_ready"], 1)
            pool.affine_select(out=ident[:, :], in_=ident[:, :], compare_op=ALU.not_equal, fill=1.0, base=0,
                               pattern=[[-1, P]], channel_multiplier=1).then_inc(sm["ident_ready"], 1)
            pool.wait_ge(sm["consts"], 6)
            pool.affine_select(out=mask[:, 0:P], in_=mask[:, 0:P], compare_op=ALU.is_gt, fill=NEG, base=0,
                               pattern=[[1, P]], channel_multiplier=-1).then_inc(sm["consts"], 1)
            pool.affine_select(out=mask[:, P:2 * P], in_=mask[:, P:2 * P], compare_op=ALU.is_ge, fill=NEG, base=0,
                               pattern=[[-1, P]], channel_multiplier=1).then_inc(sm["consts"], 1)

            def inv_rms(src, mean, dst, c, s, before):
                w = src.shape[1]
                pool.tensor_tensor(mean, src, small[:, c, 0:w], ALU.mult).then_inc(s, 1)
                wait(pool, s, before + 1)
                pool.tensor_tensor(mean, mean, small[:, 1, 0:w], ALU.add).then_inc(s, 1)
                wait(pool, s, before + 2)
                pool.tensor_tensor(dst, mean, small[:, 0, 0:w], ALU.pow).then_inc(s, 1)

            for r in range(NR):
                pool.wait_ge(sm["x_sq"], r + 1)
                inv_rms(ss_x[:, r:r + 1], ss_x[:, NR + r:NR + r + 1], ss_x[:, r:r + 1], 3, sm["x_pow"], 3 * r)

            def norms(d, b):
                seq = d["K"] * 2 + b
                wait(pool, sm["ss_ready"], seq + 1)
                inv_rms(ss_h[:, 0:8], ss_h[:, 8:16], ss_h[:, 16:24], 2, sm["rs_ready"], seq * 3)

            def lo_v(st):
                i, k = st["i"], st["k"]
                lo, w = (2 * P, P) if k == "A" else (3 * P, HD)
                wait(pool, sm["v_hi_ready"], st["G"] + 1)
                pool.tensor_tensor(v_lo[:, i, 0:w], qkv[:, i % 2, lo:lo + w], v_hi[:, i, 0:w].bitcast(F32),
                                   ALU.subtract).then_inc(sm["v_split"], 1)

            def split_y(part):
                if part is None:
                    return
                for k in range(*Y_PARTS[part]):
                    pool.wait_ge(sm["y_hi"], k + 1)
                    dst = hT_lo[:, k, 512:1024]
                    pool.tensor_tensor(dst, dst.bitcast(F32), hT_hi[:, k, 512:1024].bitcast(F32), ALU.subtract)\
                        .then_inc(y_lo[1], 1)

            def scale_probs(st):
                i, lo = st["i"], P if st["i"] == 0 else 0
                wait(pool, sm["b_sum"], (st["G"] - AH * NR) * 2 + 2)
                part = expd[:, i % 2, :].rearrange("p (n s) -> p n s", n=4)[:, :, lo:256]
                pool.tensor_tensor(part, part, inv_sum[:, i % 2, :].unsqueeze(2).to_broadcast([P, 4, 256 - lo]),
                                   ALU.mult).then_inc(sm["probs_scaled"], 1)

            for s in range(4, 6):
                norms(KV_TILES[0], s - 4)

            def body(it, first):
                for s in range(16):
                    i = s // 2
                    cur = step_at(i, it, first)
                    back1 = step_at(i - 1, it, first)
                    split_y(y_split_at(first, s))
                    if s % 2 and cur and cur["k"] == "B":
                        scale_probs(cur)
                    tb = turned_before(it, first, s)
                    if tb and tb[0]["norm"]:
                        norms(tb[0], tb[2])
                    if s % 2:
                        if back1 and back1["k"] == "A":
                            wait(pool, sm["o_read"], back1["G"] * 2 + 1)
                            inv_rms(ss_o[:, 2:3], ss_o[:, 1:2], ss_o[:, 0:1], 4, sm["o_pow"], back1["G"] * 3)
                        if cur:
                            lo_v(cur)

            iterations(pool, body)


_INS = ["x", "positions", "norm_w", "w_in", "q_norm_a", "k_norm_a", "lambda_q1", "lambda_k1", "lambda_q2",
        "lambda_k2", "subln_w", "q_norm_b", "k_norm_b", "sinks", "w_out"]


def kernel(**inputs):
    import concourse.bacc as bacc
    from concourse.bass_utils import run_bass_kernel_spmd

    nc = bacc.Bacc("TRN2", target_bir_lowering=False, num_devices=1)
    arrays, args = {}, []
    for name in _INS:
        a = np.ascontiguousarray(inputs[name])
        arrays[f"in_{name}"] = a
        args.append(nc.dram_tensor(f"in_{name}", a.shape, mybir.dt.from_np(a.dtype), kind="ExternalInput").ap())
    freq = (np.float32(10000.0) ** (-(np.arange(0, HD, 2, dtype=np.float32) / np.float32(HD)))).astype(np.float32)
    arrays["in_inv_freq"] = freq.reshape(1, HALF)
    args.append(nc.dram_tensor("in_inv_freq", (1, HALF), F32, kind="ExternalInput").ap())
    out = nc.dram_tensor("out_0", (1, S, D), F32, kind="ExternalOutput").ap()
    decoder_layer(nc, *args, out)
    r = run_bass_kernel_spmd(nc, [arrays], core_ids=[0])
    return r.results[0]["out_0"]
```

```python
import math
from contextlib import ExitStack

import concourse.bass as bass
import numpy as np
from concourse import mybir

F32 = mybir.dt.float32
F32R = mybir.dt.float32r
I32 = mybir.dt.int32
ALU = mybir.AluOpType
ACT = mybir.ActivationFunctionType
AX = mybir.AxisListType.X

P = 128
D = 2048
S = 1024
HD = 64
HALF = HD // 2
NR = S // P
KT = D // P
AH = 8
BC = 4
AW = 1024
QB0 = 4 * AW
KB0 = QB0 + 1024
VB0 = KB0 + 128
GB0 = VB0 + 128
EPS = 1e-6
NEG = -1e30
LAM_INIT = 0.8 - 0.6 * math.exp(-0.3 * 0)
QSCALE = HD ** -0.5
NQ_IN = 4 * (2 + 4 * (AH + BC))
N_AT_A = [1, 1, 1, 1, 2, 2, 2, 2]

KINDS = "A" * AH + "B" * BC
PHASES = [(0, 1), (1, 6), (7, 1), (8, 1), (9, 1), (10, 1), (11, 1), (12, 1)]
SP_PHASES = [(0, 1), (1, 5), (6, 1), (7, 1), (8, 1), (9, 1), (10, 1), (11, 1), (12, 1)]


OK = 12
GROUPS = [(h, n) for h in range(2) for n in (1, 2, 3)] + [(0, 0), (1, 0)]
OUT_TILES = [(g, k) for g, (h, n) in enumerate(GROUPS) for k in range(0 if n else OK, KT)]
NQ_OUT = NQ_IN + 16
Y_PARTS = [(0, 3), (3, 6), (6, 9), (9, 12), (12, 14), (14, 16)]


def kind(it):
    return KINDS[it] if 0 <= it < len(KINDS) else None


def proj_kind(it):
    return "O" if it == len(KINDS) else kind(it)


def tile_desc(c, p):
    k, c = c
    if k == "O":
        return dict(kind=k, p=p, T=26 + 2 * BC + p, GT=0, norm=False, turned=True)
    if k == "A":
        return dict(unit=c, p=p, kind=k, T=c * 3 + (2 + min(p, 3)), K=c * 2 + (1 + p), GT=c, w=p,
                    norm=p < 2, turned=p < 3)
    return dict(unit=c, p=p, kind=k, T=c * 2 + (26 - 2 * AH + min(p, 2)), K=c * 2 + (17 - 2 * AH + p),
                GT=c * 2 + (8 - 2 * AH + max(p - 2, 0)), w=2, norm=p < 2, turned=p < 2)


KV_TILES = [dict(kind="kv", p=0, T=0, K=0, GT=0, w=3, norm=True, turned=True),
            dict(kind="kv", p=1, T=1, K=1, GT=0, w=3, norm=False, turned=True)]


def step_at(i, it, first_it):
    back = i < 0
    k = kind(first_it - 1 if back else first_it)
    i = i % NR
    unit = it - 1 if back else it
    return dict(i=i, k=k, G=unit * NR + i, unit=unit) if k else None


def uses_of(first_it):
    out = []
    cur, prev, nxt = kind(first_it), kind(first_it - 1), kind(first_it + 1)
    proj = proj_kind(first_it + 1)
    for s in range(16):
        i = s // 2
        turned = []
        if s % 4 < 2 and s >= 4:
            p = s // 4 - 1
            if proj and tile_desc((proj, 0), p)["turned"]:
                turned.append(("PT", p, s % 2))
        elif s < 2 and first_it in (-1, len(KINDS)):
            turned.append(("PT", "before", s))
        if s % 2 == 0:
            out += turned
            k, j = (cur, i - 1) if i >= 1 else (prev, NR - 1)
            if k:
                out += [("AT", j, m) for m in range(2 if k == "B" else N_AT_A[j])]
        else:
            k, j = (cur, i - 2) if i >= 2 else (prev, NR - 2 + i)
            if k == "A":
                out.append(("YT", j))
            out += turned
            if i + 1 < NR and cur or i + 1 == NR and nxt:
                out.append(("T", (i + 1) % NR))
    return out


KV_USES = [("PT", "k", 0), ("PT", "k", 1)]
BASE = {}


def _count_bases():
    n = 32 + len(KV_USES)
    for it in range(-1, 13):
        BASE[it] = n
        n += len(uses_of(it))
    return n


_count_bases()


def use_number(name, it, first_it):
    return BASE[first_it] + uses_of(first_it).index(name) + (it - first_it) * len(uses_of(first_it))


def bank_of(name, first_it):
    return (BASE[first_it] + uses_of(first_it).index(name)) % 2


def qk_split(i, it, first):
    if i:
        return use_number(("T", i), it, first) + 1
    return BASE[first] + (it - first) * len(uses_of(first))


def at_spans(st):
    if st["k"] == "A":
        w = (st["i"] + 1) * P
        return [(0, min(w, 512))] + ([(512, w)] if w > 512 else [])
    return [(0, 512), (512, 1024)] if st["i"] else [(0, 256), (256, 512)]


def loads_by(k, unit, i):
    if k == "A":
        return unit * 64 + 16 * (i // 2 + 1)
    return (unit - AH) * 192 + (AH * 64 + 48 * (i // 2 + 1))


def stored_before(st):
    if st["k"] == "A":
        return st["unit"] * 64 + 16 * (st["i"] // 2)
    return (st["unit"] - AH) * 128 + (AH * 64 + 32 * (st["i"] // 2))


def decoder_layer(nc, x, positions, norm_w, w_in, q_norm_a, k_norm_a, lambda_q1, lambda_k1,
                  lambda_q2, lambda_k2, subln_w, q_norm_b, k_norm_b, sinks, w_out, inv_freq, out):
    for f, n in PHASES:
        assert n == 1 or len({len(uses_of(f + d)) for d in range(n)}) == 1
        assert n == 1 or len(uses_of(f)) % 2 == 0

    x2, out2 = x[0], out[0]
    scr_a = nc.dram_tensor("qkv_a_dram", (AH, S, 3 * P), F32).ap()
    scr_q = nc.dram_tensor("q_b_dram", (BC, S, 2 * P), F32).ap()
    scr_kv = nc.dram_tensor("kv_b_dram", (S, 2 * P), F32).ap()
    scr_g = nc.dram_tensor("gates_dram", (AH + 2 * BC, P, S), F32).ap()
    scr_part = nc.dram_tensor("out_part_dram", (S, 512), F32).ap()
    scr_y = nc.dram_tensor("y_dram", (D, S), F32).ap()

    with ExitStack() as ctx:
        def sb(name, shape, dt=F32):
            return ctx.enter_context(nc.sbuf_tensor(name, shape, dt))

        def sem(name):
            return ctx.enter_context(nc.semaphore(name))

        hT_hi = sb("hT_hi", [P, KT, S], F32R)
        hT_lo = sb("hT_lo", [P, KT, S], F32R)
        w_raw = sb("w_raw_sb", [P, 2, 512])
        w_hi = sb("w_hi_sb", [P, 4, 512], F32R)
        w_lo = sb("w_lo_sb", [P, 4, 512], F32R)
        with nc.sbuf_tensor("x_raw_sb", [P, 3 * D + 2 * 512], F32) as x_raw_sb:
            x_raw = [x_raw_sb[:, j * D:(j + 1) * D] for j in range(3)]
            x_pieces = [x_raw_sb[:, 3 * D + j * 512:3 * D + (j + 1) * 512] for j in range(2)]
        parts = sb("attention_parts", [P, 7, S], F32R)
        k_dup = [parts[:, 0, :], parts[:, 1, :]]
        v_hi, v_lo = (parts[:, c, :].rearrange("p (n e) -> p n e", n=NR) for c in (2, 3))
        aT_hi, aT_lo = parts[:, 4, :], parts[:, 5, :]
        kT_lo = parts[:, 6, :]
        o_second_b = parts[0:HD, 1, 0:512]
        q_pair = sb("q_hi_lo", [P, 4 * P], F32R)
        expd = sb("expd", [P, 2, S])
        stage_rows = sb("stage_rows", [P, 4 * 512])
        qkv = sb("qkv_sb", [P, 2, 448])
        gate_y = sb("gate_y", [P, 2, 512])
        o_sb = sb("o_sb", [P, 256])
        mask = sb("mask", [P, 2 * P])
        ident = sb("ident", [P, P])
        cos_t = sb("cos_t", [P, NR, HALF])
        sin_t = sb("sin_t", [P, NR, HALF])
        head_w = sb("head_w", [P, 4, HD])
        norm_c = sb("norm_c", [P, KT])
        sub_c = sb("sub_c", [P, 2])
        sink_t = sb("sink_t", [P, 4 * BC])
        pos_i = sb("pos_i", [P, NR], I32)
        pos_f = sb("pos_f", [P, NR])
        ss_x = sb("ss_x", [P, 2 * NR])
        small = sb("small", [P, 5, 8])
        neg_lam = sb("neg_lam", [P, 8])
        neg_max = sb("neg_max", [P, 8])
        sink_e = sb("sink_e", [P, 4])
        sums = sb("sums", [P, 4])
        inv_sum = sb("inv_sum", [P, 2, 4])
        coef = sb("coef", [P, 1])
        ss_o = sb("ss_o", [P, 3])
        ss_h = sb("ss_h", [P, 24])

        stage = stage_rows[:, 0:1024].rearrange("p (b c) -> p b c", b=2)
        rows = stage_rows[:, 1024:2048].rearrange("p (b c) -> p b c", b=2)
        x_buf = [expd[:, :, :].rearrange("p a b -> p (a b)"), stage_rows[:, :]]
        x_sc = [gate_y[:, 0, :], gate_y[:, 1, :]] + x_pieces

        ps_a = ctx.enter_context(nc.psum_tensor("ps_a", [P, 4, 512], F32))
        ps_b = ctx.enter_context(nc.psum_tensor("ps_b", [P, 4, 512], F32))
        p_proj = [ps_a[:, 0, :], ps_a[:, 1, :]]
        p_s = ps_a[:, 2:4, :]
        p_tr = [ps_b[:, 0, :], ps_b[:, 1, :]]
        p_o = ps_b[:, 2, :]
        p_tmp = ps_b[:, 3, :]
        half_rows = [slice(0, HD), slice(HD, P)]

        names = """consts ident_ready par_in lam_in lam_sum lam_exp pos_in ang rope_arg rope_ready
            x_sq x_pow x_scaled x_hi norm_in
            w_hi_ready w_lo_ready w_used
            tp_done tp_free sq_ready ss_ready norm_chain rs_ready
            t_hi v_hi_ready v_split s_done masked max_ready x_done sink_ready sink_exp
            comb_chain comb_done at_hi pv_done o_read o_second o_joined o_squared o_pow o_ready b_sum probs_scaled
            y_hi out_ready row_summed pp_done""".split()
        sm = {n: sem("s_" + n) for n in names}

        def pair(name):
            return [sem(f"s_{name}{b}") for b in range(2)]

        x_in = [sem(f"s_x_in{b}") for b in range(3)]
        x_lo = {"dve": sem("s_x_lo_dve"), "pool": sem("s_x_lo_pool")}
        w_in_sem, pp_copied = pair("w_in"), pair("pp_copied")
        pp_tanh, pp_gated, gstored = pair("pp_tanh"), pair("pp_gated"), pair("gstored")
        rst_ready, stored, loaded = pair("rst_ready"), pair("stored"), pair("loaded")
        gate_ld, ystored = pair("gate_ld"), pair("ystored")
        y_in, res_in, out_st, x_rows_in = pair("y_in"), pair("res_in"), pair("out_st"), pair("x_rows_in")
        y_lo = pair("y_lo")
        block = ctx.enter_context(nc.Block())

        def wait_x_lo(eng, n):
            r, g = n // 4, n % 4
            if g == 0:
                eng.wait_ge(x_lo["dve"], r + 1)
            else:
                eng.wait_ge(x_lo["pool"], 3 * r + g)

        def x_lo_part(eng, n, by):
            r, g = n // 4, n % 4
            dst = (slice(None), slice(4 * g, 4 * g + 4), slice(r * P, (r + 1) * P))
            eng.wait_ge(sm["x_hi"], n + 1)
            eng.tensor_tensor(hT_lo[dst], x_sc[n % 4].rearrange("p (k t) -> p k t", k=4),
                              hT_hi[dst].bitcast(F32), ALU.subtract).then_inc(x_lo[by], 1)

        def wait(eng, s, value):
            if isinstance(value, int) and value <= 0:
                return
            eng.wait_ge(s, value)

        def iterations(eng, body, phases=PHASES):
            body(-1, -1)
            for f, n in phases:
                if n == 1:
                    body(f, f)
                else:
                    with eng.Fori(f, f + n) as it:
                        body(it, f)

        def proj_tile(it, first, s):
            nxt = proj_kind(first + 1)
            if not nxt:
                return None, None, tile_desc(("O", 0), 3)
            p = s // 4
            d = tile_desc((nxt, it + 1), p)
            u = (it + 1) * 4 + (2 + p)
            if p:
                before = tile_desc((nxt, it + 1), p - 1)
            elif first == -1:
                before = KV_TILES[1]
            else:
                before = tile_desc((kind(first), it), 3)
            return d, u, before

        def y_split_at(first, s):
            if first >= len(KINDS) - 2:
                t = (first - (len(KINDS) - 2)) * 16 + s
                return {15: 0, 16: 1, 17: 2, 18: 3, 24: 4, 35: 5}.get(t)
            return None

        def split_width(first, s):
            return OK // 4 * P if proj_kind(first + 1 + s // 16) == "O" and s // 16 < 2 else 512

        def turned_before(it, first, s):
            d, u, before = proj_tile(it, first, s)
            if s % 4 > 1 or not before["turned"] or d is None and s > 1:
                return None
            name = ("PT", "before", s) if s < 2 else ("PT", s // 4 - 1, s % 2)
            return before, name, s % 2

        @block.sync
        def _(sp):
            def load_x(r):
                wait(sp, sm["x_scaled"], r - 2)
                sp.dma_start(x_raw[r % 3], x2[r * P:(r + 1) * P, :]).then_inc(x_in[r % 3], 16)

            def load_quarter(u, q, col):
                wait(sp, sm["w_lo_ready"], u * 4 + (q - 1))
                src = w_in[0, q * 512:(q + 1) * 512, bass.ds(col, P)].rearrange("(k r) c -> r k c", k=4)
                sp.dma_start(w_raw[:, q % 2, :].rearrange("p (k c) -> p k c", k=4), src)\
                  .then_inc(w_in_sem[q % 2], 16)

            def load_quarter_o(p, q):
                Q = NQ_IN + 4 * p + q
                wait(sp, sm["w_lo_ready"], Q - 1)
                n = OK // 4
                src = w_out[0, q * n * P:(q + 1) * n * P, p * P:(p + 1) * P].rearrange("(k r) c -> r k c", k=n)
                sp.dma_start(w_raw[:, Q % 2, 0:n * P].rearrange("p (k c) -> p k c", k=n), src)\
                  .then_inc(w_in_sem[Q % 2], 16)

            def load_w_out(j):
                if j >= len(OUT_TILES):
                    return
                g, k = OUT_TILES[j]
                n, Q = GROUPS[g][1], NQ_OUT + j
                wait(sp, sm["w_lo_ready"], Q - 1)
                sp.dma_start(w_raw[:, Q % 2, :], w_out[0, k * P:(k + 1) * P, n * 512:(n + 1) * 512])\
                  .then_inc(w_in_sem[Q % 2], 16)

            def load_y(j):
                lo, hi = Y_PARTS[j]
                done = NR // 2 * 16 * (AH + 2 * min(BC, (hi * P - AW) // 256))
                for b in range(2):
                    sp.wait_ge(ystored[b], done)
                sp.wait_ge(sm["w_used"], NQ_IN - 4 + (hi - 1) // 4 + 1)
                if j >= 2:
                    for b in range(2):
                        sp.wait_ge(y_lo[b], Y_PARTS[j - 2][1])
                src = scr_y[lo * P:hi * P, :].rearrange("(k p) t -> p k t", p=P)
                sp.dma_start(hT_lo[:, lo:hi, :].bitcast(F32), src)\
                  .then_inc(y_in[j % 2], 16)

            def load_x_rows(p, b):
                wait(sp, stored[b], 16 * tile_desc(("O", 0), p)["T"])
                src = x2[b * 512:(b + 1) * 512, p * P:(p + 1) * P].rearrange("(r t) c -> t r c", r=4)
                sp.dma_start(rows[:, b, :].rearrange("p (r c) -> p r c", r=4), src).then_inc(x_rows_in[b], 16)

            def column(k, c, p):
                if k == "A":
                    return c * P + AW * p
                return (c - AH) * 256 + ((QB0 if p < 2 else GB0) + P * (p % 2))

            def load_ahead(it, first, s):
                p, q, far = (s + 4) // 4, s % 4, 0
                if p == 4:
                    p, far = 0, 1
                k = proj_kind(first + 1 + far)
                if k == "O":
                    load_quarter_o(p, q)
                elif k:
                    c = it + (1 + far)
                    load_quarter(c * 4 + (2 + p), q, column(k, c, p))
                elif first == len(KINDS) - 1:
                    load_w_out(q)
                elif s < 4:
                    for j in range(4):
                        if s == 2 and j == 2:
                            load_y(5)
                        load_w_out(4 * s + 4 + j)

            def store_rows(d, b, n):
                if d["norm"]:
                    wait(sp, rst_ready[b], d["K"] + 1)
                else:
                    wait(sp, sm["tp_free"], n + 1)
                t, p = slice(b * 512, (b + 1) * 512), d["p"]
                c = slice(p * P, (p + 1) * P)
                if d["kind"] == "A":
                    dst = scr_a[bass.ds(d["unit"], 1), t, c].rearrange("a (r t) c -> t (a r) c", r=4)
                elif d["kind"] == "B":
                    dst = scr_q[bass.ds(d["unit"] - AH, 1), t, c].rearrange("a (r t) c -> t (a r) c", r=4)
                elif d["kind"] == "O":
                    dst = scr_part[t, c].rearrange("(r t) c -> t r c", r=4)
                else:
                    dst = scr_kv[t, c].rearrange("(r t) c -> t r c", r=4)
                sp.dma_start(dst, rows[:, b, :].rearrange("p (r c) -> p r c", r=4)).then_inc(stored[b], 16)

            def store_gate(d, b):
                wait(sp, pp_gated[b], d["GT"] + 1)
                sp.dma_start(scr_g[bass.ds(d["GT"], 1), :, b * 512:(b + 1) * 512].rearrange("a p t -> p (a t)"),
                               stage[:, b, :]).then_inc(gstored[b], 16)

            def load_step(nk, unit, i):
                G = unit * NR + i
                if not (isinstance(G, int) and G < 2):
                    wait(sp, sm["v_split"], G - 1)
                t = slice(i * P, (i + 1) * P)
                if nk == "A":
                    wait(sp, stored[i // 4], unit * 48 + 80)
                    sp.dma_start(qkv[:, i % 2, 0:3 * P], scr_a[bass.ds(unit, 1), t, :].rearrange("a t c -> t (a c)"))\
                        .then_inc(loaded[i % 2], 16)
                    return
                j = unit - AH
                wait(sp, stored[i // 4], j * 32 + 16 * 28)
                kv = (j // 2) * HD
                sp.dma_start(qkv[:, i % 2, 0:2 * P], scr_q[bass.ds(j, 1), t, :].rearrange("a t c -> t (a c)"))\
                    .then_inc(loaded[i % 2], 16)
                sp.dma_start(qkv[:, i % 2, 256:384].rearrange("p (a c) -> p a c", a=2),
                               scr_kv[t, bass.ds(kv, HD)].unsqueeze(1).to_broadcast([P, 2, HD]))\
                    .then_inc(loaded[i % 2], 16)
                sp.dma_start(qkv[:, i % 2, 384:448], scr_kv[t, bass.ds(kv + P, HD)]).then_inc(loaded[i % 2], 16)

            def load_gate(st):
                i, unit = st["i"], st["unit"]
                t = slice(i * P, (i + 1) * P)
                wait(sp, ystored[i % 2], stored_before(st))
                if st["k"] == "A":
                    wait(sp, gstored[i // 4], unit * 16 + 16)
                    sp.dma_start(gate_y[:, i % 2, 0:P], scr_g[bass.ds(unit, 1), :, t].rearrange("a p t -> p (a t)"))\
                      .then_inc(gate_ld[i % 2], 16)
                    return
                j = unit - AH
                wait(sp, gstored[i // 4], j * 32 + 160)
                for r in range(2):
                    dst = gate_y[0:HD, i % 2, r * 256:(r + 1) * 256].rearrange("d (a t) -> d a t", a=2)
                    src = scr_g[bass.ds(j * 2 + AH, 2), r * HD:(r + 1) * HD, t].rearrange("a d t -> d a t")
                    sp.dma_start(dst, src).then_inc(gate_ld[i % 2], 16)

            def store_y(st, it, first):
                i = st["i"]
                t = slice(i * P, (i + 1) * P)
                if st["k"] == "A":
                    wait(sp, sm["tp_free"], use_number(("YT", i), it, first) + 1)
                    sp.dma_start(scr_y[bass.ds(st["unit"] * P, P), t], gate_y[:, i % 2, 0:P])\
                      .then_inc(ystored[i % 2], 16)
                    return
                wait(sp, sm["o_read"], st["G"] * 2 + 2)
                for r in range(2):
                    dst = scr_y[bass.ds((st["unit"] - AH) * 256 + AW, 256), t]\
                        .rearrange("(a r d) t -> r d a t", a=2, r=2)[r]
                    sp.dma_start(dst, gate_y[0:HD, i % 2, r * 256:(r + 1) * 256].rearrange("d (a t) -> d a t", a=2))\
                      .then_inc(ystored[i % 2], 16)

            for r in range(3):
                load_x(r)
            for q in range(2):
                load_quarter(0, q, KB0)
            pars = [(head_w[:, n, :], w.partition_broadcast(P)[:, 0, :])
                    for n, w in enumerate((q_norm_a, k_norm_a, q_norm_b, k_norm_b))]
            pars += [(sub_c[:, 0:1], subln_w[0].rearrange("(p a) -> p a", a=1)),
                     (sink_t[:, :], sinks.partition_broadcast(P)[:, 0, :])]
            sp.dma_start(pos_i[:, :], positions[0].rearrange("(r p) -> p r", p=P),
                          allow_slow_non_contiguous=True).then_inc(sm["pos_in"], 16)
            sp.dma_start(qkv[:, 1, 384:384 + HALF], inv_freq.partition_broadcast(P)[:, 0, :]).then_inc(sm["pos_in"], 16)
            for n, w in enumerate((lambda_q1, lambda_k1, lambda_q2, lambda_k2)):
                sp.dma_start(qkv[:, 0, n * HD:(n + 1) * HD], w.partition_broadcast(P)[:, 0, :])\
                   .then_inc(sm["lam_in"], 16)
            for dst, src in pars:
                sp.dma_start(dst, src, allow_slow_non_contiguous=True).then_inc(sm["par_in"], 16)
            for r in range(3, NR):
                load_x(r)
                if r in (5, 6):
                    load_quarter(0, r - 3, KB0)
            for s in range(8):
                if s < 4:
                    load_quarter(1, s, VB0)
                else:
                    load_quarter(2, s - 4, 0)
                if 4 <= s < 6:
                    store_rows(KV_TILES[0], s - 4, 32 + s - 4)
            sp.wait_ge(sm["lam_sum"], 1)
            sp.wait_ge(sm["rope_arg"], 2)

            def body(it, first):
                for s in range(16):
                    i = s // 2
                    d, u, before = proj_tile(it, first, s)
                    load_ahead(it, first, s)
                    t = (first - (len(KINDS) - 2)) * 16 + s
                    if t in (13, 14, 15, 16, 20):
                        load_y((13, 14, 15, 16, 20).index(t))
                    if first == len(KINDS) and s == 1:
                        store_y(step_at(-1, it, first), it, first)
                    if d and s % 4 == 3 and not d["turned"]:
                        store_gate(d, 0)
                        store_gate(d, 1)
                    cur = step_at(i, it, first)
                    back1 = step_at(i - 1, it, first)
                    back2 = step_at(i - 2, it, first)
                    if s % 2 == 0:
                        if cur and i + 1 < NR:
                            load_step(cur["k"], it, i + 1)
                        elif i + 1 == NR and kind(first + 1):
                            load_step(kind(first + 1), it + 1, 0)
                        if back2 and back2["k"] == "B" and not (first == len(KINDS) and s == 2):
                            store_y(back2, it, first)
                        if back1:
                            load_gate(back1)
                    elif back2 and back2["k"] == "A":
                        store_y(back2, it, first)
                    tb = turned_before(it, first, s)
                    if tb:
                        store_rows(tb[0], tb[2], use_number(tb[1], it, first))
                    if d and d["kind"] == "O" and s % 4 == 2:
                        for b in range(2):
                            load_x_rows(d["p"], b)
                    if first == len(KINDS) and s == 1:
                        sp.wait_ge(sm["tp_done"], use_number(("AT", NR - 1, 1), it, first) + 1)
                        load_res(0)
                    if first == len(KINDS) and s == 3:
                        load_res(1)

            def part(a, g):
                h, n = GROUPS[g]
                return a[h * 512:(h + 1) * 512, n * 512:(n + 1) * 512].rearrange("(r p) c -> p r c", r=4)

            def load_res(g):
                if g >= 2:
                    sp.wait_ge(out_st[g % 2], 16 * (g // 2))
                else:
                    for b in range(2):
                        sp.wait_ge(stored[b], 16 * (26 + 2 * BC + 4))
                src = part(x2 if GROUPS[g][1] else scr_part, g)
                sp.dma_start(x_buf[g % 2].rearrange("p (r c) -> p r c", r=4), src).then_inc(res_in[g % 2], 16)

            def store_out(g):
                sp.wait_ge(sm["out_ready"], 4 * (g + 1))
                sp.dma_start(part(out2, g), x_buf[g % 2].rearrange("p (r c) -> p r c", r=4))\
                  .then_inc(out_st[g % 2], 16)

            iterations(sp, body, SP_PHASES)

            for j in range(16, len(OUT_TILES)):
                g, k = OUT_TILES[j]
                load_w_out(j + 4)
                if k == (4 if GROUPS[g][1] else OK + 2):
                    store_out(g - 1)
                if k == 8 and g + 1 < len(GROUPS):
                    load_res(g + 1)
                if g == len(GROUPS) - 1 and k == OK:
                    load_res(g)
            for r in range(4):
                g = len(GROUPS) - 1
                sp.wait_ge(sm["out_ready"], 4 * g + r + 1)
                sp.dma_start(part(out2, g)[:, r], x_buf[g % 2][:, r * 512:(r + 1) * 512]).then_inc(out_st[g % 2], 16)
            for b in range(2):
                sp.wait_ge(out_st[b], 16 * (len(GROUPS) // 2) + (48 if b else 0))
                sp.wait_ge(gstored[b], 16 * (AH + 2 * BC))
                sp.wait_ge(ystored[b], 8 * NR * (AH + 2 * BC))

        @block.scalar
        def _(act):
            def split_w(Q, b4, w=512):
                wait(act, w_in_sem[b4 % 2], (Q - b4) * 8 + 16 * (b4 // 2 + 1))
                wait(act, sm["w_used"], Q - 3)
                act.activation(w_hi[:, b4, 0:w], w_raw[:, b4 % 2, 0:w], ACT.Copy).then_inc(sm["w_hi_ready"], 1)

            act.dma_start(norm_c[:, :], norm_w[0].rearrange("(k p) -> p k", p=P),
                          allow_slow_non_contiguous=True).then_inc(sm["norm_in"], 16)

            def square_x(r):
                act.wait_ge(x_in[r % 3], 16 * (r // 3 + 1))
                act.activation(hT_lo[:, :, r * P:(r + 1) * P], x_raw[r % 3].rearrange("p (k t) -> p k t", k=KT),
                               ACT.Square, accum_out=ss_x[:, r:r + 1]).then_inc(sm["x_sq"], 1)

            square_x(0)
            square_x(1)
            for r in range(NR):
                for g in range(4):
                    act.wait_ge(sm["tp_free"], 4 * r + g + 1)
                    act.activation(hT_hi[:, 4 * g:4 * g + 4, r * P:(r + 1) * P],
                                   x_sc[(4 * r + g) % 4].rearrange("p (k t) -> p k t", k=4), ACT.Copy)\
                       .then_inc(sm["x_hi"], 1)
                    if g == 1 and r + 2 < NR:
                        square_x(r + 2)
                if 1 <= r < 5:
                    split_w(r - 1, r - 1)

            act.wait_ge(sm["rope_arg"], 2)
            act.activation(cos_t[:, :, :], cos_t[:, :, :], ACT.Sin).then_inc(sm["rope_ready"], 1)
            act.activation(sin_t[:, :, :], sin_t[:, :, :], ACT.Sin).then_inc(sm["rope_ready"], 1)
            act.wait_ge(sm["lam_sum"], 1)
            act.activation(neg_lam[:, 2:4], neg_lam[:, 0:2], ACT.Exp).then_inc(sm["lam_exp"], 1)

            def stage_free(before, b, it, first):
                if before is None:
                    return
                if before["norm"]:
                    wait(act, rst_ready[b], before["K"] + 1)
                elif before["turned"]:
                    n = (use_number(("PT", before["p"], b), it, first) if before is not KV_TILES[1]
                         else BASE[-1] + b)
                    wait(act, sm["tp_free"], n + 1)
                else:
                    wait(act, gstored[b], before["GT"] * 16 + 16)

            def evacuate(d, before, u, it, first):
                for b in range(2):
                    wait(act, sm["w_used" if b else "pp_done"], u * 4 + 4 if b else u + 1)
                    stage_free(before, b, it, first)
                    if d["turned"]:
                        act.activation(stage[:, b, :], p_proj[b], ACT.Copy).then_inc(pp_copied[b], 1)
                    else:
                        act.activation(stage[:, b, :], p_proj[b], ACT.Tanh, scale=0.5).then_inc(pp_tanh[b], 1)

            def square_heads(d, n, bank, b):
                wait(act, sm["tp_done"], n + 1)
                if not (isinstance(d["K"], int) and d["K"] == 0 and b == 0):
                    wait(act, sm["norm_chain"], d["K"] * 6 + 3 * b)
                act.activation(p_tmp, p_tr[bank], ACT.Square).then_inc(sm["sq_ready"], 1)

            def body(it, first):
                Q0 = (it + 1) * 16 + 8
                for s in range(16):
                    i = s // 2
                    d, u, before = proj_tile(it, first, s)
                    split_y(y_split_at(first, s))
                    if d:
                        split_w(Q0 + (s + 2), (s + 2) % 4, split_width(first, s + 2))
                        if s % 4 == 3:
                            evacuate(d, before, u, it, first)
                    elif s < 4:
                        for j in range(4 * s + 2, 4 * s + 6):
                            split_w(NQ_OUT + j, j % 4)
                    cur = step_at(i, it, first)
                    back1 = step_at(i - 1, it, first)
                    back2 = step_at(i - 2, it, first)
                    tb = turned_before(it, first, s)
                    if tb and tb[0]["norm"]:
                        square_heads(tb[0], use_number(tb[1], it, first), bank_of(tb[1], first), tb[2])
                    if s % 2 == 0:
                        if back2 and back2["k"] == "A":
                            wait(act, sm["o_pow"], back2["G"] * 4 + 4)
                            act.activation(o_sb[:, 0:P], o_sb[:, 0:P], ACT.Copy, scale=ss_o[:, 0:1])\
                               .then_inc(sm["o_ready"], 1)
                        if back1:
                            wait(act, sm["pv_done"], back1["G"])
                            for m, (lo, hi) in enumerate(at_spans(back1)):
                                name = ("AT", back1["i"], m)
                                wait(act, sm["tp_done"], use_number(name, it, first) + 1)
                                act.activation(aT_hi[:, lo:hi], p_tr[bank_of(name, first)][:, 0:hi - lo],
                                               ACT.Copy).then_inc(sm["at_hi"], 1)
                        if cur and cur["k"] == "A":
                            exp_a(cur, 0)
                        elif cur:
                            exp_b(cur, it - AH)
                    else:
                        if cur and cur["k"] == "A":
                            exp_a(cur, 1)
                        if back1 and back1["k"] == "A":
                            wait(act, sm["pv_done"], back1["G"] + 1)
                            act.activation(o_sb[:, P:2 * P], p_o[:, P:2 * P], ACT.Copy).then_inc(sm["o_second"], 1)
                        elif back1:
                            wait(act, sm["pv_done"], back1["G"] + 1)
                            act.activation(o_second_b, p_o[HD:P, :], ACT.Copy).then_inc(sm["o_second"], 1)
                        nk = cur["k"] if cur and i + 1 < NR else kind(first + 1) if i + 1 == NR else None
                        if nk:
                            name = ("T", (i + 1) % NR)
                            n = use_number(name, it, first)
                            bank = p_tr[bank_of(name, first)]
                            wait(act, sm["tp_done"], n + 1)
                            hi_qk(nk, (i + 1) % NR, bank)
                        if back1 and back1["k"] == "A":
                            wait(act, sm["o_read"], back1["G"] * 2 + 2)
                            act.activation(p_o[:, 2 * P:3 * P], o_sb[:, 0:P], ACT.Square,
                                           scale=inv_sum[:, back1["i"] % 2, 0:1], accum_out=ss_o[:, 2:3])\
                               .then_inc(sm["o_squared"], 1)
                        if cur:
                            hi_v(cur, it)

            def split_y(part):
                if part is None:
                    return
                act.wait_ge(y_in[part % 2], 16 * (part // 2 + 1))
                for k in range(*Y_PARTS[part]):
                    act.activation(hT_hi[:, k, :], hT_lo[:, k, :].bitcast(F32), ACT.Copy).then_inc(sm["y_hi"], 1)

            def hi_qk(nk, j, bank):
                w = P if nk == "A" else 2 * P
                for c, h in enumerate(half_rows):
                    ins = act.activation(q_pair[h, c * w:(c + 1) * w], bank[h, 0:w], ACT.Copy, scale=QSCALE)
                ins.then_inc(sm["t_hi"], 1)
                t = slice(j * P, (j + 1) * P)
                if nk == "A":
                    for c, h in enumerate(half_rows):
                        for dst in half_rows:
                            ins = act.activation(k_dup[c][dst, t], bank[h, w:w + P], ACT.Copy)
                else:
                    ins = act.activation(k_dup[0][:, t], bank[:, w:w + P], ACT.Copy)
                ins.then_inc(sm["t_hi"], 1)

            def hi_v(st, it):
                i, k = st["i"], st["k"]
                lo, w = (2 * P, P) if k == "A" else (3 * P, HD)
                if i == 0:
                    wait(act, sm["pv_done"], st["G"])
                wait(act, loaded[i % 2], loads_by(k, it, i))
                act.activation(v_hi[:, i, 0:w], qkv[:, i % 2, lo:lo + w], ACT.Copy).then_inc(sm["v_hi_ready"], 1)

            def exp_a(st, c):
                wait(act, sm["max_ready"], st["G"] * 2 + (c + 1))
                if c == 0:
                    wait(act, sm["comb_done"], st["G"])
                w = (st["i"] + 1) * P
                flat = p_s.rearrange("p a b -> p (a b)")
                act.activation(expd[:, c, 0:w], flat[:, 0:w], ACT.Exp, bias=neg_max[:, c:c + 1],
                               accum_out=sums[:, c:c + 1]).then_inc(sm["x_done"], 1)

            def exp_b(st, j):
                gb = st["G"] - AH * NR
                lo = P if st["i"] == 0 else 0
                wait(act, sm["sink_ready"], gb * 4 + 4)
                wait(act, sm["b_sum"], gb * 2)
                for r in range(2):
                    for p in range(2):
                        n = 2 * r + p
                        ins = act.activation(expd[:, st["i"] % 2, n * 256 + lo:n * 256 + 256],
                                             p_s[:, r, p * 256 + lo:p * 256 + 256], ACT.Exp,
                                             bias=neg_max[:, n:n + 1], accum_out=sums[:, n:n + 1])
                    ins.then_inc(sm["x_done"], 1)
                act.activation(sink_e[:, :], neg_max[:, 4:8], ACT.Exp).then_inc(sm["sink_exp"], 1)

            for s in range(8):
                if s >= 2:
                    split_w(s + 2, (s + 2) % 4)
                u = s // 4
                if s % 4 == 3:
                    evacuate(KV_TILES[u], KV_TILES[0] if u else None, u, -1, -1)
                if 4 <= s < 6:
                    square_heads(KV_TILES[0], 32 + s - 4, (32 + s - 4) % 2, s - 4)
            iterations(act, body)

            for j in range(18, len(OUT_TILES)):
                split_w(NQ_OUT + j, j % 4)

        @block.tensor
        def _(pe):
            def three(dst, a_hi, a_lo, b_hi, b_lo, start, stop):
                pe.matmul(dst, a_hi, b_hi, start=start, stop=False)
                pe.matmul(dst, a_hi, b_lo, start=False, stop=False)
                return pe.matmul(dst, a_lo, b_hi, start=False, stop=stop)

            def bank_free(n):
                wait(pe, sm["tp_free"], n - 1)

            def quarter(d, u, q, b, before):
                part_o = d["kind"] == "O"
                nk = OK // 4 if part_o else 4
                if part_o:
                    wait(pe, y_lo[b], nk * (q + 1))
                if b == 0:
                    wait(pe, sm["w_lo_ready"], u * 4 + (q + 1))
                if q == 0 and before is not None:
                    if before["turned"]:
                        wait(pe, pp_copied[b], before["T"] + 1)
                    else:
                        wait(pe, pp_gated[b], before["GT"] + 1)
                for k in range(nk):
                    w = slice(k * P, (k + 1) * P)
                    t = slice(b * 512, (b + 1) * 512)
                    kk = nk * q + k
                    mm = three(p_proj[b], w_hi[:, q, w], w_lo[:, q, w], hT_hi[:, kk, t], hT_lo[:, kk, t],
                               kk == 0, kk == 4 * nk - 1)
                if b:
                    mm.then_inc(sm["w_used"], 1)
                elif q == 3:
                    mm.then_inc(sm["pp_done"], 1)

            def turn_tile(d, b, n, bank):
                wait(pe, pp_copied[b], d["T"] + 1)
                bank_free(n)
                for r in range(4):
                    mm = pe.transpose(p_tr[bank][:, r * P:(r + 1) * P], stage[:, b, r * P:(r + 1) * P], ident[:, :])
                mm.then_inc(sm["tp_done"], 1)

            def q_times_k(dst, q, k, h, k_lo):
                pe.matmul(dst, q, k, start=True, stop=False)
                return pe.matmul(dst, q[h, :], k_lo, start=False, stop=True)

            def scores_a(st, c, it, first):
                i = st["i"]
                w = (i + 1) * P
                if c == 0:
                    wait(pe, sm["tp_free"], qk_split(i, it, first))
                wait(pe, sm["x_done"], st["G"] * 2 + c)
                flat = p_s.rearrange("p a b -> p (a b)")
                h = slice(c * HD, (c + 1) * HD)
                for lo in range(0, w, 512):
                    t = slice(lo, min(w, lo + 512))
                    mm = q_times_k(flat[:, t], q_pair[:, c * P:(c + 1) * P], k_dup[c][:, t], h, kT_lo[h, t])
                mm.then_inc(sm["s_done"], 1)

            def scores_b(st, it, first):
                i = st["i"]
                wait(pe, sm["tp_free"], qk_split(i, it, first))
                wait(pe, sm["x_done"], st["G"] * 2)
                t = slice(max(i - 1, 0) * P, (i + 1) * P)
                lo = P if i == 0 else 0
                for r in range(2):
                    h = slice(r * HD, (r + 1) * HD)
                    for p in range(2):
                        mm = q_times_k(p_s[:, r, p * 256 + lo:p * 256 + 256],
                                       q_pair[:, (2 * r + p) * P:(2 * r + p + 1) * P], k_dup[0][:, t], h, kT_lo[h, t])
                    mm.then_inc(sm["s_done"], 1)

            def turn_probs(st, it, first):
                i = st["i"]
                if st["k"] == "A":
                    wait(pe, sm["comb_done"], st["G"] + 1)
                    blocks = [expd[:, 1, b * P:(b + 1) * P] for b in range(i + 1)]
                else:
                    wait(pe, sm["probs_scaled"], st["G"] - (AH * NR - 1))
                    blocks = [expd[:, i % 2, n * 256 + b * P:n * 256 + (b + 1) * P]
                              for n in range(4) for b in ((0, 1) if i else (1,))]
                for m, (lo, hi) in enumerate(at_spans(st)):
                    name = ("AT", i, m)
                    bank_free(use_number(name, it, first))
                    for b in range((hi - lo) // P):
                        mm = pe.transpose(p_tr[bank_of(name, first)][:, b * P:(b + 1) * P],
                                          blocks[lo // P + b], ident[:, :])
                    mm.then_inc(sm["tp_done"], 1)

            def values(st, it, first):
                i = st["i"]
                last = ("AT", i, len(at_spans(st)) - 1)
                wait(pe, sm["v_split"], st["G"] + 1)
                wait(pe, sm["tp_free"], use_number(last, it, first) + 1)
                wait(pe, sm["o_read"], st["G"] * 2)
                if st["k"] == "A":
                    for b in range(i + 1):
                        a = slice(b * P, (b + 1) * P)
                        pe.matmul(p_o[:, 0:2 * P].rearrange("t (c e) -> t c e", c=2), aT_hi[:, a],
                                  parts[:, 2:4, a], start=b == 0, stop=False)
                        mm = pe.matmul(p_o[:, 0:P], aT_lo[:, a], v_hi[:, b, :], start=False, stop=b == i)
                else:
                    nb = 2 if i else 1
                    a_hi, a_lo = (a[:, 0:4 * nb * P].rearrange("k (n b t) -> k b n t", n=4, b=nb)
                                  for a in (aT_hi, aT_lo))
                    dst = p_o.rearrange("d (n t) -> d n t", n=4)
                    for b in range(nb):
                        vb = i - (nb - 1) + b
                        pe.matmul(dst, v_hi[:, vb, :], a_hi[:, b], start=b == 0, stop=False)
                        mm = pe.matmul(dst, v_hi[:, vb, :], a_lo[:, b], start=False, stop=b == nb - 1)
                mm.then_inc(sm["pv_done"], 1)

            def turn_o(st, it, first):
                name = ("YT", st["i"])
                wait(pe, sm["o_ready"], st["G"] + 1)
                bank_free(use_number(name, it, first))
                pe.transpose(p_tr[bank_of(name, first)][:, 0:P], o_sb[:, 0:P], ident[:, :])\
                  .then_inc(sm["tp_done"], 1)

            def turn_qk(nk, i, it, first):
                name = ("T", i)
                wait(pe, loaded[i % 2], loads_by(nk, it + 1 if i == 0 else it, i))
                n = use_number(name, it, first)
                bank_free(n)
                bank = p_tr[bank_of(name, first)]
                for a in range(2 if nk == "A" else 3):
                    mm = pe.transpose(bank[:, a * P:(a + 1) * P], qkv[:, i % 2, a * P:(a + 1) * P], ident[:, :])
                mm.then_inc(sm["tp_done"], 1)

            def out_bank_free(g):
                if g == 0:
                    for b in range(2):
                        pe.wait_ge(pp_copied[b], tile_desc(("O", 0), 3)["T"] + 1)
                    pe.wait_ge(sm["x_done"], 2 * NR * len(KINDS))
                elif g == 1:
                    pe.wait_ge(sm["tp_free"], BASE[12] + len(uses_of(12)))
                    pe.wait_ge(sm["o_read"], 2 * NR * len(KINDS))
                else:
                    pe.wait_ge(sm["out_ready"], 4 * (g - 1))

            def out_tile(j):
                g, k = OUT_TILES[j]
                half, n = GROUPS[g]
                first_k = 0 if n else OK
                if k == first_k:
                    out_bank_free(g)
                pe.wait_ge(sm["w_lo_ready"], NQ_OUT + j + 1)
                pe.wait_ge(y_lo[half], k + 1)
                for r in range(4):
                    t = slice(half * 512 + r * P, half * 512 + (r + 1) * P)
                    mm = three((ps_a, ps_b)[g % 2][:, r, :], hT_hi[:, k, t], hT_lo[:, k, t],
                               w_hi[:, j % 4, :], w_lo[:, j % 4, :], k == first_k, k == KT - 1)
                mm.then_inc(sm["w_used"], 1)

            def body(it, first):
                for s in range(16):
                    i = s // 2
                    d, u, before = proj_tile(it, first, s)
                    cur = step_at(i, it, first)
                    back1 = step_at(i - 1, it, first)
                    back2 = step_at(i - 2, it, first)
                    tb = turned_before(it, first, s)
                    if d:
                        quarter(d, u, s % 4, 0, before)
                    elif s < 4:
                        out_tile(4 * s)
                        out_tile(4 * s + 1)
                    if s % 2 == 0:
                        if tb:
                            turn_tile(tb[0], tb[2], use_number(tb[1], it, first), bank_of(tb[1], first))
                    elif back2 and back2["k"] == "A":
                        turn_o(back2, it, first)
                    if d:
                        quarter(d, u, s % 4, 1, before)
                    elif s < 4:
                        if s == 1:
                            values(back1, it, first)
                        out_tile(4 * s + 2)
                        out_tile(4 * s + 3)
                    if s % 2 == 0:
                        if cur and cur["k"] == "A":
                            scores_a(cur, 0, it, first)
                        elif cur:
                            scores_b(cur, it, first)
                        if back1:
                            turn_probs(back1, it, first)
                        continue
                    if tb:
                        turn_tile(tb[0], tb[2], use_number(tb[1], it, first), bank_of(tb[1], first))
                    if cur and cur["k"] == "A":
                        scores_a(cur, 1, it, first)
                    if back1 and d:
                        values(back1, it, first)
                    nk = cur["k"] if cur and i + 1 < NR else kind(first + 1) if i + 1 == NR else None
                    if nk:
                        turn_qk(nk, (i + 1) % NR, it, first)

            def first_half_k(q, g):
                if g == 0:
                    pe.wait_ge(sm["w_lo_ready"], q + 1)
                if q == g == 0:
                    wait_x_lo(pe, 2 * NR - 4)
                    wait_x_lo(pe, 2 * NR - 1)
                w, kk = slice(g * P, (g + 1) * P), 4 * q + g
                return three(p_proj[0], w_hi[:, q, w], w_lo[:, q, w], hT_hi[:, kk, 0:512], hT_lo[:, kk, 0:512],
                             kk == 0, kk == KT - 1)

            pe.wait_ge(sm["ident_ready"], 2)
            for r in range(NR):
                pe.wait_ge(sm["x_scaled"], r + 1)
                for g in range(4):
                    n = 4 * r + g
                    wait(pe, sm["tp_free"], n - 3)
                    for k in range(4):
                        f = (4 * g + k) * P
                        mm = pe.transpose(ps_b[:, g, k * P:(k + 1) * P], x_buf[r % 2][:, f:f + P], ident[:, :])
                    mm.then_inc(sm["tp_done"], 1)
                    q = r - NR // 2 - 1
                    if q >= 0:
                        mm = first_half_k(q, g)
            for g in range(4):
                mm = first_half_k(3, g)
            mm.then_inc(sm["pp_done"], 1)
            wait_x_lo(pe, 4 * NR - 4)
            wait_x_lo(pe, 4 * NR - 1)
            for s in range(8):
                u = s // 4
                if u:
                    quarter(KV_TILES[u], u, s % 4, 0, KV_TILES[0])
                quarter(KV_TILES[u], u, s % 4, 1, KV_TILES[0] if u else None)
                if 4 <= s < 6:
                    turn_tile(KV_TILES[0], s - 4, 32 + s - 4, s % 2)
            iterations(pe, body)

            last = [j for j, (g, k) in enumerate(OUT_TILES) if g == len(GROUPS) - 1]
            for j in range(16, last[0]):
                out_tile(j)
            out_bank_free(len(GROUPS) - 1)
            for r in range(4):
                t = slice(512 + r * P, 512 + (r + 1) * P)
                for j in last:
                    k = OUT_TILES[j][1]
                    if r == 0:
                        pe.wait_ge(sm["w_lo_ready"], NQ_OUT + j + 1)
                    mm = three(ps_b[:, r, :], hT_hi[:, k, t], hT_lo[:, k, t], w_hi[:, j % 4, :], w_lo[:, j % 4, :],
                               j == last[0], j == last[-1])
                mm.then_inc(sm["row_summed"], 1)

        @block.vector
        def _(dve):
            links = [0]

            def link(ins):
                links[0] += 1
                ins.then_inc(sm["ang"], 1)
                dve.wait_ge(sm["ang"], links[0])

            def tt(o, a, b, op):
                return dve.tensor_tensor(o, a, b, op)

            def split_w(Q, b4, w=512):
                wait(dve, sm["w_hi_ready"], Q + 1)
                tt(w_lo[:, b4, 0:w], w_raw[:, b4 % 2, 0:w], w_hi[:, b4, 0:w].bitcast(F32), ALU.subtract)\
                    .then_inc(sm["w_lo_ready"], 1)

            def scale_x(r):
                dve.wait_ge(sm["x_pow"], 3 * (r + 1))
                if r >= 2:
                    dve.wait_ge(sm["tp_done"], 4 * (r - 1))
                dve.tensor_scalar(x_buf[r % 2], x_raw[r % 3], ss_x[:, r:r + 1], None, ALU.mult)\
                   .then_inc(sm["x_scaled"], 1)

            scale_x(0)
            dve.wait_ge(sm["norm_in"], 16)
            for r in range(NR):
                for g in range(4):
                    n = 4 * r + g
                    dve.wait_ge(sm["tp_done"], n + 1)
                    if n >= 4:
                        wait_x_lo(dve, n - 4)
                    tt(x_sc[n % 4].rearrange("p (k t) -> p k t", k=4),
                       ps_b[:, g, :].rearrange("p (k t) -> p k t", k=4),
                       norm_c[:, 4 * g:4 * g + 4].unsqueeze(2).to_broadcast([P, 4, P]), ALU.mult)\
                        .then_inc(sm["tp_free"], 1)
                    if g == 1:
                        x_lo_part(dve, n - 1, "dve")
                        if r + 1 < NR:
                            scale_x(r + 1)
                        if 2 <= r < 6:
                            split_w(r - 2, r - 2)

            ang = qkv[:, 1, 128:384]
            ang3 = ang.rearrange("p (r f) -> p r f", r=NR)
            dve.wait_ge(sm["pos_in"], 32)
            link(dve.tensor_copy(pos_f[:, :], pos_i[:, :]))
            link(tt(ang3, pos_f[:, :].unsqueeze(2).to_broadcast([P, NR, HALF]),
                    qkv[:, 1, 384:384 + HALF].unsqueeze(1).to_broadcast([P, NR, HALF]), ALU.mult))
            left, parts = 2 * math.pi, []
            for _ in range(3):
                e = 2.0 ** (math.floor(math.log2(left)) - 7)
                parts.append(math.floor(left / e) * e)
                left -= parts[-1]
            parts.append(left)
            magic = 1.5 * 2.0 ** 23
            turns = o_sb[:, :]
            for table, quarter_turn in ((cos_t, 0.25), (sin_t, 0.0)):
                t2 = table[:, :, :].rearrange("p r f -> p (r f)")
                link(dve.tensor_scalar(turns, ang, 0.5 / math.pi, quarter_turn, ALU.mult, ALU.add))
                link(dve.tensor_scalar(turns, turns, magic, magic, ALU.add, ALU.subtract))
                src = ang
                for c in parts:
                    link(dve.scalar_tensor_tensor(t2, turns, -c, src, ALU.mult, ALU.add))
                    src = t2
                link(dve.tensor_scalar(t2, t2, quarter_turn * 2 * math.pi, 3.1415925, ALU.add, ALU.min))
                dve.tensor_scalar(t2, t2, -3.1415925, None, ALU.max).then_inc(sm["rope_arg"], 1)

            dve.wait_ge(sm["lam_in"], 64)
            lv = qkv[:, 0, 0:256].rearrange("p (a b c) -> p a b c", a=2, b=2)
            prod = qkv[:, 1, 0:128].rearrange("p (a c) -> p a c", a=2)
            link(tt(prod, lv[:, :, 0, :], lv[:, :, 1, :], ALU.mult))
            dve.tensor_reduce(neg_lam[:, 0:2], prod, AX, ALU.add).then_inc(sm["lam_sum"], 1)
            dve.wait_ge(sm["lam_exp"], 1)
            link(tt(neg_lam[:, 4:5], neg_lam[:, 3:4], neg_lam[:, 2:3], ALU.subtract))
            link(dve.tensor_scalar(neg_lam[:, 5:6], neg_lam[:, 4:5], LAM_INIT, None, ALU.subtract))
            dve.wait_ge(sm["par_in"], 16 * 6)
            link(dve.tensor_scalar(sub_c[:, 1:2], sub_c[:, 0:1], 0.5 * (1 - LAM_INIT), None, ALU.mult))

            def split_y(part):
                if part is None:
                    return
                for k in range(*Y_PARTS[part]):
                    dve.wait_ge(sm["y_hi"], k + 1)
                    dst = hT_lo[:, k, 0:512]
                    tt(dst, dst.bitcast(F32), hT_hi[:, k, 0:512].bitcast(F32), ALU.subtract).then_inc(y_lo[0], 1)

            def gate(d, b):
                wait(dve, pp_tanh[b], d["GT"] + 1)
                dve.scalar_tensor_tensor(stage[:, b, :], stage[:, b, :], 1.0, p_proj[b], ALU.add, ALU.mult)\
                   .then_inc(pp_gated[b], 1)

            def rows_out(d, b, n, bank):
                dst = rows[:, b, :]
                wait(dve, stored[b], d["T"] * 16)
                if d["kind"] == "O":
                    wait(dve, x_rows_in[b], 16 * (d["p"] + 1))
                    wait(dve, sm["tp_done"], n + 1)
                    tt(dst, p_tr[bank], dst, ALU.add).then_inc(sm["tp_free"], 1)
                    return
                if not d["norm"]:
                    wait(dve, sm["tp_done"], n + 1)
                    dve.tensor_copy(dst, p_tr[bank]).then_inc(sm["tp_free"], 1)
                    return
                seq = d["K"] * 2 + b
                wait(dve, sm["sq_ready"], seq + 1)
                wait(dve, sm["rs_ready"], seq * 3)
                dve.tensor_reduce(ss_h[:, 0:8], p_tmp.rearrange("p (g c) -> p g c", g=8), AX, ALU.add)\
                   .then_inc(sm["ss_ready"], 1)
                x3 = dst.rearrange("p (g c) -> p g c", g=8)
                tt(x3, p_tr[bank].rearrange("p (g c) -> p g c", g=8),
                   head_w[:, d["w"], :].unsqueeze(1).to_broadcast([P, 8, HD]), ALU.mult)\
                    .then_inc(sm["tp_free"], 1)

            def rotate(d, b, n):
                if not d["norm"]:
                    return
                seq = d["K"] * 2 + b
                dst = rows[:, b, :]
                x5 = dst.rearrange("p (r h f c) -> p r h f c", r=4, h=2, f=2)
                t5 = p_tmp.rearrange("p (r h f c) -> p r h f c", r=4, h=2, f=2)
                r4 = slice(4 * b, 4 * b + 4)
                sn = sin_t[:, r4, :].unsqueeze(2).to_broadcast([P, 4, 2, HALF])
                cs = cos_t[:, r4, :].unsqueeze(2).to_broadcast([P, 4, 4, HALF])
                wait(dve, sm["tp_free"], n + 1)
                wait(dve, sm["ss_ready"], seq + 1)
                tt(t5[:, :, :, 0, :], x5[:, :, :, 1, :], sn, ALU.mult)
                tt(t5[:, :, :, 1, :], x5[:, :, :, 0, :], sn, ALU.mult).then_inc(sm["norm_chain"], 1)
                x4 = dst.rearrange("p (r g c) -> p r g c", r=4, g=4)
                wait(dve, sm["norm_chain"], seq * 3 + 1)
                tt(x4, x4, cs, ALU.mult).then_inc(sm["norm_chain"], 1)
                wait(dve, sm["norm_chain"], seq * 3 + 2)
                tt(x5[:, :, :, 0, :], x5[:, :, :, 0, :], t5[:, :, :, 0, :], ALU.subtract)
                tt(x5[:, :, :, 1, :], x5[:, :, :, 1, :], t5[:, :, :, 1, :], ALU.add)\
                    .then_inc(sm["norm_chain"], 1)

            def max_a(st, c):
                i = st["i"]
                flat = p_s.rearrange("p a b -> p (a b)")
                last = flat[:, i * P:(i + 1) * P]
                n = st["G"] * 2 + (c + 1)
                wait(dve, sm["s_done"], n)
                tt(last, last, mask[:, P:2 * P], ALU.add).then_inc(sm["masked"], 1)
                wait(dve, sm["masked"], n)
                dve.tensor_reduce(neg_max[:, c:c + 1], flat[:, 0:(i + 1) * P], AX, ALU.max, negate=True)\
                   .then_inc(sm["max_ready"], 1)

            def max_b(st, j):
                lo = P if st["i"] == 0 else 0
                gb = st["G"] - AH * NR
                for r in range(2):
                    wait(dve, sm["s_done"], st["G"] * 2 + (r + 1))
                    part = p_s[:, r, :].rearrange("p (a b) -> p a b", a=2)[:, :, lo:256]
                    tt(part, part, mask[:, lo:256].unsqueeze(1).to_broadcast([P, 2, 256 - lo]), ALU.add)\
                        .then_inc(sm["masked"], 1)
                wait(dve, sm["masked"], st["G"] * 2 + 2)
                sk = sink_t[:, bass.ds(j * 4, 4)].rearrange("t (p r) -> t r p", r=2)
                low, high = (neg_max[:, n:n + 4].rearrange("t (r p) -> t r p", r=2) for n in (0, 4))
                flat = p_s.rearrange("p a b -> p (a b)").rearrange("p (n s) -> p n s", n=4)
                dve.tensor_reduce(neg_max[:, 0:4], flat[:, :, lo:256], AX, ALU.max).then_inc(sm["sink_ready"], 1)
                wait(dve, sm["sink_ready"], gb * 4 + 1)
                tt(high, low, sk, ALU.max).then_inc(sm["sink_ready"], 1)
                wait(dve, sm["sink_ready"], gb * 4 + 2)
                dve.tensor_scalar(neg_max[:, 0:4], neg_max[:, 4:8], -1.0, None, ALU.mult)\
                   .then_inc(sm["sink_ready"], 1)
                wait(dve, sm["sink_ready"], gb * 4 + 3)
                tt(high, low, sk, ALU.add).then_inc(sm["sink_ready"], 1)

            def lo_probs(st, it, first):
                for m, (lo, hi) in enumerate(at_spans(st)):
                    name = ("AT", st["i"], m)
                    if st["k"] == "A":
                        seq = st["unit"] * 12 + sum(N_AT_A[:st["i"]]) + m
                    else:
                        seq = (st["unit"] - AH) * 16 + (12 * AH + 2 * st["i"] + m)
                    wait(dve, sm["at_hi"], seq + 1)
                    tt(aT_lo[:, lo:hi], p_tr[bank_of(name, first)][:, 0:hi - lo], aT_hi[:, lo:hi].bitcast(F32),
                       ALU.subtract).then_inc(sm["tp_free"], 1)

            def lo_qk(nk, i, it, first):
                name = ("T", i)
                bank = p_tr[bank_of(name, first)]
                w = P if nk == "A" else 2 * P
                unit = it + 1 if i == 0 else it
                wait(dve, sm["t_hi"], (unit * NR + i) * 2 + 2)
                t = slice(i * P, (i + 1) * P)
                for c, h in enumerate(half_rows):
                    col = slice(c * w, (c + 1) * w)
                    dve.scalar_tensor_tensor(q_pair[half_rows[1 - c], col], bank[h, 0:w], QSCALE,
                                             q_pair[h, col].bitcast(F32), ALU.mult, ALU.subtract)
                if nk == "A":
                    for c, h in enumerate(half_rows):
                        ins = tt(kT_lo[h, t], bank[h, w:w + P], k_dup[c][h, t].bitcast(F32), ALU.subtract)
                else:
                    ins = tt(kT_lo[:, t], bank[:, w:w + P], k_dup[0][:, t].bitcast(F32), ALU.subtract)
                ins.then_inc(sm["tp_free"], 1)

            def combine(st):
                inv = inv_sum[:, st["i"] % 2, :]
                wait(dve, sm["x_done"], st["G"] * 2 + 2)
                dve.reciprocal(inv[:, 0:2], sums[:, 0:2]).then_inc(sm["comb_chain"], 1)
                wait(dve, sm["comb_chain"], st["G"] * 2 + 1)
                dve.tensor_scalar(coef[:, :], sums[:, 0:1], neg_lam[:, 5:6], inv[:, 1:2], ALU.mult, ALU.mult)\
                   .then_inc(sm["comb_chain"], 1)
                wait(dve, sm["comb_chain"], st["G"] * 2 + 2)
                w = (st["i"] + 1) * P
                dve.scalar_tensor_tensor(expd[:, 1, 0:w], expd[:, 1, 0:w], coef[:, :], expd[:, 0, 0:w],
                                         ALU.mult, ALU.add).then_inc(sm["comb_done"], 1)

            def sum_b(st):
                gb = st["G"] - AH * NR
                wait(dve, sm["sink_exp"], gb + 1)
                tt(sums[:, :], sums[:, :], sink_e[:, :], ALU.add).then_inc(sm["b_sum"], 1)
                wait(dve, sm["b_sum"], gb * 2 + 1)
                dve.reciprocal(inv_sum[:, st["i"] % 2, :], sums[:, :]).then_inc(sm["b_sum"], 1)

            def y_out(st, it, first):
                i = st["i"]
                wait(dve, gate_ld[i % 2], stored_before(st) + (16 if st["k"] == "A" else 32))
                if st["k"] == "A":
                    name, w = ("YT", i), P
                    wait(dve, sm["tp_done"], use_number(name, it, first) + 1)
                    dve.scalar_tensor_tensor(gate_y[:, i % 2, 0:w], p_tr[bank_of(name, first)][:, 0:w], sub_c[:, 1:2],
                                             gate_y[:, i % 2, 0:w], ALU.mult, ALU.mult).then_inc(sm["tp_free"], 1)
                else:
                    wait(dve, sm["o_second"], st["G"] + 1)
                    tt(p_o[0:HD, :], p_o[0:HD, :], o_second_b.bitcast(F32), ALU.add).then_inc(sm["o_joined"], 1)
                    wait(dve, sm["o_joined"], st["G"] - (AH * NR - 1))
                    dve.scalar_tensor_tensor(gate_y[0:HD, i % 2, :], p_o[0:HD, :], 0.5, gate_y[0:HD, i % 2, :],
                                             ALU.mult, ALU.mult).then_inc(sm["o_read"], 2)

            dve.wait_ge(sm["consts"], 8)
            for s in range(8):
                if s >= 2:
                    split_w(s + 2, (s + 2) % 4)
                if s == 4:
                    dve.wait_ge(sm["rope_ready"], 2)
                if 4 <= s < 6:
                    rows_out(KV_TILES[0], s - 4, 32 + s - 4, s % 2)
                    rotate(KV_TILES[0], s - 4, 32 + s - 4)

            def body(it, first):
                Q0 = (it + 1) * 16 + 8
                for s in range(16):
                    i = s // 2
                    d, u, before = proj_tile(it, first, s)
                    split_y(y_split_at(first, s))
                    cur = step_at(i, it, first)
                    back1 = step_at(i - 1, it, first)
                    back2 = step_at(i - 2, it, first)
                    to_gate = back2 and back2["k"] == ("A" if s % 2 else "B")
                    if d:
                        split_w(Q0 + (s + 2), (s + 2) % 4, split_width(first, s + 2))
                    elif s < 4:
                        for j in range(4 * s + 2, 4 * s + 6):
                            split_w(NQ_OUT + j, j % 4)
                    if first == len(KINDS) and s == 1:
                        y_out(back1, it, first)
                    elif to_gate and not (first == len(KINDS) and s == 2):
                        y_out(back2, it, first)
                    if d and s % 4 == 3 and not d["turned"]:
                        gate(d, 0)
                        gate(d, 1)
                    if s % 2 and cur and cur["k"] == "B":
                        sum_b(cur)
                    tb = turned_before(it, first, s)
                    if tb:
                        n = use_number(tb[1], it, first)
                        rows_out(tb[0], tb[2], n, bank_of(tb[1], first))
                    if s % 2 == 0:
                        if cur and cur["k"] == "A":
                            max_a(cur, 0)
                        elif cur:
                            max_b(cur, it - AH)
                        if back1:
                            lo_probs(back1, it, first)
                    else:
                        if cur and cur["k"] == "A":
                            max_a(cur, 1)
                        if back1 and back1["k"] == "A":
                            wait(dve, sm["o_second"], back1["G"] + 1)
                            tt(o_sb[:, 0:P], p_o[:, 0:P], o_sb[:, P:2 * P], ALU.add).then_inc(sm["o_read"], 2)
                        if cur and cur["k"] == "A":
                            combine(cur)
                        nk = cur["k"] if cur and i + 1 < NR else kind(first + 1) if i + 1 == NR else None
                        if nk:
                            lo_qk(nk, (i + 1) % NR, it, first)
                    if tb:
                        rotate(tb[0], tb[2], n)

            iterations(dve, body)

            def add_group(g):
                dve.wait_ge(res_in[g % 2], 16 * (g // 2 + 1))
                res = x_buf[g % 2].rearrange("p (r c) -> p r c", r=4)
                for r in range(4):
                    if g == len(GROUPS) - 1:
                        dve.wait_ge(sm["row_summed"], r + 1)
                    tt(res[:, r, :], (ps_a, ps_b)[g % 2][:, r, :], res[:, r, :], ALU.add)\
                        .then_inc(sm["out_ready"], 1)

            for j in range(16, len(OUT_TILES)):
                g = OUT_TILES[j - 1][0]
                if j + 2 < len(OUT_TILES) and g < len(GROUPS) - 1:
                    split_w(NQ_OUT + j + 2, (j + 2) % 4)
                if j + 4 == len(OUT_TILES):
                    split_w(NQ_OUT + j + 3, (j + 3) % 4)
                if OUT_TILES[j][0] != g:
                    dve.wait_ge(sm["w_used"], NQ_OUT + j)
                    add_group(g)
            add_group(len(GROUPS) - 1)

        @block.gpsimd
        def _(pool):
            pool.memset(ident[:, :], 0.0).then_inc(sm["ident_ready"], 1)
            pool.memset(mask[:, :], 0.0).then_inc(sm["consts"], 1)
            for c, value in enumerate((-0.5, EPS, 1 / HD, 1 / D, 1 / P)):
                pool.memset(small[:, c, :], value).then_inc(sm["consts"], 1)
            pool.wait_ge(sm["ident_ready"], 1)
            pool.affine_select(out=ident[:, :], in_=ident[:, :], compare_op=ALU.not_equal, fill=1.0, base=0,
                               pattern=[[-1, P]], channel_multiplier=1).then_inc(sm["ident_ready"], 1)
            pool.wait_ge(sm["consts"], 6)
            pool.affine_select(out=mask[:, 0:P], in_=mask[:, 0:P], compare_op=ALU.is_gt, fill=NEG, base=0,
                               pattern=[[1, P]], channel_multiplier=-1).then_inc(sm["consts"], 1)
            pool.affine_select(out=mask[:, P:2 * P], in_=mask[:, P:2 * P], compare_op=ALU.is_ge, fill=NEG, base=0,
                               pattern=[[-1, P]], channel_multiplier=1).then_inc(sm["consts"], 1)

            def inv_rms(src, mean, dst, c, s, before):
                w = src.shape[1]
                pool.tensor_tensor(mean, src, small[:, c, 0:w], ALU.mult).then_inc(s, 1)
                wait(pool, s, before + 1)
                pool.tensor_tensor(mean, mean, small[:, 1, 0:w], ALU.add).then_inc(s, 1)
                wait(pool, s, before + 2)
                pool.tensor_tensor(dst, mean, small[:, 0, 0:w], ALU.pow).then_inc(s, 1)

            def x_rms(r):
                pool.wait_ge(sm["x_sq"], r + 1)
                inv_rms(ss_x[:, r:r + 1], ss_x[:, NR + r:NR + r + 1], ss_x[:, r:r + 1], 3, sm["x_pow"], 3 * r)

            x_rms(0)
            x_rms(1)
            for r in range(NR):
                for g in range(1, 4):
                    x_lo_part(pool, 4 * r + g, "pool")
                    if g == 1 and r + 2 < NR:
                        x_rms(r + 2)

            def norms(d, b):
                seq = d["K"] * 2 + b
                wait(pool, sm["ss_ready"], seq + 1)
                inv_rms(ss_h[:, 0:8], ss_h[:, 8:16], ss_h[:, 16:24], 2, sm["rs_ready"], seq * 3)

            def scale_rows(d, b):
                if not d["norm"]:
                    return
                seq = d["K"] * 2 + b
                wait(pool, sm["norm_chain"], seq * 3 + 3)
                wait(pool, sm["rs_ready"], seq * 3 + 3)
                x3 = rows[:, b, :].rearrange("p (g c) -> p g c", g=8)
                pool.tensor_tensor(x3, x3, ss_h[:, 16:24].unsqueeze(2).to_broadcast([P, 8, HD]), ALU.mult)\
                    .then_inc(rst_ready[b], 1)

            def lo_v(st):
                i, k = st["i"], st["k"]
                lo, w = (2 * P, P) if k == "A" else (3 * P, HD)
                wait(pool, sm["v_hi_ready"], st["G"] + 1)
                dst = v_lo[:, i, :] if k == "A" else v_hi[:, i, HD:P]
                pool.tensor_tensor(dst, qkv[:, i % 2, lo:lo + w], v_hi[:, i, 0:w].bitcast(F32),
                                   ALU.subtract).then_inc(sm["v_split"], 1)

            def split_y(part):
                if part is None:
                    return
                for k in range(*Y_PARTS[part]):
                    pool.wait_ge(sm["y_hi"], k + 1)
                    dst = hT_lo[:, k, 512:1024]
                    pool.tensor_tensor(dst, dst.bitcast(F32), hT_hi[:, k, 512:1024].bitcast(F32), ALU.subtract)\
                        .then_inc(y_lo[1], 1)

            def scale_probs(st):
                i, lo = st["i"], P if st["i"] == 0 else 0
                wait(pool, sm["b_sum"], (st["G"] - AH * NR) * 2 + 2)
                part = expd[:, i % 2, :].rearrange("p (n s) -> p n s", n=4)[:, :, lo:256]
                pool.tensor_tensor(part, part, inv_sum[:, i % 2, :].unsqueeze(2).to_broadcast([P, 4, 256 - lo]),
                                   ALU.mult).then_inc(sm["probs_scaled"], 1)

            for s in range(4, 6):
                norms(KV_TILES[0], s - 4)
                scale_rows(KV_TILES[0], s - 4)

            def body(it, first):
                for s in range(16):
                    i = s // 2
                    cur = step_at(i, it, first)
                    back1 = step_at(i - 1, it, first)
                    split_y(y_split_at(first, s))
                    if s % 2 and cur and cur["k"] == "B":
                        scale_probs(cur)
                    tb = turned_before(it, first, s)
                    if tb and tb[0]["norm"]:
                        norms(tb[0], tb[2])
                    if s % 2:
                        if back1 and back1["k"] == "A":
                            wait(pool, sm["o_squared"], back1["G"] + 1)
                            inv_rms(ss_o[:, 2:3], ss_o[:, 1:2], ss_o[:, 0:1], 4, sm["o_pow"], back1["G"] * 4)
                            wait(pool, sm["o_pow"], back1["G"] * 4 + 3)
                            pool.tensor_tensor(ss_o[:, 0:1], ss_o[:, 0:1], inv_sum[:, back1["i"] % 2, 0:1], ALU.mult)\
                                .then_inc(sm["o_pow"], 1)
                        if cur:
                            lo_v(cur)
                    if tb:
                        scale_rows(tb[0], tb[2])

            iterations(pool, body)


_INS = ["x", "positions", "norm_w", "w_in", "q_norm_a", "k_norm_a", "lambda_q1", "lambda_k1", "lambda_q2",
        "lambda_k2", "subln_w", "q_norm_b", "k_norm_b", "sinks", "w_out"]


def kernel(**inputs):
    import concourse.bacc as bacc
    from concourse.bass_utils import run_bass_kernel_spmd

    nc = bacc.Bacc("TRN2", target_bir_lowering=False, num_devices=1)
    arrays, args = {}, []
    for name in _INS:
        a = np.ascontiguousarray(inputs[name])
        arrays[f"in_{name}"] = a
        args.append(nc.dram_tensor(f"in_{name}", a.shape, mybir.dt.from_np(a.dtype), kind="ExternalInput").ap())
    freq = (np.float32(10000.0) ** (-(np.arange(0, HD, 2, dtype=np.float32) / np.float32(HD)))).astype(np.float32)
    arrays["in_inv_freq"] = freq.reshape(1, HALF)
    args.append(nc.dram_tensor("in_inv_freq", (1, HALF), F32, kind="ExternalInput").ap())
    out = nc.dram_tensor("out_0", (1, S, D), F32, kind="ExternalOutput").ap()
    decoder_layer(nc, *args, out)
    r = run_bass_kernel_spmd(nc, [arrays], core_ids=[0])
    return r.results[0]["out_0"]
```
